# Optimizing a Trainium2 kernel written in Bass

```python
import jax
import jax.numpy as jnp
from jax import lax
import numpy as np

D_MODEL = 1024
BATCH = 1
SEQ = 2048
DEPTH = 1
DEC_BATCH = 1
DEC_SEQ = 32
PAST_LEN = 1024

CHUNK = 64
D_MIX = 2 * D_MODEL
N_MIX_GROUPS = 4
D_GROUP = D_MIX // N_MIX_GROUPS
CONV_W = 4
LRU_BLOCK = 64
LRU_BLOCKS = D_GROUP // LRU_BLOCK
LRU_C = 8.0
RWKV_HEAD = 64
RWKV_HEADS = D_GROUP // RWKV_HEAD
RWKV_RANK_W = 64
RWKV_RANK_A = 64
RWKV_SHIFT_W = 3 * D_GROUP + RWKV_RANK_W + RWKV_RANK_A
RWKV_DECAY_SCALE = 0.6065306597126334
RWKV_LN_EPS = 64e-5
SSD_HEAD = 64
SSD_HEADS = D_GROUP // SSD_HEAD
SSD_STATE = 64
SSD_GROUPS = 2
SSD_CONV_CH = D_GROUP + 2 * SSD_GROUPS * SSD_STATE
HGRN_HEADS = 8
HGRN_DK = D_GROUP // HGRN_HEADS
HGRN_DV = D_GROUP // HGRN_HEADS
MEM_LEN = 256
MEM_HEADS = 4
MEM_HEAD_DIM = D_MODEL // MEM_HEADS
NORM_EPS = 1e-6
SPLITS = (D_GROUP, D_GROUP, RWKV_SHIFT_W, D_GROUP, SSD_CONV_CH, SSD_HEADS, D_GROUP, D_GROUP, D_GROUP, D_GROUP, D_GROUP)
D_IN_PROJ = 8 * D_GROUP + RWKV_SHIFT_W + SSD_CONV_CH + SSD_HEADS

kernel_name = 'hybrid_stream_encoder_step'

def rms_norm(x, g):
    xf = x.astype(jnp.float32)
    y = xf * lax.rsqrt(jnp.mean(xf * xf, axis=-1, keepdims=True) + NORM_EPS)
    return (y * g.astype(jnp.float32)).astype(x.dtype)

def split_last(t, sizes):
    out, s = [], 0
    for n in sizes:
        out.append(t[..., s:s + n])
        s += n
    return out

def chunk_len(T):
    return CHUNK if T % CHUNK == 0 else T

def causal_conv(x, buf, w, b):
    T = x.shape[1]
    xp = jnp.concatenate([buf.astype(x.dtype), x], axis=1)
    y = b
    for j in range(CONV_W):
        y = y + xp[:, j:j + T] * w[j]
    return y, xp[:, T:]

def rg_lru(x, h0, w_r, b_r, w_i, b_i, lam):
    Bsz, T, C = x.shape
    xb = x.reshape(Bsz, T, LRU_BLOCKS, LRU_BLOCK)
    r = jax.nn.sigmoid(jnp.einsum('btnd,nde->btne', xb, w_r).reshape(Bsz, T, C) + b_r)
    i = jax.nn.sigmoid(jnp.einsum('btnd,nde->btne', xb, w_i).reshape(Bsz, T, C) + b_i)
    log_a = -LRU_C * r * jax.nn.softplus(-lam)
    a = jnp.exp(log_a)
    u = jnp.sqrt(-jnp.expm1(2.0 * log_a)) * (i * x)
    u = u.at[:, 0].add(a[:, 0] * h0)

    def combine(left, right):
        return (left[0] * right[0], right[0] * left[1] + right[1])

    _, h = lax.associative_scan(combine, (a, u), axis=1)
    return h, h[:, -1]

def rwkv7_mix(pb, prev, s0, mu, w0, w_up, a0, a_up, k_k, k_a, r_k, ln_g, ln_b):
    Bsz, T, _ = pb.shape
    shifted = jnp.concatenate([prev[:, None, :].astype(pb.dtype), pb[:, :-1]], axis=1)
    xm = pb + (shifted - pb) * mu
    r, k, v, wl, al = split_last(xm, (D_GROUP, D_GROUP, D_GROUP, RWKV_RANK_W, RWKV_RANK_A))
    decay = jnp.exp(-RWKV_DECAY_SCALE * jax.nn.sigmoid(w0 + jnp.matmul(jnp.tanh(wl), w_up)))
    a = jax.nn.sigmoid(a0 + jnp.matmul(al, a_up))
    hd = lambda t: t.reshape(Bsz, T, RWKV_HEADS, RWKV_HEAD)
    kk = hd(k * k_k)
    kk = kk * lax.rsqrt(jnp.sum(kk * kk, axis=-1, keepdims=True) + 1e-12)
    k = k * (1.0 + (a - 1.0) * k_a)
    r, k, v, a, decay = hd(r), hd(k), hd(v), hd(a), hd(decay)

    def step(S, inp):
        r_t, w_t, k_t, v_t, kk_t, a_t = inp
        sa = jnp.einsum('bhvk,bhk->bhv', S, -kk_t)
        S = S * w_t[:, :, None, :] + sa[..., None] * (kk_t * a_t)[:, :, None, :] + v_t[..., None] * k_t[:, :, None, :]
        return S, jnp.einsum('bhvk,bhk->bhv', S, r_t)

    tm = lambda t: jnp.moveaxis(t, 1, 0)
    sT, y = lax.scan(step, s0, (tm(r), tm(decay), tm(k), tm(v), tm(kk), tm(a)))
    y = jnp.moveaxis(y, 0, 1)
    m = jnp.mean(y, axis=-1, keepdims=True)
    var = jnp.mean(jnp.square(y - m), axis=-1, keepdims=True)
    y = ((y - m) * lax.rsqrt(var + RWKV_LN_EPS)).reshape(Bsz, T, D_GROUP) * ln_g + ln_b
    bonus = jnp.sum(r * k * r_k, axis=-1, keepdims=True) * v
    y = y + bonus.reshape(Bsz, T, D_GROUP)
    return y, pb[:, -1], sT

def ssd_scan(x, dt, A, Bm, Cm, h0):
    Bsz, T, H, P = x.shape
    L = chunk_len(T)
    nc = T // L
    rep = H // SSD_GROUPS
    Bh = jnp.repeat(Bm, rep, axis=2)
    Ch = jnp.repeat(Cm, rep, axis=2)
    ch = lambda t: t.reshape((Bsz, nc, L) + t.shape[2:])
    x, dt, Bh, Ch = ch(x), ch(dt), ch(Bh), ch(Cm if False else Ch)
    acs = jnp.cumsum(dt * A, axis=2)
    mask = jnp.tril(jnp.ones((L, L), dtype=bool))[None, None, :, :, None]
    seg = acs[:, :, :, None, :] - acs[:, :, None, :, :]
    decay = jnp.exp(jnp.where(mask, seg, -jnp.inf))
    scores = jnp.einsum('bclhn,bcshn->bclsh', Ch, Bh) * decay * dt[:, :, None, :, :]
    y = jnp.einsum('bclsh,bcshp->bclhp', scores, x)
    dlast = jnp.exp(acs[:, :, -1:, :] - acs)
    st = jnp.einsum('bclhn,bclh,bclhp->bchpn', Bh, dlast * dt, x)
    tot = jnp.exp(acs[:, :, -1, :])

    def step(h, inp):
        s_c, g_c = inp
        return h * g_c[:, :, None, None] + s_c, h

    hT, hin = lax.scan(step, h0, (jnp.moveaxis(st, 1, 0), jnp.moveaxis(tot, 1, 0)))
    hin = jnp.moveaxis(hin, 0, 1)
    y = y + jnp.einsum('bclhn,bchpn,bclh->bclhp', Ch, hin, jnp.exp(acs))
    return y.reshape(Bsz, T, H, P), hT

def hgrn2_chunked(q, logf, v, s0):
    Bsz, T, H, K = q.shape
    L = chunk_len(T)
    nc = T // L
    k = -jnp.expm1(logf)
    to_c = lambda t: jnp.moveaxis(t.reshape(Bsz, nc, L, H, t.shape[-1]), 1, 0)
    mask = jnp.tril(jnp.ones((L, L), dtype=bool))[None, :, :, None, None]

    def step(S, inp):
        qc, lfc, kc, vc = inp
        b = jnp.cumsum(lfc, axis=1)
        o = jnp.einsum('blhk,bhkv->blhv', qc * jnp.exp(b), S)
        dec = jnp.exp(jnp.where(mask, b[:, :, None] - b[:, None, :], -jnp.inf))
        att = jnp.einsum('bthk,bshk,btshk->btsh', qc, kc, dec)
        o = o + jnp.einsum('btsh,bshv->bthv', att, vc)
        bl = b[:, -1]
        S = S * jnp.exp(bl)[..., None] + jnp.einsum('bshk,bshv->bhkv', kc * jnp.exp(bl[:, None] - b), vc)
        return S, o

    sT, o = lax.scan(step, s0, (to_c(q), to_c(logf), to_c(k), to_c(v)))
    return jnp.moveaxis(o, 0, 1).reshape(Bsz, T, H, v.shape[-1]), sT

def mem_kv(mem, g, w_k, w_v):
    m = rms_norm(mem, g)
    Bsz = mem.shape[0]
    k = jnp.matmul(m, w_k).reshape(Bsz, MEM_LEN, MEM_HEADS, MEM_HEAD_DIM)
    v = jnp.matmul(m, w_v).reshape(Bsz, MEM_LEN, MEM_HEADS, MEM_HEAD_DIM)
    return k, v

def cross_attn(h, mk, mv, w_q, w_o):
    Bsz, T, _ = h.shape
    q = jnp.matmul(h, w_q).reshape(Bsz, T, MEM_HEADS, MEM_HEAD_DIM)
    s = jnp.einsum('bthd,bmhd->bhtm', q, mk).astype(jnp.float32) * (MEM_HEAD_DIM ** -0.5)
    p = jax.nn.softmax(s, axis=-1).astype(mv.dtype)
    o = jnp.einsum('bhtm,bmhd->bthd', p, mv).reshape(Bsz, T, D_MODEL)
    return jnp.matmul(o.astype(h.dtype), w_o)

def setup_inputs(seed: int = 0) -> dict:
    key = jax.random.key(seed)
    ks = iter(jax.random.split(key, 64))
    f32 = jnp.float32
    nrm = lambda shape, s: jax.random.normal(next(ks), shape, f32) * s
    uni = lambda shape, lo, hi: jax.random.uniform(next(ks), shape, f32, lo, hi)
    gain = lambda shape: 1.0 + nrm(shape, 0.02)
    u_lru = uni((DEPTH, D_GROUP), 0.9, 0.999)
    a_lru = u_lru ** (1.0 / LRU_C)
    dt0 = jnp.exp(uni((DEPTH, SSD_HEADS), float(np.log(1e-3)), float(np.log(1e-1))))
    return {
        'x_prompt': nrm((BATCH, SEQ, D_MODEL), 1.0),
        'x_sample': nrm((DEC_BATCH, DEC_SEQ, D_MODEL), 1.0),
        'state_lru_conv': nrm((DEPTH, DEC_BATCH, CONV_W - 1, D_GROUP), 1.0),
        'state_lru_h': nrm((DEPTH, DEC_BATCH, D_GROUP), 0.5),
        'state_rwkv_shift': nrm((DEPTH, DEC_BATCH, RWKV_SHIFT_W), 1.0),
        'state_rwkv_wkv': nrm((DEPTH, DEC_BATCH, RWKV_HEADS, RWKV_HEAD, RWKV_HEAD), 0.1),
        'state_ssd_conv': nrm((DEPTH, DEC_BATCH, CONV_W - 1, SSD_CONV_CH), 1.0),
        'state_ssd_h': nrm((DEPTH, DEC_BATCH, SSD_HEADS, SSD_HEAD, SSD_STATE), 0.1),
        'state_hgrn_s': nrm((DEPTH, DEC_BATCH, HGRN_HEADS, HGRN_DK, HGRN_DV), 0.1),
        'cache_mem_k': nrm((DEPTH, DEC_BATCH, MEM_LEN, MEM_HEADS, MEM_HEAD_DIM), 1.0),
        'cache_mem_v': nrm((DEPTH, DEC_BATCH, MEM_LEN, MEM_HEADS, MEM_HEAD_DIM), 1.0),
        'mem_prompt': nrm((BATCH, MEM_LEN, D_MODEL), 1.0),
        'g_pre': gain((DEPTH, D_MODEL)),
        'g_post': gain((DEPTH, D_MODEL)),
        'g_pre_x': gain((DEPTH, D_MODEL)),
        'g_post_x': gain((DEPTH, D_MODEL)),
        'w_in': nrm((DEPTH, D_MODEL, D_IN_PROJ), D_MODEL ** -0.5),
        'w_out': nrm((DEPTH, D_MIX, D_MODEL), D_MIX ** -0.5),
        'lru_conv_w': nrm((DEPTH, CONV_W, D_GROUP), CONV_W ** -0.5),
        'lru_conv_b': nrm((DEPTH, D_GROUP), 0.01),
        'lru_w_r': nrm((DEPTH, LRU_BLOCKS, LRU_BLOCK, LRU_BLOCK), LRU_BLOCK ** -0.5),
        'lru_b_r': nrm((DEPTH, D_GROUP), 0.01),
        'lru_w_i': nrm((DEPTH, LRU_BLOCKS, LRU_BLOCK, LRU_BLOCK), LRU_BLOCK ** -0.5),
        'lru_b_i': nrm((DEPTH, D_GROUP), 0.01),
        'lru_lambda': jnp.log(a_lru) - jnp.log1p(-a_lru),
        'rwkv_mu': uni((DEPTH, RWKV_SHIFT_W), 0.0, 1.0),
        'rwkv_w0': nrm((DEPTH, D_GROUP), 1.0),
        'rwkv_w_up': nrm((DEPTH, RWKV_RANK_W, D_GROUP), RWKV_RANK_W ** -0.5),
        'rwkv_a0': nrm((DEPTH, D_GROUP), 0.5),
        'rwkv_a_up': nrm((DEPTH, RWKV_RANK_A, D_GROUP), RWKV_RANK_A ** -0.5),
        'rwkv_k_k': 0.85 + nrm((DEPTH, D_GROUP), 0.05),
        'rwkv_k_a': 1.0 + nrm((DEPTH, D_GROUP), 0.05),
        'rwkv_r_k': nrm((DEPTH, RWKV_HEADS, RWKV_HEAD), 0.1),
        'rwkv_ln_g': gain((DEPTH, D_GROUP)),
        'rwkv_ln_b': nrm((DEPTH, D_GROUP), 0.01),
        'ssd_conv_w': nrm((DEPTH, CONV_W, SSD_CONV_CH), CONV_W ** -0.5),
        'ssd_conv_b': nrm((DEPTH, SSD_CONV_CH), 0.01),
        'ssd_dt_bias': dt0 + jnp.log(-jnp.expm1(-dt0)),
        'ssd_a_log': jnp.log(uni((DEPTH, SSD_HEADS), 1.0, 16.0)),
        'ssd_d': 1.0 + nrm((DEPTH, SSD_HEADS), 0.1),
        'ssd_norm_g': gain((DEPTH, D_GROUP)),
        'hgrn_lb_logits': nrm((DEPTH, D_GROUP), 1.0),
        'hgrn_norm_g': gain((DEPTH, D_GROUP)),
        'mem_g': gain((DEPTH, D_MODEL)),
        'mem_w_q': nrm((DEPTH, D_MODEL, D_MODEL), D_MODEL ** -0.5),
        'mem_w_k': nrm((DEPTH, D_MODEL, D_MODEL), D_MODEL ** -0.5),
        'mem_w_v': nrm((DEPTH, D_MODEL, D_MODEL), D_MODEL ** -0.5),
        'mem_w_o': nrm((DEPTH, D_MODEL, D_MODEL), D_MODEL ** -0.5),
    }

def reference(x_prompt, x_sample, state_lru_conv, state_lru_h, state_rwkv_shift, state_rwkv_wkv,
              state_ssd_conv, state_ssd_h, state_hgrn_s, cache_mem_k, cache_mem_v, mem_prompt,
              g_pre, g_post, g_pre_x, g_post_x, w_in, w_out,
              lru_conv_w, lru_conv_b, lru_w_r, lru_b_r, lru_w_i, lru_b_i, lru_lambda,
              rwkv_mu, rwkv_w0, rwkv_w_up, rwkv_a0, rwkv_a_up, rwkv_k_k, rwkv_k_a, rwkv_r_k, rwkv_ln_g, rwkv_ln_b,
              ssd_conv_w, ssd_conv_b, ssd_dt_bias, ssd_a_log, ssd_d, ssd_norm_g,
              hgrn_lb_logits, hgrn_norm_g,
              mem_g, mem_w_q, mem_w_k, mem_w_v, mem_w_o):
    f32 = jnp.float32
    lb_all = jnp.cumsum(jax.nn.softmax(hgrn_lb_logits.astype(f32), axis=0), axis=0)
    lb_all = lb_all - lb_all[0]

    def run(x, mk, mv, conv_a, h_a, shift_b, wkv_b, conv_c, h_c, s_d):
        Bsz, T = x.shape[0], x.shape[1]
        n_conv_a, n_h_a, n_shift_b, n_wkv_b, n_conv_c, n_h_c, n_s_d = [], [], [], [], [], [], []
        for l in range(DEPTH):
            h = rms_norm(x, g_pre[l])
            p = jnp.matmul(h, w_in[l]).astype(f32)
            xa, ga, pb, gb, xbc, dtr, z, qd, fd, idd, gd = split_last(p, SPLITS)
            xa_c, nca = causal_conv(xa, conv_a[l], lru_conv_w[l], lru_conv_b[l])
            ya, nha = rg_lru(xa_c, h_a[l].astype(f32), lru_w_r[l], lru_b_r[l], lru_w_i[l], lru_b_i[l], lru_lambda[l])
            ya = ya * jax.nn.silu(ga)
            yb, nsb, nwb = rwkv7_mix(pb, shift_b[l].astype(f32), wkv_b[l].astype(f32), rwkv_mu[l], rwkv_w0[l],
                                     rwkv_w_up[l], rwkv_a0[l], rwkv_a_up[l], rwkv_k_k[l], rwkv_k_a[l],
                                     rwkv_r_k[l], rwkv_ln_g[l], rwkv_ln_b[l])
            yb = yb * jax.nn.silu(gb)
            xbc_c, ncc = causal_conv(xbc, conv_c[l], ssd_conv_w[l], ssd_conv_b[l])
            xbc_c = jax.nn.silu(xbc_c)
            xs, bm, cm = split_last(xbc_c, (D_GROUP, SSD_GROUPS * SSD_STATE, SSD_GROUPS * SSD_STATE))
            xs = xs.reshape(Bsz, T, SSD_HEADS, SSD_HEAD)
            dt = jax.nn.softplus(dtr + ssd_dt_bias[l])
            yc, nhc = ssd_scan(xs, dt, -jnp.exp(ssd_a_log[l].astype(f32)),
                               bm.reshape(Bsz, T, SSD_GROUPS, SSD_STATE), cm.reshape(Bsz, T, SSD_GROUPS, SSD_STATE),
                               h_c[l].astype(f32))
            yc = (yc + ssd_d[l][:, None] * xs).reshape(Bsz, T, D_GROUP)
            yc = rms_norm(yc * jax.nn.silu(z), ssd_norm_g[l])
            lb = lb_all[l]
            logf = jnp.logaddexp(jnp.log(lb), jnp.log1p(-lb) + jax.nn.log_sigmoid(fd))
            hh = lambda t: t.reshape(Bsz, T, HGRN_HEADS, t.shape[-1] // HGRN_HEADS)
            yd, nsd = hgrn2_chunked(hh(jax.nn.silu(qd)), hh(logf), hh(idd), s_d[l].astype(f32))
            yd = rms_norm(yd, hgrn_norm_g[l].reshape(HGRN_HEADS, HGRN_DV)).reshape(Bsz, T, D_GROUP)
            yd = yd * jax.nn.silu(gd)
            y = jnp.matmul(jnp.concatenate([ya, yb, yc, yd], axis=-1).astype(x.dtype), w_out[l])
            x = x + rms_norm(y, g_post[l])
            hx = rms_norm(x, g_pre_x[l])
            x = x + rms_norm(cross_attn(hx, mk[l], mv[l], mem_w_q[l], mem_w_o[l]), g_post_x[l])
            n_conv_a.append(nca)
            n_h_a.append(nha)
            n_shift_b.append(nsb)
            n_wkv_b.append(nwb)
            n_conv_c.append(ncc)
            n_h_c.append(nhc)
            n_s_d.append(nsd)
        return (x, jnp.stack(n_conv_a), jnp.stack(n_h_a), jnp.stack(n_shift_b), jnp.stack(n_wkv_b),
                jnp.stack(n_conv_c), jnp.stack(n_h_c), jnp.stack(n_s_d))

    Bp = x_prompt.shape[0]
    zeros = lambda *s: jnp.zeros((DEPTH, Bp) + s, f32)
    kv = [mem_kv(mem_prompt, mem_g[l], mem_w_k[l], mem_w_v[l]) for l in range(DEPTH)]
    mem_k_p = jnp.stack([t[0] for t in kv])
    mem_v_p = jnp.stack([t[1] for t in kv])
    (y_prompt, lru_conv_p, lru_h_p, rwkv_shift_p, rwkv_wkv_p, ssd_conv_p, ssd_h_p, hgrn_s_p) = run(
        x_prompt, mem_k_p, mem_v_p,
        zeros(CONV_W - 1, D_GROUP), zeros(D_GROUP), zeros(RWKV_SHIFT_W),
        zeros(RWKV_HEADS, RWKV_HEAD, RWKV_HEAD), zeros(CONV_W - 1, SSD_CONV_CH),
        zeros(SSD_HEADS, SSD_HEAD, SSD_STATE), zeros(HGRN_HEADS, HGRN_DK, HGRN_DV))
    (y_sample, lru_conv_s, lru_h_s, rwkv_shift_s, rwkv_wkv_s, ssd_conv_s, ssd_h_s, hgrn_s_s) = run(
        x_sample, cache_mem_k, cache_mem_v, state_lru_conv, state_lru_h, state_rwkv_shift, state_rwkv_wkv,
        state_ssd_conv, state_ssd_h, state_hgrn_s)
    return (y_prompt, y_sample, lru_conv_p, lru_conv_s, lru_h_p, lru_h_s, rwkv_shift_p, rwkv_shift_s,
            rwkv_wkv_p, rwkv_wkv_s, ssd_conv_p, ssd_conv_s, ssd_h_p, ssd_h_s, hgrn_s_p, hgrn_s_s,
            mem_k_p, mem_v_p)


_drawn_inputs = setup_inputs


def setup_inputs(seed=0):
    import zlib

    import numpy as np

    out = dict(_drawn_inputs(seed))
    spreads = {}
    factors = {'state_hgrn_s': 8.0,
     'g_post': 4.065,
     'g_pre_x': 5.003,
     'g_post_x': 18.62,
     'lru_b_r': 8.0,
     'lru_b_i': 8.0,
     'rwkv_k_k': 3.86,
     'rwkv_ln_g': 8.0,
     'rwkv_ln_b': 27.722,
     'ssd_conv_b': 3.16,
     'ssd_norm_g': 5.04,
     'hgrn_norm_g': 8.0,
     'mem_g': 2.813}
    for name, (base, spread) in spreads.items():
        noise = np.random.default_rng([zlib.crc32(name.encode()), seed]).standard_normal(out[name].shape)
        drawn = base * np.exp(spread * noise) if base else spread * noise
        out[name] = jnp.asarray(drawn.astype(out[name].dtype))
    for name, factor in factors.items():
        out[name] = (out[name] * factor).astype(out[name].dtype)
    return out
```

```python
from contextlib import ExitStack

import concourse.bass as bass
from concourse import mybir

F32 = mybir.dt.float32
ALU = mybir.AluOpType
ACT = mybir.ActivationFunctionType
AX_X = mybir.AxisListType.X

P = 128
BANK = 512
D_MODEL = 1024
D_GROUP = 512
CONV_W = 4
HALO = CONV_W - 1
HEADS = 8
HEAD = 64
PAIRS = HEADS // 2
SUB = 32
MEM_LEN = 256
MEM_HEADS = 4
MEM_HEAD_DIM = D_MODEL // MEM_HEADS
D_MIX = 4 * D_GROUP
SSD_CONV_CH = 768
SHIFT_W = 3 * D_GROUP + 2 * HEAD
LRU_C = 8.0
DECAY_SCALE = 0.6065306597126334
NORM_EPS = 1e-6
RWKV_LN_EPS = 64e-5
KT = D_MODEL // P
YT = D_MIX // P

XA, GA, PB, GB, XBC, Z, QD, FD, ID, GD, N_CH_TILES = 0, 4, 8, 21, 25, 31, 35, 39, 43, 47, 51
DT_COL = P * Z
D_IN_PROJ = P * N_CH_TILES + HEADS


class Steps:

    def __init__(self, sem, key, table):
        self.sem, self.names, self.base, self.seen = sem, table.setdefault(key, []), 1, []
        self.index = {n: k + 1 for k, n in enumerate(self.names)}

    def start(self, eng):
        eng.sem_inc(self.sem, 1)

    def iteration(self, i):
        self.base, self.seen = i * len(self.names) + 1, []

    def did(self, name):
        self.seen.append(name)
        assert self.names[len(self.seen) - 1] == name, (name, self.names[len(self.seen) - 1])
        return self.sem, 1

    def at(self, name):
        return self.sem, self.base + self.index[name]

    def before(self):
        return self.sem, self.base

    def last(self):
        return self.sem, self.base + len(self.seen)


def bc(ap, dim, n):
    v = ap.unsqueeze(dim)
    shape = list(v.shape)
    shape[dim] = n
    return v.broadcast_to(shape)


def project_pass(nc, x_prompt, x_sample, g_pre, w_in, pc, dtr, conv_states, TP, TS):
    TALL = TP + TS
    GROUPS = 5
    N = TALL // GROUPS
    NT = TP // P
    assert GROUPS * N == TALL and N <= BANK and TS <= P

    with ExitStack() as ctx:
        def sb(name, shape):
            return ctx.enter_context(nc.sbuf_tensor(f"in_{name}", shape, F32))

        def sem(name):
            return ctx.enter_context(nc.semaphore(f"in_{name}"))

        ctx.enter_context(nc.allow_non_contiguous_dma(reason="states and vectors over channels, once"))
        hT = sb("hT", [P, KT, TALL])
        x_in = [sb(f"x_in{j}", [P, D_MODEL]) for j in range(2)]
        junk = sb("junk", [P, D_MODEL])
        rstd = sb("rstd", [P, 2])
        eps = sb("eps", [P, 1])
        ident = sb("ident", [P, P])
        g_col = sb("g_col", [P, KT])
        w_tile = [sb(f"w_tile{j}", [P, KT, P]) for j in range(2)]
        w_dt = sb("w_dt", [P, KT, HEADS])
        out = [sb(f"out{j}", [P, TALL]) for j in range(2)]
        dt_out = sb("dt_out", [P, NT + 1, HEADS])
        zeros = sb("zeros", [P, 13, HALO])
        ps = ctx.enter_context(nc.psum_tensor("in_ps", [P, 8, BANK], F32))

        const_in, link_s, const_made = sem("const_in"), sem("link"), sem("const_made")
        x_loaded = [sem(f"x_loaded{j}") for j in range(2)]
        squared, rooted = sem("squared"), sem("rooted")
        normed_at, turned, normed = sem("normed_at"), sem("turned"), sem("normed")
        w_loaded = [sem(f"w_loaded{j}") for j in range(2)]
        group_done, group_out = sem("group_done"), sem("group_out")
        stored = [sem(f"stored{j}") for j in range(2)]
        dt_done, dt_copied, dt_stored = sem("dt_done"), sem("dt_copied"), sem("dt_stored")
        halo_stored, waits_met = sem("halo_stored"), sem("waits_met")
        block = ctx.enter_context(nc.Block())

        w_view = w_in[0, :, :].rearrange("(k p) n -> p k n", p=P)

        @block.sync
        def _(sync):
            sync.dma_start(g_col[:, :], g_pre.rearrange("a (k p) -> p (a k)", p=P)).then_inc(const_in, 16)
            sync.dma_start(w_dt[:, :, :], w_view[:, :, DT_COL:DT_COL + HEADS]).then_inc(const_in, 16)

            def load_x(i, j):
                sync.dma_start(x_in[j][:, :], x_prompt[0, bass.ds(i * P, P), :]).then_inc(x_loaded[j], 16)

            def load_w(n, j):
                skip = HEADS if (n >= Z if isinstance(n, int) else after_dt[0]) else 0
                sync.dma_start(w_tile[j][:, :, :], w_view[:, :, bass.ds(n * P + skip, P)]).then_inc(w_loaded[j], 16)

            def store(n, j):
                sync.wait_ge(group_out, (n + 1) * GROUPS + GROUPS)
                sync.sem_inc(waits_met, 1)
                for g, (t0, t1) in enumerate(((0, TP), (TP, TALL))):
                    dst = pc[g][bass.ds(n, 1), :, HALO:HALO + t1 - t0].rearrange("t p m -> (t p) m")
                    sync.dma_start(dst, out[j][:, t0:t1]).then_inc(stored[j], 16)

            after_dt = [False]
            for j in range(2):
                sync.sem_inc(stored[j], 16)
                load_x(j, j)
            load_w(0, 0)
            load_w(1, 1)
            with sync.Fori(0, NT // 2 - 1) as i:
                for j in range(2):
                    sync.wait_ge(normed, 2 * i + j + 2)
                    load_x(2 * i + j + 2, j)
            sync.wait_ge(normed, NT)
            sync.dma_start(x_in[0][0:TS, :], x_sample[0, :, :]).then_inc(x_loaded[0], 16)

            def turn_over(n0, n1):
                with sync.Fori(n0 // 2, n1 // 2) as i:
                    for j in range(2):
                        store(2 * i + j, j)
                        load_w(2 * i + j + 2, j)

            turn_over(0, Z - 3)
            for n in (Z - 3, Z - 2):
                store(n, n % 2)
                load_w(n + 2, n % 2)
            after_dt[0] = True
            turn_over(Z - 1, N_CH_TILES - 3)
            store(N_CH_TILES - 3, 0)
            load_w(N_CH_TILES - 1, 0)
            store(N_CH_TILES - 2, 1)
            store(N_CH_TILES - 1, 0)
            sync.wait_ge(stored[0], 32 * (N_CH_TILES // 2 + 1) + 16)
            sync.wait_ge(stored[1], 32 * (N_CH_TILES // 2) + 16)

        @block.gpsimd
        def _(pool):
            count = [0]

            def link(ins):
                count[0] += 1
                ins.then_inc(link_s, 1)
                pool.wait_ge(link_s, count[0])

            link(pool.memset(eps[:, :], NORM_EPS))
            link(pool.memset(zeros[:, :, :], 0.0))
            link(pool.memset(ident[:, :], 0.0))
            link(pool.affine_select(out=ident[:, :], in_=ident[:, :], compare_op=ALU.not_equal, fill=1.0,
                                    base=0, pattern=[[-1, P]], channel_multiplier=1))
            pool.sem_inc(const_made, 1)
            halo = [(pc[0][XA:XA + 4, :, 0:HALO].rearrange("t p m -> p t m"), zeros[:, 0:4, :]),
                    (pc[0][XBC:XBC + 6, :, 0:HALO].rearrange("t p m -> p t m"), zeros[:, 0:6, :]),
                    (pc[0][PB:PB + 13, :, HALO - 1:HALO].rearrange("t p m -> p t m"), zeros[:, :, 0:1]),
                    (pc[1][PB:PB + 13, :, HALO - 1], conv_states["shift"].rearrange("a b (t p) -> (a b t) p", p=P))]
            for m in range(HALO):
                for t, n, name in ((XA, 4, "lru_conv"), (XBC, 6, "ssd_conv")):
                    halo.append((pc[1][t:t + n, :, m], conv_states[name][0, 0, m, :].rearrange("(t p) -> t p", p=P)))
            for dst, src in halo:
                pool.dma_start(dst, src).then_inc(halo_stored, 16)
            pool.wait_ge(dt_copied, 2)
            pool.dma_start(dtr[0].rearrange("(t p) h -> p t h", p=P), dt_out[:, 0:NT, :]).then_inc(dt_stored, 16)
            pool.dma_start(dtr[1][:, :], dt_out[0:TS, NT, :]).then_inc(dt_stored, 16)
            pool.wait_ge(halo_stored, 16 * len(halo))
            pool.wait_ge(dt_stored, 32)

        @block.scalar
        def _(act):
            act.wait_ge(const_made, 1)

            def root(t, j, load, r):
                act.wait_ge(x_loaded[j], load)
                act.activation(junk[0:r, :], x_in[j][0:r, :], ACT.Square, accum_out=rstd[0:r, j:j + 1]).then_inc(squared, 1)
                act.wait_ge(squared, 2 * t + 1)
                act.activation(rstd[0:r, j:j + 1], rstd[0:r, j:j + 1], ACT.Ln, scale=1.0 / D_MODEL, bias=eps[0:r, :]).then_inc(squared, 1)
                act.wait_ge(squared, 2 * t + 2)
                act.activation(rstd[0:r, j:j + 1], rstd[0:r, j:j + 1], ACT.Exp, scale=-0.5).then_inc(rooted, 1)

            with act.Fori(0, NT // 2) as i:
                for j in range(2):
                    act.wait_ge(normed, 2 * i + 1)
                    root(2 * i + j, j, 16 * (i + 1), P)
            root(NT, 0, 16 * (NT // 2 + 1), TS)

            act.sem_inc(group_out, GROUPS)

            def copy_out(n, j, i):
                act.wait_ge(stored[j], 32 * i + 16)
                for g in range(GROUPS):
                    act.wait_ge(group_done, GROUPS * n + g + 1)
                    act.activation(out[j][:, g * N:(g + 1) * N], ps[:, g, 0:N], ACT.Copy).then_inc(group_out, 1)

            with act.Fori(0, N_CH_TILES // 2) as i:
                for j in range(2):
                    copy_out(2 * i + j, j, i)
            copy_out(N_CH_TILES - 1, 0, N_CH_TILES // 2)

        @block.vector
        def _(vec):
            vec.sem_inc(normed, 1)
            vec.wait_ge(const_in, 32)

            def norm(t, j, r, cols):
                vec.wait_ge(rooted, t + 1)
                vec.tensor_scalar(x_in[j][0:r, :], x_in[j][0:r, :], rstd[0:r, j:j + 1], None, ALU.mult).then_inc(normed_at, 1)
                vec.wait_ge(turned, t + 1)
                src = ps[:, 4 * j:4 * j + 2, :].rearrange("p b (k t) -> p (b k) t", t=P)[:, :, 0:r]
                vec.tensor_tensor(cols, src, bc(g_col[:, :], 2, r), ALU.mult).then_inc(normed, 1)

            with vec.Fori(0, NT // 2) as i:
                for j in range(2):
                    norm(2 * i + j, j, P, hT[:, :, bass.ds((2 * i + j) * P, P)])
            norm(NT, 0, TS, hT[:, :, TP:TALL])
            vec.wait_ge(dt_done, 1)
            vec.tensor_copy(dt_out[:, 0:NT, :].rearrange("p t h -> p (t h)"), ps[:, 5, 0:NT * HEADS]).then_inc(dt_copied, 1)
            vec.tensor_copy(dt_out[0:TS, NT, :], ps[0:TS, 5, NT * HEADS:(NT + 1) * HEADS]).then_inc(dt_copied, 1)

        @block.tensor
        def _(pe):
            pe.wait_ge(const_made, 1)
            pe.wait_ge(const_in, 32)

            def turn(t, j, r, back):
                pe.wait_ge(normed_at, t + 1)
                pe.wait_ge(normed, back)
                for k in range(KT):
                    o = ps[:, 4 * j + k // 4, (k % 4) * P:(k % 4) * P + r]
                    last = pe.transpose(o, x_in[j][0:r, k * P:(k + 1) * P], ident[0:r, 0:r])
                last.then_inc(turned, 1)

            with pe.Fori(0, NT // 2) as i:
                for j in range(2):
                    turn(2 * i + j, j, P, 2 * i + 1)
            turn(NT, 0, TS, NT + 1)
            pe.wait_ge(normed, NT + 2)
            for t in range(NT + 1):
                r = P if t < NT else TS
                for k in range(KT):
                    last = pe.matmul(ps[0:r, 5, t * HEADS:(t + 1) * HEADS], hT[:, k, t * P:t * P + r], w_dt[:, k, :],
                                     start=k == 0, stop=k == KT - 1)
            last.then_inc(dt_done, 1)

            def products(n, j, i):
                pe.wait_ge(w_loaded[j], 16 * (i + 1))
                for g in range(GROUPS):
                    pe.wait_ge(group_out, GROUPS * n + g + 1)
                    for k in range(KT):
                        last = pe.matmul(ps[:, g, 0:N], w_tile[j][:, k, :], hT[:, k, g * N:(g + 1) * N],
                                         start=k == 0, stop=k == KT - 1)
                    last.then_inc(group_done, 1)

            with pe.Fori(0, N_CH_TILES // 2) as i:
                for j in range(2):
                    products(2 * i + j, j, i)
            products(N_CH_TILES - 1, 0, N_CH_TILES // 2)
STEPS = {
    'mixp': {
        'pe': [
            'up', 'kk_norm', 'lru_gates', 'acs', 'x_tok', 'ssd', 'bonus', 'mats', 'keys', 'q2', 'tu2', 'q4',
            'tu4', 'q8', 'tu8', 'q16', 'tu16', 'q32', 'tu32', 'h_keys', 'rhs0', 'sa0', 'y_rwkv0', 'rhs1',
            'sa1', 'y_rwkv', 'h_kv', 'h_out', 'yc_ms', 'yb_mean', 'yd_ms', 'yb_var',
        ],
        'vector': [
            'dt_x', 'gates', 'q_twice', 'f_one_plus', 'dt_one_plus', 'up_biased', 'log_w', 'cum',
            'cum_before', 'kp_factor', 'kp', 'lru_biased', 'lru_s', 'lru_ix', 'xbc_twice', 'a_square',
            'one_less', 'one_less_floor', 'kk_unit', 'kappa', 'r_hat', 'b_twice', 'bneg', 'khat', 'lru_u',
            'lru_carry', 'lru_u0', 'lru_cut', 'lru_h', 'lru_state', 'y_lru', 'dt_log1p1', 'dt_log1p2',
            'dt_log1p3', 'dt_log1p4', 'dt_log1p5', 'dt_log1p6', 'dt_log1p7', 'dt', 'd_a', 'logf', 'log_k',
            'h_cum', 'h_m0', 'h_end', 'h_mid_span', 'h_spans', 'h_mid', 'h_rel', 'h_kx', 'acs', 'seg',
            'seg_clamped', 'd_last0', 'd_last', 'cb0', 'cb1', 'x_dt', 'd_last_dt', 'x_dd', 'ssd_scores0',
            'ssd_scores1', 'd_x', 'yc_inter', 'yc_sum', 'yc_intra', 'yc', 'ssd_decay0', 'ssd_decay1',
            'ssd_state', 'bonus_v', 'mt_pt', 'nt_qt', 't_off0', 't0', 'b_key0', 'qi2_0', 'h_q', 'qi4_0',
            'h_q2', 'qi8_0', 'h_k2', 'qi16_0', 'qi32_0', 'att_own0', 'att_0', 'att', 'rhs0_0', 'sa0_0',
            'wkv_sum0', 'wkv0', 'rhs1_0', 'sa1_0', 'wkv_sum1', 'wkv1', 'h_smid0', 'h_decay0', 'h_state0',
            'h_smid1', 'h_decay1', 'h_states', 'yb_centred', 'yc_normed', 'y_ssd', 'yb_normed', 'yd_normed',
            'yb_gain', 'yd_gain', 'yb_bias', 'yb_bonus', 'y_rwkv', 'y_hgrn',
        ],
        'scalar': [
            'gate_tanh', 'q_tanh', 'wl_tanh', 'f_abs', 'f_exp', 'dt_abs', 'dt_exp', 'wa_tanh', 'e_cum',
            'e_neg', 'e_before', 'ri_tanh', 'lru_a', 'lru_th', 'xbc_tanh', 'xbc', 'f_ln', 'dt_ln', 'kk_ln',
            'one_less_ln', 'kk_exp', 'one_less_root', 'seg_exp', 'e_acs', 'tot0', 'tot1', 'd_last_exp',
            'b_tok', 'h_k', 'h_eq', 'h_mids', 'h_ends', 'v_tok0', 'k_key0', 't2_0', 'u2_0', 't4_0', 'u4_0',
            't8_0', 'u8_0', 't16_0', 'u16_0', 'u32_0', 'hk_key0', 'hv_tok0', 'yd_square', 'yd_copy',
            'yb_copy', 'yc_ln', 'yd_ln', 'yb_ln', 'yc_rms', 'yd_rms', 'yb_rstd',
        ],
        'pool': [
            'shift_diff', 'shift_mu', 'shift', 'kk_raw', 'kk_square', 'tap0', 'tap1', 'tap_sum1', 'tap2',
            'tap_sum2', 'tap3', 'tap_sum3', 'conv', 'rk', 'rk_weighed', 'u_off0', 'u00', 'lev2_0', 'lev4_0',
            'lev8_0', 'lev16_0', 'lev32_0', 'yc_square', 'yb_square',
        ],
    },
    'mixs': {
        'pe': [
            'up', 'kk_norm', 'lru_gates', 'acs', 'x_tok', 'ssd', 'bonus', 'mats', 'keys', 'q2', 'tu2', 'q4',
            'tu4', 'q8', 'tu8', 'q16', 'tu16', 'h_keys', 'rhs0', 'sa0', 'y_rwkv', 'h_kv', 'h_out', 'yc_ms',
            'yb_mean', 'yd_ms', 'yb_var',
        ],
        'vector': [
            'dt_x', 'gates', 'q_twice', 'f_one_plus', 'dt_one_plus', 'up_biased', 'log_w', 'cum',
            'cum_before', 'kp_factor', 'kp', 'lru_biased', 'lru_s', 'lru_ix', 'xbc_twice', 'a_square',
            'one_less', 'one_less_floor', 'kk_unit', 'kappa', 'r_hat', 'b_twice', 'bneg', 'khat', 'lru_u',
            'lru_carry', 'lru_u0', 'lru_cut', 'lru_h', 'lru_state', 'y_lru', 'dt_log1p1', 'dt_log1p2',
            'dt_log1p3', 'dt_log1p4', 'dt_log1p5', 'dt_log1p6', 'dt_log1p7', 'dt', 'd_a', 'logf', 'log_k',
            'h_cum', 'h_m0', 'h_end', 'h_mid_span', 'h_spans', 'h_mid', 'h_rel', 'h_kx', 'acs', 'seg',
            'seg_clamped', 'd_last0', 'd_last', 'cb0', 'cb1', 'x_dt', 'd_last_dt', 'x_dd', 'ssd_scores0',
            'ssd_scores1', 'd_x', 'yc_inter', 'yc_sum', 'yc_intra', 'yc', 'ssd_decay0', 'ssd_decay1',
            'ssd_state', 'bonus_v', 'mt_pt_0', 'mt_pt', 'nt_qt_0', 'nt_qt', 't_off0', 't_off64', 't0_0', 't0',
            'b_key0', 'b_key64', 'qi2_0', 'qi2_64', 'h_q', 'qi4_0', 'qi4_64', 'h_q2', 'qi8_0', 'qi8_64',
            'h_k2', 'qi16_0', 'qi16_64', 'att_own0', 'att_own64', 'att', 'rhs0_0', 'rhs0_64', 'sa0_0',
            'sa0_64', 'wkv_sum0', 'wkv0', 'h_smid0', 'h_decay0', 'h_states', 'yb_centred', 'yc_normed',
            'y_ssd', 'yb_normed', 'yd_normed', 'yb_gain', 'yd_gain', 'yb_bias', 'yb_bonus', 'y_rwkv',
            'y_hgrn',
        ],
        'scalar': [
            'gate_tanh', 'q_tanh', 'wl_tanh', 'f_abs', 'f_exp', 'dt_abs', 'dt_exp', 'wa_tanh', 'e_cum',
            'e_neg', 'e_before', 'ri_tanh', 'lru_a', 'lru_th', 'xbc_tanh', 'xbc', 'f_ln', 'dt_ln', 'kk_ln',
            'one_less_ln', 'kk_exp', 'one_less_root', 'seg_exp', 'e_acs', 'tot0', 'tot1', 'd_last_exp',
            'b_tok', 'h_k', 'h_eq', 'h_mids', 'h_ends', 'v_tok0', 'k_key0', 'v_tok64', 'k_key64', 't2_0',
            'u2_0', 't2_64', 'u2_64', 't4_0', 'u4_0', 't4_64', 'u4_64', 't8_0', 'u8_0', 't8_64', 'u8_64',
            'u16_0', 'u16_64', 'hk_key0', 'hv_tok0', 'hk_key64', 'hv_tok64', 'yd_square', 'yd_copy',
            'yb_copy', 'yc_ln', 'yd_ln', 'yb_ln', 'yc_rms', 'yd_rms', 'yb_rstd',
        ],
        'pool': [
            'shift_diff', 'shift_mu', 'shift', 'kk_raw', 'kk_square', 'tap0', 'tap1', 'tap_sum1', 'tap2',
            'tap_sum2', 'tap3', 'tap_sum3', 'conv', 'rk', 'rk_weighed', 'u_off0', 'u_off64', 'u00', 'u064',
            'lev2_0', 'lev2_64', 'lev4_0', 'lev4_64', 'lev8_0', 'lev8_64', 'lev16_0', 'lev16_64', 'yc_square',
            'yb_square',
        ],
    },
    'attp': {
        'pe_mix': [
            'mix',
        ],
        'pe_att': [
            'hx_turned', 'scores', 'p_turned', 'att',
        ],
        'vec_mix': [
            'mix_gain', 'x1', 'hx',
        ],
        'vec_att': [
            'max', 'neg_max', 'inverse', 'probs', 'att_gain', 'out',
        ],
        'act_mix': [
            'mix_root_squares', 'mix_root_ln', 'mix_root', 'x1_root_squares', 'x1_root_ln', 'x1_root',
        ],
        'act_att': [
            'hxT', 'exp0', 'exp1', 'exp2', 'exp3', 'pT', 'att_root_squares', 'att_root_ln', 'att_root',
        ],
    },
    'atts': {
        'pe_mix': [
            'mix',
        ],
        'pe_att': [
            'hx_turned', 'scores', 'p_turned', 'att',
        ],
        'vec_mix': [
            'mix_gain', 'x1', 'hx',
        ],
        'vec_att': [
            'max', 'neg_max', 'inverse', 'probs', 'att_gain', 'out',
        ],
        'act_mix': [
            'mix_root_squares', 'mix_root_ln', 'mix_root', 'x1_root_squares', 'x1_root_ln', 'x1_root',
        ],
        'act_att': [
            'hxT', 'exp0', 'exp1', 'exp2', 'exp3', 'pT', 'att_root_squares', 'att_root_ln', 'att_root',
        ],
    },
}

def make_masks(nc, ctx, L, tag):
    def sb(name, shape):
        return ctx.enter_context(nc.sbuf_tensor(f"{tag}_{name}", shape, F32))

    c = {
        "ident": sb("ident", [P, P]),
        "ones": sb("ones", [P, P]),
        "headones": sb("headones", [P, P]),
        "headmean": sb("headmean", [P, P]),
        "triu": sb("triu", [P, P]),
        "causal": sb("causal", [P, 2, L]),
        "subcausal": sb("subcausal", [P, L]),
        "eye": sb("eye", [P, L]),
        "first": sb("first", [P, 4 * P]),
    }
    levels = []
    n = 1
    while n < L:
        levels.append(n)
        n *= 2
    for n in levels:
        c[f"up{n}"] = sb(f"up{n}", [P, L])
    c["low1"] = sb("low1", [P, L])
    c["levels"] = levels
    return c


def fill_masks(pool, link, c, L):
    half = [slice(0, 64), slice(64, 128)]
    link(pool.memset(c["ones"][:, :], 1.0 / 512))
    link(pool.memset(c["headones"][:, :], 0.0))
    link(pool.memset(c["headmean"][:, :], 0.0))
    for a in half:
        link(pool.memset(c["headones"][a, a], 1.0))
        link(pool.memset(c["headmean"][a, a], 1.0 / 64))
    link(pool.memset(c["ident"][:, :], 0.0))
    link(pool.affine_select(out=c["ident"][:, :], in_=c["ident"][:, :], compare_op=ALU.not_equal,
                            fill=1.0, base=0, pattern=[[-1, P]], channel_multiplier=1))
    link(pool.memset(c["triu"][:, :], 1.0))
    link(pool.affine_select(out=c["triu"][:, :], in_=c["triu"][:, :], compare_op=ALU.is_ge,
                            fill=0.0, base=0, pattern=[[1, P]], channel_multiplier=-1))
    link(pool.memset(c["causal"][:, :, :], 1.0))
    link(pool.memset(c["subcausal"][:, :], 1.0))
    link(pool.memset(c["eye"][:, :], 0.0))
    link(pool.memset(c["low1"][:, :], 0.0))
    for n in c["levels"]:
        link(pool.memset(c[f"up{n}"][:, :], 0.0))
        v = c[f"up{n}"][:, :].rearrange("p (b r) -> p b r", r=2 * n)
        link(pool.memset(v[:, :, n:2 * n], 1.0))
    v = c["low1"][:, :].rearrange("p (b r) -> p b r", r=2)
    link(pool.memset(v[:, :, 0:1], 1.0))
    link(pool.memset(c["first"][:, :], 1.0))
    v = c["first"][:, :].rearrange("p (b r) -> p b r", r=L)
    link(pool.memset(v[:, :, 0:1], 0.0))
    for a in half:
        for k, base in ((0, -1), (1, 0)):
            v = c["causal"][a, k, :]
            link(pool.affine_select(out=v, in_=v, compare_op=ALU.is_ge, fill=0.0, base=base,
                                    pattern=[[1, L]], channel_multiplier=-1))
        v = c["subcausal"][a, :]
        link(pool.affine_select(out=v, in_=v, compare_op=ALU.is_ge, fill=0.0, base=0,
                                pattern=[[1, L]], channel_multiplier=-1))
        if L > SUB:
            v = c["subcausal"][a, SUB:L]
            link(pool.affine_select(out=v, in_=v, compare_op=ALU.is_ge, fill=0.0, base=-SUB,
                                    pattern=[[0, SUB]], channel_multiplier=1))
        v = c["eye"][a, :]
        link(pool.affine_select(out=v, in_=v, compare_op=ALU.not_equal, fill=1.0, base=0,
                                pattern=[[-1, L]], channel_multiplier=1))
        for n in c["levels"]:
            v = c[f"up{n}"][a, :].rearrange("p (b r) -> p b r", r=2 * n)
            link(pool.affine_select(out=v, in_=v, compare_op=ALU.is_ge, fill=0.0, base=0,
                                    pattern=[[-2 * n, L // (2 * n)], [0, 2 * n]], channel_multiplier=1))
            link(pool.affine_select(out=v, in_=v, compare_op=ALU.is_ge, fill=0.0, base=n - 1,
                                    pattern=[[2 * n, L // (2 * n)], [0, 2 * n]], channel_multiplier=-1))
        v = c["low1"][a, :].rearrange("p (b r) -> p b r", r=2)
        link(pool.affine_select(out=v, in_=v, compare_op=ALU.is_equal, fill=0.0, base=-1,
                                pattern=[[-2, L // 2], [0, 2]], channel_multiplier=1))


def mixer_pass(nc, tag, T, TT, L, pc, dtr, yt, w, state_in, state_out):
    NCH, NSUB = TT // L, L // SUB
    NB = min(2, T // TT)
    rows = [slice(0, P)] if L == 64 else [slice(0, L), slice(64, 64 + L)]
    halves = [slice(0, 64), slice(64, 128)]
    hrows = [slice(0, L), slice(64, 64 + L)]

    with ExitStack() as ctx:
        def sb(name, shape):
            return ctx.enter_context(nc.sbuf_tensor(f"{tag}_{name}", shape, F32))

        def sem(name):
            return ctx.enter_context(nc.semaphore(f"{tag}_{name}"))

        ctx.enter_context(nc.allow_non_contiguous_dma(reason="vectors over channels, one value per partition, once"))
        c = make_masks(nc, ctx, L, tag)
        ps = ctx.enter_context(nc.psum_tensor(f"{tag}_ps", [P, 8, BANK], F32))

        conv_in = [sb(f"conv_in{j}", [P, 10, HALO + TT]) for j in range(NB)]
        mix_in = [sb(f"mix_in{j}", [P, 13, 1 + TT]) for j in range(NB)]
        gate_in = [sb(f"gate_in{j}", [P, 16, TT]) for j in range(NB)]
        hg_in = [sb(f"hg_in{j}", [P, 12, TT]) for j in range(NB)]
        dt_in = [sb(f"dt_in{j}", [TT, HEADS]) for j in range(NB)]

        conv_w = sb("conv_w", [P, 4, 10])
        conv_b = sb("conv_b", [P, 10])
        lru_w = sb("lru_w", [P, 2, 4, P])
        lru_b = sb("lru_b", [P, 2, 4])
        lam = sb("lam", [P, 4])
        mu = sb("mu", [P, 13])
        up_w = sb("up_w", [P, D_GROUP])
        up_b = sb("up_b", [P, 2, 4])
        kvec = sb("kvec", [P, 6, 4])
        gains = sb("gains", [P, 2, 4])
        dt_par = sb("dt_par", [P, 2, HEADS])
        half_ka = sb("half_ka", [P, 4])
        neg_a = sb("neg_a", [P, HEADS])
        sp = sb("sp", [P, 4, 4])

        lru_h = sb("lru_h", [P, 4])
        wkv = sb("wkv", [P, PAIRS, HEAD])
        ssd_h = sb("ssd_h", [P, 4, HEAD])
        hg_s = sb("hg_s", [P, PAIRS, HEAD])
        turn = sb("turn", [P, 2, PAIRS, HEAD])

        cv = sb("cv", [P, 10, TT])
        cv_term = sb("cv_term", [P, 10, TT])
        seg = cv_term[:, 0:HEADS, :]
        ri_buf = sb("ri_buf", [P, 2 * D_GROUP])
        ri = ri_buf[:, 0:8 * TT].rearrange("p (a t) -> p a t", a=8)
        x_dt, x_dd = (ri_buf[:, a:a + D_GROUP].rearrange("p (h v) -> p h v", h=HEADS) for a in (0, D_GROUP))

        def twice(name):
            b = sb(name, [P, D_GROUP])
            return (b[:, 0:4 * TT].rearrange("p (a t) -> p a t", a=4),
                    b[:, 0:NCH * PAIRS * L].rearrange("p (c q t) -> p c q t", c=NCH, q=PAIRS),
                    b[:, 0:NCH * PAIRS * HEAD].rearrange("p (c q t) -> p c q t", c=NCH, q=PAIRS), b)

        ls, _, hv_tok, _ = twice("ls_hv_tok")
        la, _, hk_key, _ = twice("la_hk_key")
        lth, tinv, _, _ = twice("lth_tinv")
        lu, qi, _, _ = twice("lu_qi")
        gate = sb("gate", [P, 16, TT])
        y_out = sb("y_out", [P, 16, TT])
        xbc = sb("xbc", [P, 6, TT])
        dts = sb("dts", [P, 10, HEADS])
        d_a = sb("d_a", [P, HEADS])
        acs = sb("acs", [P, HEADS])
        cb = sb("cb", [P, 2, TT])
        e_acs = sb("e_acs", [P, PAIRS, TT])
        tot = sb("tot", [P, HEADS])
        b_tok = sb("b_tok", [P, P])
        yc = sb("yc", [P, 4, TT])
        yc2 = sb("yc2", [P, 4, TT])
        rms = sb("rms", [P, TT])
        eps = sb("eps", [P, 3])
        xm = sb("xm", [P, 13, TT])
        tw = sb("tw", [64, TT])
        wa = sb("wa", [P, 8, TT])
        cum, _, hs_mid, _ = twice("cum_hs_mid")
        cum_b = sb("cum_b", [P, 4, TT])
        yd = cum_b
        e_cum = sb("e_cum", [P, 4, TT])
        e_neg, _, _, rhs_sa = twice("e_neg_rhs_sa")
        rhs, sa = (rhs_sa[:, a:a + 256].rearrange("p (q v) -> p q v", q=PAIRS) for a in (0, 256))
        kk = sb("kk", [P, 4, TT])
        kk2 = sb("kk2", [P, 4, TT])
        kp = sb("kp", [P, 4, TT])
        kr = sb("kr", [P, 4, 2, TT])
        bneg = sb("bneg", [P, 4, TT])
        khat = sb("khat", [P, 4, TT])
        bv = sb("bv", [P, 4, TT])
        mt_pt = sb("mt_pt", [P, NCH, PAIRS, 2 * L])
        nt_qt = sb("nt_qt", [P, NCH, PAIRS, 2 * L])
        lev = {n: sb(f"lev{n}", [P, NCH, PAIRS, L]) for n in c["levels"]}
        uinv = sb("uinv", [P, NCH, PAIRS, L])
        v_tok = sb("v_tok", [P, NCH, PAIRS, HEAD])
        b_key = sb("b_key", [P, NCH, PAIRS, HEAD])
        k_key = sb("k_key", [P, NCH, PAIRS, HEAD])
        yb = sb("yb", [P, 4, TT])
        yb2 = sb("yb2", [P, 4, TT])
        fe, att, _, _ = twice("fe_att")
        logf = sb("logf", [P, 4, TT])
        hcum = sb("hcum", [P, 4, TT])
        hk = sb("hk", [P, 4, TT])
        hq = sb("hq", [P, 4, TT])
        hq2 = sb("hq2", [P, 4, TT])
        tq = sb("tq", [P, 4, TT])
        mids = sb("mids", [P, 4 * NCH, 2, NSUB])
        ends = sb("ends", [P, 4 * NCH, 2])
        yd2 = sb("yd2", [P, 4, TT])

        weights_in, states_in = sem("weights_in"), sem("states_in")
        loaded = [sem(f"loaded{j}") for j in range(NB)]
        stored = sem("stored")
        states_stored = sem("states_stored")
        lru_w_clear, masks_made, pool_link = sem("lru_w_clear"), sem("masks_made"), sem("pool_link")
        vec_link, prep_vec, prep_act = sem("vec_link"), sem("prep_vec"), sem("prep_act")
        waits_met = sem("waits_met")
        turned_in, turned_out = sem("turned_in"), sem("turned_out")
        states_set, turn_pe = sem("states_set"), sem("turn_pe")
        table = STEPS.setdefault(tag, {})
        pe_s = Steps(sem("pe_steps"), "pe", table)
        v_s = Steps(sem("vector_steps"), "vector", table)
        a_s = Steps(sem("scalar_steps"), "scalar", table)
        g_s = Steps(sem("pool_steps"), "pool", table)
        all_steps = (pe_s, v_s, a_s, g_s)
        def col(v):
            return v.rearrange("a (t p) -> p (a t)", p=P)

        weights = [
            (conv_b[:, 0:4], col(w["lru_conv_b"])), (conv_b[:, 4:10], col(w["ssd_conv_b"])),
            (lru_b[:, 0, :], col(w["lru_b_r"])), (lru_b[:, 1, :], col(w["lru_b_i"])),
            (lam[:, :], col(w["lru_lambda"])), (mu[:, :], col(w["rwkv_mu"])),
            (up_w[0:64, :], w["rwkv_w_up"][0, :, :]), (up_w[64:128, :], w["rwkv_a_up"][0, :, :]),
            (up_b[:, 0, :], col(w["rwkv_w0"])), (up_b[:, 1, :], col(w["rwkv_a0"])),
            (kvec[:, 0, :], col(w["rwkv_k_k"])), (kvec[:, 1, :], col(w["rwkv_k_a"])),
            (kvec[:, 2, :], col(w["rwkv_r_k"].rearrange("a h k -> a (h k)"))),
            (kvec[:, 3, :], col(w["rwkv_ln_g"])), (kvec[:, 4, :], col(w["rwkv_ln_b"])),
            (gains[:, 0, :], col(w["ssd_norm_g"])), (gains[:, 1, :], col(w["hgrn_norm_g"])),
            (dt_par[:, 0, :], w["ssd_dt_bias"].broadcast_to([P, HEADS])),
            (dt_par[:, 1, :], w["ssd_a_log"].broadcast_to([P, HEADS])),
        ]
        for j in range(CONV_W):
            weights += [(conv_w[:, j, 0:4], col(w["lru_conv_w"][:, j, :])),
                        (conv_w[:, j, 4:10], col(w["ssd_conv_w"][:, j, :]))]
        for h in range(2):
            d = w["ssd_d"].rearrange("a (q h) -> h (a q)", h=2)[h:h + 1, :]
            weights.append((kvec[halves[h], 5, :], d.broadcast_to([64, PAIRS])))
            for g, name in ((0, "lru_w_r"), (1, "lru_w_i")):
                block_w = w[name].rearrange("a (q h) d e -> h d (a q) e", h=2)
                weights.append((lru_w[halves[h], g, :, halves[h]], block_w[h, :, :, :]))

        def state_views(s):
            out = [(lru_h[:, :], col(s["lru_h"].rearrange("a b c -> (a b) c"))),
                   (hg_s[:, :, :], s["hgrn_s"].rearrange("a b (q h) k v -> (h k) (a b q) v", h=2))]
            for h in range(2):
                wk = s["wkv"].rearrange("a b (q h) v k -> h v (a b q) k", h=2)
                out.append((turn[halves[h], 0, :, :], wk[h, :, :, :]))
                sh = s["ssd_h"].rearrange("a b h p n -> p (a b h) n")
                out.append((turn[halves[h], 1, :, :], sh[:, 4 * h:4 * h + 4, :]))
            return out

        LOADS = 9
        TILES = T // TT
        block = ctx.enter_context(nc.Block())

        @block.sync
        def _(sync):
            sync.wait_ge(lru_w_clear, 1)
            for dst, src in weights:
                sync.dma_start(dst, src).then_inc(weights_in, 16)
            if state_in is not None:
                for dst, src in state_views(state_in):
                    sync.dma_start(dst, src).then_inc(states_in, 16)

            def load(i, j):
                t0 = i * TT
                for dst, t, n, off, m in (
                        (conv_in[j][:, 0:4, :], XA, 4, 0, HALO + TT), (conv_in[j][:, 4:10, :], XBC, 6, 0, HALO + TT),
                        (mix_in[j][:, :, :], PB, 13, HALO - 1, 1 + TT), (gate_in[j][:, 0:4, :], GA, 4, HALO, TT),
                        (gate_in[j][:, 4:8, :], GB, 4, HALO, TT), (gate_in[j][:, 8:12, :], Z, 4, HALO, TT),
                        (gate_in[j][:, 12:16, :], GD, 4, HALO, TT), (hg_in[j][:, :, :], QD, 12, HALO, TT)):
                    src = pc[t:t + n, :, bass.ds(t0 + off, m)].rearrange("t p m -> p t m")
                    sync.dma_start(dst, src).then_inc(loaded[j], 16)
                sync.dma_start(dt_in[j][:, :], dtr[bass.ds(t0, TT), :]).then_inc(loaded[j], 16)

            def tile(i, j, more):
                for s in all_steps:
                    s.iteration(i)
                sync.wait_ge(*v_s.at("y_hgrn"))
                sync.sem_inc(waits_met, 1)
                sync.dma_start(yt[:, :, bass.ds(i * TT, TT)].rearrange("t p m -> p t m"),
                               y_out[:, :, :]).then_inc(stored, 16)
                if more:
                    for s in all_steps:
                        s.iteration(i + 1)
                        sync.wait_ge(*s.before())
                        sync.sem_inc(waits_met, 1)
                    load(i + NB, j)

            sync.sem_inc(stored, 16)
            for j in range(NB):
                load(j, j)
            if TILES > NB:
                with sync.Fori(0, TILES // NB - 1) as i:
                    for j in range(NB):
                        tile(NB * i + j, j, True)
            for j in range(NB):
                tile(TILES - NB + j, j, False)
            sync.wait_ge(stored, 16 * (TILES + 1))
            sync.wait_ge(turned_out, 2)
            out = [(src, dst) for dst, src in state_views(state_out)]
            for j in range(HALO):
                for name, a, n in (("lru_conv", 0, 4), ("ssd_conv", 4, 6)):
                    out.append((col(state_out[name][:, 0, j, :]), conv_in[NB - 1][:, a:a + n, TT + j]))
            out.append((col(state_out["shift"][:, 0, :]), mix_in[NB - 1][:, :, TT]))
            for dst, src in out:
                sync.dma_start(dst, src).then_inc(states_stored, 16)
            sync.wait_ge(states_stored, 16 * len(out))

        def each_tile(eng, body):
            def tile(i, j, n):
                for s in all_steps:
                    s.iteration(i)
                for s in all_steps:
                    eng.wait_ge(*s.before())
                eng.wait_ge(loaded[j], 16 * LOADS * (n + 1))
                body(j, i)
            if TILES == NB:
                for j in range(NB):
                    tile(j, j, 0)
            else:
                with eng.Fori(0, TILES // NB) as i:
                    for j in range(NB):
                        tile(NB * i + j, j, i)

        def chunk(ap, k):
            return ap[..., k * L:(k + 1) * L]

        @block.gpsimd
        def _(pool):
            count = [0]

            def link(ins):
                count[0] += 1
                ins.then_inc(pool_link, 1)
                pool.wait_ge(pool_link, count[0])

            link(pool.memset(lru_w[:, :, :, :], 0.0))
            pool.sem_inc(lru_w_clear, 1)
            for k, e in enumerate((1e-12, NORM_EPS, RWKV_LN_EPS)):
                link(pool.memset(eps[:, k:k + 1], e))
            fill_masks(pool, link, c, L)
            pool.sem_inc(masks_made, 1)
            pool.wait_ge(weights_in, 16 * len(weights))

            def body(j, i):
                def mul(o, a, b, name, op=ALU.mult):
                    pool.wait_ge(*g_s.last())
                    pool.tensor_tensor(o, a, b, op).then_inc(*g_s.did(name))

                xin, mi = conv_in[j], mix_in[j]
                mul(xm[:, :, :], mi[:, :, 0:TT], mi[:, :, 1:1 + TT], "shift_diff", ALU.subtract)
                mul(xm[:, :, :], xm[:, :, :], bc(mu[:, :], 2, TT), "shift_mu")
                mul(xm[:, :, :], xm[:, :, :], mi[:, :, 1:1 + TT], "shift", ALU.add)
                mul(kk[:, :, :], xm[:, 4:8, :], bc(kvec[:, 0, :], 2, TT), "kk_raw")
                mul(kk2[:, :, :], kk[:, :, :], kk[:, :, :], "kk_square")
                mul(cv[:, :, :], xin[:, :, 0:TT], bc(conv_w[:, 0, :], 2, TT), "tap0")
                for k in range(1, CONV_W):
                    mul(cv_term[:, :, :], xin[:, :, k:k + TT], bc(conv_w[:, k, :], 2, TT), f"tap{k}")
                    mul(cv[:, :, :], cv[:, :, :], cv_term[:, :, :], f"tap_sum{k}", ALU.add)
                mul(cv[:, :, :], cv[:, :, :], bc(conv_b[:, :], 2, TT), "conv", ALU.add)
                pool.wait_ge(*v_s.at("kp"))
                pool.wait_ge(*pe_s.at("kk_norm"))
                mul(kk2[:, :, :], xm[:, 0:4, :], kp[:, :, :], "rk")
                mul(kk2[:, :, :], kk2[:, :, :], bc(kvec[:, 2, :], 2, TT), "rk_weighed")
                pool.wait_ge(*v_s.at("mt_pt"))
                mt = mt_pt[:, :, :, 0:L].rearrange("p c q t -> p (c q) t")
                both = lambda a, r: a[r].rearrange("p c q t -> p (c q) t")
                for r in rows:
                    mul(both(uinv, r), mt[r], bc(c["up1"][r, :], 1, NCH * PAIRS), f"u_off{r.start}", ALU.mult)
                for r in rows:
                    mul(both(uinv, r), both(uinv, r), bc(c["eye"][r, :], 1, NCH * PAIRS), f"u0{r.start}", ALU.add)
                for n in c["levels"][1:]:
                    for r in rows:
                        mul(both(lev[n], r), mt[r], bc(c[f"up{n}"][r, :], 1, NCH * PAIRS), f"lev{n}_{r.start}", ALU.mult)
                pool.wait_ge(*v_s.at("yc"))
                mul(yc2[:, :, :], yc[:, :, :], yc[:, :, :], "yc_square")
                pool.wait_ge(*v_s.at("yb_centred"))
                mul(yb2[:, :, :], yb[:, :, :], yb[:, :, :], "yb_square")

            g_s.start(pool)
            each_tile(pool, body)

        @block.scalar
        def _(act):
            act.wait_ge(weights_in, 16 * len(weights))
            act.activation(sp[:, 0, :], lam[:, :], ACT.Exp, scale=-1.0).then_inc(prep_act, 1)
            act.activation(neg_a[:, :], dt_par[:, 1, :], ACT.Exp).then_inc(prep_act, 1)
            act.wait_ge(prep_vec, 1)
            act.activation(sp[:, 2, :], sp[:, 1, :], ACT.Ln).then_inc(prep_act, 1)

            def body(j, i):
                def f(o, x, fn, name, scale=1.0, **k):
                    act.activation(o, x, fn, scale=scale, **k).then_inc(*a_s.did(name))

                f(gate[:, :, :], gate_in[j][:, :, :], ACT.Tanh, "gate_tanh", 0.5)
                f(tq[:, :, :], hg_in[j][:, 0:4, :], ACT.Tanh, "q_tanh", 0.5)
                act.wait_ge(*g_s.at("shift"))
                f(tw[:, :], xm[0:64, 12, :], ACT.Tanh, "wl_tanh")
                f(fe[:, :, :], hg_in[j][:, 4:8, :], ACT.Abs, "f_abs")
                act.wait_ge(*a_s.last())
                f(fe[:, :, :], fe[:, :, :], ACT.Exp, "f_exp", -1.0)
                act.wait_ge(*v_s.at("dt_x"))
                f(dts[0:TT, 1, :], dts[0:TT, 0, :], ACT.Abs, "dt_abs")
                act.wait_ge(*a_s.last())
                f(dts[0:TT, 2, :], dts[0:TT, 1, :], ACT.Exp, "dt_exp", -1.0)
                act.wait_ge(*v_s.at("up_biased"))
                f(wa[:, :, :], wa[:, :, :], ACT.Tanh, "wa_tanh", 0.5)
                act.wait_ge(*v_s.at("cum_before"))
                f(e_cum[:, :, :], cum[:, :, :], ACT.Exp, "e_cum")
                f(e_neg[:, :, :], cum[:, :, :], ACT.Exp, "e_neg", -1.0)
                f(cum_b[:, :, :], cum_b[:, :, :], ACT.Exp, "e_before")
                act.wait_ge(*v_s.at("lru_biased"))
                f(ri[:, :, :], ri[:, :, :], ACT.Tanh, "ri_tanh", 0.5)
                act.wait_ge(*v_s.at("lru_s"))
                f(la[:, :, :], ls[:, :, :], ACT.Exp, "lru_a", -1.0)
                f(lth[:, :, :], ls[:, :, :], ACT.Tanh, "lru_th")
                act.wait_ge(*g_s.at("conv"))
                f(xbc[:, :, :], cv[:, 4:10, :], ACT.Tanh, "xbc_tanh", 0.5)
                act.wait_ge(*v_s.at("xbc_twice"))
                f(xbc[:, :, :], xbc[:, :, :], ACT.Copy, "xbc", 0.5)
                act.wait_ge(*v_s.at("f_one_plus"))
                f(logf[:, :, :], logf[:, :, :], ACT.Ln, "f_ln")
                act.wait_ge(*v_s.at("dt_one_plus"))
                f(dts[0:TT, 4, :], dts[0:TT, 3, :], ACT.Ln, "dt_ln")
                act.wait_ge(*pe_s.at("kk_norm"))
                f(yb[:, :, :], ps[:, 4, 0:4 * TT].rearrange("p (q t) -> p q t", q=4), ACT.Ln, "kk_ln", 1.0, bias=eps[:, 0:1])
                act.wait_ge(*v_s.at("one_less_floor"))
                f(lth[:, :, :], lth[:, :, :], ACT.Ln, "one_less_ln")
                act.wait_ge(*a_s.last())
                f(yb[:, :, :], yb[:, :, :], ACT.Exp, "kk_exp", -0.5)
                f(lth[:, :, :], lth[:, :, :], ACT.Exp, "one_less_root", 0.5)
                act.wait_ge(*v_s.at("seg_clamped"))
                f(seg[0:TT, :, :], seg[0:TT, :, :], ACT.Exp, "seg_exp")
                f(e_acs[:, :, :], ps[:, 0, 0:4 * TT].rearrange("p (q t) -> p q t", q=4), ACT.Exp, "e_acs")
                act.wait_ge(*v_s.at("d_last"))
                f(tot[:, 0:4], ps[:, 6, 0:4 * TT].rearrange("p (q t) -> p q t", q=4)[:, :, TT - 1], ACT.Exp, "tot0")
                f(tot[:, 4:8], ps[:, 7, 0:4 * TT].rearrange("p (q t) -> p q t", q=4)[:, :, TT - 1], ACT.Exp, "tot1")
                f(dts[0:TT, 8, :], dts[0:TT, 8, :], ACT.Exp, "d_last_exp")
                act.wait_ge(*pe_s.at("x_tok"))
                f(b_tok[0:TT, :], ps[0:TT, 5, 0:P], ACT.Copy, "b_tok")
                act.wait_ge(*v_s.at("h_kx"))
                f(hk[:, :, :], hk[:, :, :], ACT.Exp, "h_k")
                f(hcum[:, :, :], hcum[:, :, :], ACT.Exp, "h_eq")
                act.wait_ge(*v_s.at("h_spans"))
                f(mids[:, :, :, :].rearrange("p a b u -> p (a b u)"), mids[:, :, :, :].rearrange("p a b u -> p (a b u)"), ACT.Exp, "h_mids")
                f(ends[:, :, :].rearrange("p a b -> p (a b)"), ends[:, :, :].rearrange("p a b -> p (a b)"), ACT.Exp, "h_ends")
                act.wait_ge(*pe_s.at("keys"))
                for r in rows:
                    f(v_tok[r].rearrange("p c q v -> p (c q v)"), ps[r, 3, 0:NCH * 256], ACT.Copy, f"v_tok{r.start}")
                    f(k_key[r].rearrange("p c q v -> p (c q v)"), ps[r, 5, 0:NCH * 256], ACT.Copy, f"k_key{r.start}")
                for n in c["levels"][1:]:
                    last = n == c["levels"][-1]
                    act.wait_ge(*pe_s.at(f"tu{n}"))
                    for r in rows:
                        if not last:
                            f(tinv[r].rearrange("p c q t -> p (c q t)"), ps[r, 7, 0:NCH * 4 * L], ACT.Copy, f"t{n}_{r.start}")
                        f(uinv[r].rearrange("p c q t -> p (c q t)"), ps[r, 0, 0:NCH * 4 * L], ACT.Copy, f"u{n}_{r.start}")
                act.wait_ge(*pe_s.at("h_keys"))
                for r in rows:
                    f(hk_key[r].rearrange("p c q v -> p (c q v)"), ps[r, 7, 0:NCH * 256], ACT.Copy, f"hk_key{r.start}")
                    f(hv_tok[r].rearrange("p c q v -> p (c q v)"), ps[r, 0, 0:NCH * 256], ACT.Copy, f"hv_tok{r.start}")
                act.wait_ge(*pe_s.at("h_out"))
                hp = ps[:, 6, 0:4 * TT].rearrange("p (q t) -> p q t", q=4)
                f(yd2[:, :, :], hp, ACT.Square, "yd_square")
                f(yd[:, :, :], hp, ACT.Copy, "yd_copy")
                act.wait_ge(*pe_s.at("y_rwkv"))
                f(yb[:, :, :], ps[:, 4, 0:4 * TT].rearrange("p (q t) -> p q t", q=4), ACT.Copy, "yb_copy")
                tile_of = lambda b: ps[:, b, 0:4 * TT].rearrange("p (q t) -> p q t", q=4)
                act.wait_ge(*pe_s.at("yb_var"))
                f(rms[:, :], ps[:, 7, 0:TT], ACT.Ln, "yc_ln", bias=eps[:, 1:2])
                f(yd2[:, :, :], tile_of(2), ACT.Ln, "yd_ln", bias=eps[:, 1:2])
                f(yb2[:, :, :], tile_of(1), ACT.Ln, "yb_ln", bias=eps[:, 2:3])
                act.wait_ge(*a_s.last())
                f(rms[:, :], rms[:, :], ACT.Exp, "yc_rms", -0.5)
                f(yd2[:, :, :], yd2[:, :, :], ACT.Exp, "yd_rms", -0.5)
                f(yb2[:, :, :], yb2[:, :, :], ACT.Exp, "yb_rstd", -0.5)

            a_s.start(act)
            each_tile(act, body)

        @block.tensor
        def _(pe):
            pe.wait_ge(masks_made, 1)
            pe.wait_ge(weights_in, 16 * len(weights))
            ident = c["ident"]

            def mm(o, a, b, start=True, stop=True):
                return pe.matmul(o, a, b, start=start, stop=stop)

            def settle():
                pe.sem_inc(waits_met, 1)

            def turn_states(name_sem):
                for k in range(2):
                    src = turn[:, k, :, :] if name_sem is turned_in else (wkv, ssd_h)[k][:, :, :]
                    for h in halves:
                        for q in range(PAIRS):
                            last = mm(ps[h, k, q * HEAD:(q + 1) * HEAD], src[h, q, :], ident[h, h])
                last.then_inc(turn_pe, 1)

            if state_in is not None:
                pe.wait_ge(states_in, 16 * 6)
                turn_states(turned_in)
            pe.wait_ge(states_set, 1)

            def body(j, i):
                def tile_of(b, n=4):
                    return ps[:, b, 0:n * TT].rearrange("p (q t) -> p q t", q=n)
                pe.wait_ge(*a_s.at("wl_tanh"))
                settle()
                for t in range(4):
                    mm(tile_of(2)[:, t, :], up_w[0:64, t * P:(t + 1) * P], tw[:, :])
                for t in range(4):
                    last = mm(tile_of(3)[:, t, :], up_w[64:128, t * P:(t + 1) * P], xm[64:128, 12, :])
                last.then_inc(*pe_s.did("up"))
                pe.wait_ge(*g_s.at("kk_square"))
                settle()
                mm(ps[:, 4, 0:4 * TT], c["headones"][:, :], kk2[:, :, :].rearrange("p a b -> p (a b)")).then_inc(*pe_s.did("kk_norm"))
                pe.wait_ge(*g_s.at("conv"))
                settle()
                for g in range(2):
                    for t in range(4):
                        last = mm(tile_of(g)[:, t, :], lru_w[:, g, t, :], cv[:, t, :])
                last.then_inc(*pe_s.did("lru_gates"))
                pe.wait_ge(*v_s.at("d_a"))
                pe.wait_ge(*v_s.at("lru_biased"))
                settle()
                for h in range(HEADS):
                    row = bc(d_a[0:TT, h], 1, P) if False else d_a[0:TT, h:h + 1].broadcast_to([TT, P])
                    mm(tile_of(6 + h // 4)[:, h % 4, :], row, c["triu"][0:TT, 0:TT])
                for h in range(HEADS):
                    row = d_a[0:TT, h:h + 1].broadcast_to([TT, 64])
                    mm(tile_of(0)[halves[h % 2], h // 2, :], row, c["triu"][0:TT, 0:TT])
                pe.wait_ge(*v_s.at("up_biased"))
                settle()
                mm(ps[0:TT, 3, 0:HEADS], c["triu"][0:TT, 0:TT], d_a[0:TT, :])
                pe.wait_ge(*a_s.at("xbc"))
                settle()
                for g in range(2):
                    last = mm(ps[0:TT, 1 + g, 0:TT], xbc[halves[g], 4, :], xbc[halves[g], 5, :])
                last.then_inc(*pe_s.did("acs"))
                pe.wait_ge(*v_s.at("kk_unit"))
                settle()
                for t in range(4):
                    pe.transpose(ps[0:TT, 4, t * P:(t + 1) * P], xbc[:, t, :], ident[:, :])
                pe.transpose(ps[0:TT, 5, 0:P], xbc[:, 4, :], ident[:, :]).then_inc(*pe_s.did("x_tok"))
                pe.wait_ge(*v_s.at("ssd_scores1"))
                pe.wait_ge(*v_s.at("x_dd"))
                settle()
                for h in range(HEADS):
                    mm(tile_of(1)[halves[h % 2], h // 2, :], x_dt[0:TT, h, :], seg[0:TT, h, :])
                for h in range(HEADS):
                    g = h // 4
                    mm(ps[halves[h % 2], 2 + g, (h // 2 - 2 * g) * TT:(h // 2 - 2 * g + 1) * TT],
                       ssd_h[halves[g], h % 4, :], xbc[halves[g], 5, :])
                pe.wait_ge(*a_s.at("b_tok"))
                settle()
                for g in range(2):
                    last = mm(ps[halves[g], 4, 0:4 * HEAD], b_tok[0:TT, halves[g]],
                              x_dd[0:TT, 4 * g:4 * g + 4, :].rearrange("p h v -> p (h v)"))
                last.then_inc(*pe_s.did("ssd"))
                pe.wait_ge(*g_s.at("rk_weighed"))
                settle()
                mm(ps[:, 5, 0:4 * TT], c["headones"][:, :], kk2[:, :, :].rearrange("p a b -> p (a b)")).then_inc(*pe_s.did("bonus"))
                pe.wait_ge(*v_s.at("khat"))
                pe.wait_ge(*a_s.at("tot1"))
                pe.wait_ge(*v_s.at("d_last"))
                pe.wait_ge(*v_s.at("yc_intra"))
                settle()
                for k in range(NCH):
                    for b, left in ((6, bneg), (0, khat)):
                        for h in range(HEADS):
                            hh, q = h % 2, h // 2
                            mm(ps[hrows[hh], b + k, q * 2 * L:(q + 1) * 2 * L].rearrange("p (a t) -> p a t", a=2),
                               chunk(left[halves[hh], q, :], k), chunk(kr[halves[hh], q, :, :], k))
                    for h in range(HEADS):
                        hh, q = h % 2, h // 2
                        last = mm(ps[hrows[hh], 2, (k * PAIRS + q) * L:(k * PAIRS + q + 1) * L],
                                  chunk(kr[halves[hh], q, 0, :], k), chunk(bneg[halves[hh], q, :], k))
                last.then_inc(*pe_s.did("mats"))
                pe.wait_ge(*v_s.at("bonus_v"))
                pe.wait_ge(*v_s.at("ssd_state"))
                settle()
                for b, src in ((3, xm[:, 8:12, :]), (4, bneg[:, :, :]), (5, khat[:, :, :])):
                    for k in range(NCH):
                        for h in range(HEADS):
                            hh, q = h % 2, h // 2
                            o = ps[hrows[hh], b, (k * PAIRS + q) * HEAD:(k * PAIRS + q + 1) * HEAD]
                            last = mm(o, chunk(src[halves[hh], q, :], k), ident[halves[hh], halves[hh]])
                last.then_inc(*pe_s.did("keys"))
                for n in c["levels"][1:]:
                    first, final = n == 2, n == c["levels"][-1]
                    if first:
                        pe.wait_ge(*v_s.at("t0"))
                        pe.wait_ge(*g_s.at(f"lev{c['levels'][-1]}_{rows[-1].start}"))
                        settle()
                    else:
                        pe.wait_ge(*a_s.at(f"u{n // 2}_{rows[-1].start}"))
                        settle()

                    def each(b, left, right):
                        for k in range(NCH):
                            for h in range(HEADS):
                                hh, q = h % 2, h // 2
                                last = mm(ps[hrows[hh], b, (k * PAIRS + q) * L:(k * PAIRS + q + 1) * L],
                                          left[hrows[hh], k, q, :], right[hrows[hh], k, q, :])
                        return last
                    each(6, lev[n], tinv).then_inc(*pe_s.did(f"q{n}"))
                    pe.wait_ge(*v_s.at(f"qi{n}_{rows[-1].start}"))
                    settle()
                    if not final:
                        each(7, uinv, qi)
                    each(0, qi, uinv).then_inc(*pe_s.did(f"tu{n}"))
                pe.wait_ge(*v_s.at("h_q2"))
                settle()
                for k in range(NCH):
                    for h in range(HEADS):
                        hh, q = h % 2, h // 2
                        mm(ps[hrows[hh], 5, (k * PAIRS + q) * L:(k * PAIRS + q + 1) * L],
                           chunk(hk[halves[hh], q, :], k), chunk(hq[halves[hh], q, :], k))
                if NSUB == 2:
                    for k in range(NCH):
                        for h in range(HEADS):
                            hh, q = h % 2, h // 2
                            o = ps[64 * hh:64 * hh + SUB, 6, (k * PAIRS + q) * SUB:(k * PAIRS + q + 1) * SUB]
                            mm(o, hk[halves[hh], q, k * L:k * L + SUB], hq2[halves[hh], q, k * L + SUB:(k + 1) * L])
                pe.wait_ge(*a_s.at(f"u{c['levels'][-1]}_{rows[-1].start}"))
                pe.wait_ge(*v_s.at("h_k2"))
                settle()
                for b, src in ((7, logf[:, :, :]), (0, hg_in[j][:, 8:12, :])):
                    for k in range(NCH):
                        for h in range(HEADS):
                            hh, q = h % 2, h // 2
                            o = ps[hrows[hh], b, (k * PAIRS + q) * HEAD:(k * PAIRS + q + 1) * HEAD]
                            last = mm(o, chunk(src[halves[hh], q, :], k), ident[halves[hh], halves[hh]])
                last.then_inc(*pe_s.did("h_keys"))
                for k in range(NCH):
                    for h in range(HEADS):
                        hh, q = h % 2, h // 2
                        o = ps[hrows[hh], 1, q * HEAD:(q + 1) * HEAD]
                        if k and h == 0:
                            pe.wait_ge(*v_s.at(f"wkv{k - 1}"))
                            settle()
                        mm(o, chunk(kr[halves[hh], q, 0, :], k), wkv[halves[hh], q, :], True, False)
                        last = mm(o, nt_qt[hrows[hh], k, q, 0:L], v_tok[hrows[hh], k, q, :], False, True)
                    last.then_inc(*pe_s.did(f"rhs{k}"))
                    pe.wait_ge(*v_s.at(f"rhs{k}_{rows[-1].start}"))
                    settle()
                    for h in range(HEADS):
                        hh, q = h % 2, h // 2
                        last = mm(ps[hrows[hh], 2, q * HEAD:(q + 1) * HEAD], uinv[hrows[hh], k, q, :], rhs[hrows[hh], q, :])
                    last.then_inc(*pe_s.did(f"sa{k}"))
                    pe.wait_ge(*v_s.at(f"sa{k}_{rows[-1].start}"))
                    settle()
                    for h in range(HEADS):
                        hh, q = h % 2, h // 2
                        o = ps[halves[hh], 3, q * HEAD:(q + 1) * HEAD]
                        mm(o, b_key[hrows[hh], k, q, :], sa[hrows[hh], q, :], True, False)
                        last = mm(o, k_key[hrows[hh], k, q, :], v_tok[hrows[hh], k, q, :], False, True)
                    for h in range(HEADS):
                        hh, q = h % 2, h // 2
                        o = chunk(ps[halves[hh], 4, q * TT:(q + 1) * TT], k)
                        mm(o, wkv[halves[hh], q, :], chunk(kr[halves[hh], q, 1, :], k), True, False)
                        mm(o, sa[hrows[hh], q, :], mt_pt[hrows[hh], k, q, L:2 * L], False, False)
                        last = mm(o, v_tok[hrows[hh], k, q, :], nt_qt[hrows[hh], k, q, L:2 * L], False, True)
                    last.then_inc(*pe_s.did(f"y_rwkv" if k == NCH - 1 else f"y_rwkv{k}"))
                pe.wait_ge(*a_s.at(f"hv_tok{rows[-1].start}"))
                pe.wait_ge(*v_s.at("att"))
                settle()
                for k in range(NCH):
                    for h in range(HEADS):
                        hh, q = h % 2, h // 2
                        last = mm(ps[halves[hh], 5, (k * PAIRS + q) * HEAD:(k * PAIRS + q + 1) * HEAD],
                                  hk_key[hrows[hh], k, q, :], hv_tok[hrows[hh], k, q, :])
                last.then_inc(*pe_s.did("h_kv"))
                pe.wait_ge(*v_s.at("h_states"))
                settle()
                for k in range(NCH):
                    for h in range(HEADS):
                        hh, q = h % 2, h // 2
                        o = chunk(ps[halves[hh], 6, q * TT:(q + 1) * TT], k)
                        mm(o, hs_mid[halves[hh], k, q, :], chunk(hq2[halves[hh], q, :], k), True, False)
                        last = mm(o, hv_tok[hrows[hh], k, q, :], att[hrows[hh], k, q, :], False, True)
                last.then_inc(*pe_s.did("h_out"))
                pe.wait_ge(*g_s.at("yc_square"))
                settle()
                for t in range(4):
                    last = mm(ps[:, 7, 0:TT], c["ones"][:, :], yc2[:, t, :], t == 0, t == 3)
                last.then_inc(*pe_s.did("yc_ms"))
                flat = lambda x: x[:, :, :].rearrange("p a b -> p (a b)")
                pe.wait_ge(*a_s.at("yb_copy"))
                settle()
                mm(ps[:, 0, 0:4 * TT], c["headmean"][:, :], flat(yb)).then_inc(*pe_s.did("yb_mean"))
                pe.wait_ge(*a_s.at("yd_square"))
                settle()
                mm(ps[:, 2, 0:4 * TT], c["headmean"][:, :], flat(yd2)).then_inc(*pe_s.did("yd_ms"))
                pe.wait_ge(*g_s.at("yb_square"))
                settle()
                mm(ps[:, 1, 0:4 * TT], c["headmean"][:, :], flat(yb2)).then_inc(*pe_s.did("yb_var"))

            pe_s.start(pe)
            each_tile(pe, body)
            for s in all_steps:
                s.iteration(TILES)
                pe.wait_ge(*s.before())
                settle()
            turn_states(turned_out)

        @block.vector
        def _(vec):
            count = [0]

            def link(ins):
                count[0] += 1
                ins.then_inc(vec_link, 1)
                vec.wait_ge(vec_link, count[0])

            vec.wait_ge(masks_made, 1)
            vec.wait_ge(weights_in, 16 * len(weights))
            vec.wait_ge(prep_act, 2)
            vec.tensor_scalar(sp[:, 1, :], sp[:, 0, :], 1.0, None, ALU.add).then_inc(prep_vec, 1)
            vec.wait_ge(prep_vec, 1)
            vec.wait_ge(prep_act, 3)
            log1p(vec, link, sp[:, 0, :], sp[:, 1, :], sp[:, 2, :], sp[:, 3, :], ls[:, 0:4, 0])
            link(vec.tensor_scalar(sp[:, 3, :], sp[:, 3, :], LRU_C / 2, None, ALU.mult))
            link(vec.tensor_scalar(half_ka[:, :], kvec[:, 1, :], 0.5, None, ALU.mult))
            link(vec.tensor_scalar(neg_a[:, :], neg_a[:, :], -1.0, None, ALU.mult))
            if state_in is None:
                for s in (lru_h[:, :], wkv[:, :, :], ssd_h[:, :, :], hg_s[:, :, :]):
                    link(vec.memset(s, 0.0))
            else:
                vec.wait_ge(turn_pe, 1)
                for k, s in enumerate((wkv, ssd_h)):
                    link(vec.tensor_copy(s[:, :, :].rearrange("p q v -> p (q v)"), ps[:, k, 0:4 * HEAD]))
            vec.sem_inc(states_set, 1)

            def body(j, i):
                vec.wait_ge(stored, 16 * i + 16)
                tt = lambda o, a, b, op, name: vec.tensor_tensor(o, a, b, op).then_inc(*v_s.did(name))
                ts = lambda o, a, s1, s2, op0, op1, name: vec.tensor_scalar(o, a, s1, s2, op0, op1).then_inc(*v_s.did(name)) if op1 is not None else vec.tensor_scalar(o, a, s1, None, op0).then_inc(*v_s.did(name))
                stt = lambda o, a, s1, b, op0, op1, name: vec.scalar_tensor_tensor(o, a, s1, b, op0, op1).then_inc(*v_s.did(name))
                def own():
                    vec.wait_ge(*v_s.last())
                MUL, ADD, SUB_ = ALU.mult, ALU.add, ALU.subtract
                four = lambda b: ps[:, b, 0:4 * TT].rearrange("p (q t) -> p q t", q=4)
                eight = lambda b: ps[:, b:b + 2, 0:4 * TT].rearrange("p b (q t) -> p b q t", q=4)
                as8 = lambda x: x[:, :, :].rearrange("p (b q) t -> p b q t", b=2)
                fd = hg_in[j][:, 4:8, :]
                tt(dts[0:TT, 0, :], dt_in[j][:, :], dt_par[0:TT, 0, :], ADD, "dt_x")
                vec.wait_ge(*a_s.at("gate_tanh"))
                stt(gate[:, :, :], gate[:, :, :], 1.0, gate_in[j][:, :, :], ADD, MUL, "gates")
                vec.wait_ge(*a_s.at("q_tanh"))
                stt(tq[:, :, :], tq[:, :, :], 1.0, hg_in[j][:, 0:4, :], ADD, MUL, "q_twice")
                vec.wait_ge(*a_s.at("f_exp"))
                ts(logf[:, :, :], fe[:, :, :], 1.0, None, ADD, None, "f_one_plus")
                vec.wait_ge(*a_s.at("dt_exp"))
                ts(dts[0:TT, 3, :], dts[0:TT, 2, :], 1.0, None, ADD, None, "dt_one_plus")
                vec.wait_ge(*pe_s.at("up"))
                tt(as8(wa), eight(2), bc(up_b[:, :, :], 3, TT), ADD, "up_biased")
                vec.wait_ge(*a_s.at("wa_tanh"))
                ts(wa[:, 0:4, :], wa[:, 0:4, :], -DECAY_SCALE / 2, -DECAY_SCALE / 2, MUL, ADD, "log_w")
                own()
                vec.tensor_tensor_scan(cum[:, :, :].rearrange("p a t -> p (a t)"), c["first"][:, 0:4 * TT],
                                       wa[:, 0:4, :].rearrange("p a t -> p (a t)"), 0.0, MUL, ADD).then_inc(*v_s.did("cum"))
                own()
                tt(cum_b[:, :, :], cum[:, :, :], wa[:, 0:4, :], SUB_, "cum_before")
                stt(kp[:, :, :], wa[:, 4:8, :], -1.0, bc(half_ka[:, :], 2, TT), ADD, MUL, "kp_factor")
                own()
                stt(kp[:, :, :], kp[:, :, :], 1.0, xm[:, 4:8, :], ADD, MUL, "kp")
                own()
                vec.wait_ge(*pe_s.at("lru_gates"))
                tt(as8(ri), eight(0), bc(lru_b[:, :, :], 3, TT), ADD, "lru_biased")
                vec.wait_ge(*a_s.at("ri_tanh"))
                stt(ls[:, :, :], ri[:, 0:4, :], 1.0, bc(sp[:, 3, :], 2, TT), ADD, MUL, "lru_s")
                stt(lu[:, :, :], ri[:, 4:8, :], 1.0, cv[:, 0:4, :], ADD, MUL, "lru_ix")
                vec.wait_ge(*a_s.at("xbc_tanh"))
                stt(xbc[:, :, :], xbc[:, :, :], 1.0, cv[:, 4:10, :], ADD, MUL, "xbc_twice")
                vec.wait_ge(*a_s.at("lru_th"))
                tt(ls[:, :, :], la[:, :, :], la[:, :, :], MUL, "a_square")
                own()
                stt(lth[:, :, :], ls[:, :, :], 1.0, lth[:, :, :], ADD, MUL, "one_less")
                own()
                ts(lth[:, :, :], lth[:, :, :], 1e-18, None, ALU.max, None, "one_less_floor")
                vec.wait_ge(*a_s.at("kk_exp"))
                tt(kk[:, :, :], kk[:, :, :], yb[:, :, :], MUL, "kk_unit")
                own()
                tt(kr[:, :, 0, :], kk[:, :, :], cum_b[:, :, :], MUL, "kappa")
                tt(kr[:, :, 1, :], xm[:, 0:4, :], e_cum[:, :, :], MUL, "r_hat")
                stt(bneg[:, :, :], wa[:, 4:8, :], 1.0, kk[:, :, :], ADD, MUL, "b_twice")
                own()
                stt(bneg[:, :, :], bneg[:, :, :], -0.5, e_neg[:, :, :], MUL, MUL, "bneg")
                tt(khat[:, :, :], kp[:, :, :], e_neg[:, :, :], MUL, "khat")
                vec.wait_ge(*a_s.at("one_less_root"))
                stt(lu[:, :, :], lu[:, :, :], 0.5, lth[:, :, :], MUL, MUL, "lru_u")
                own()
                tt(sp[:, 0, :], la[:, :, 0], lru_h[:, :], MUL, "lru_carry")
                own()
                tt(lu[:, :, 0], lu[:, :, 0], sp[:, 0, :], ADD, "lru_u0")
                vec.memset(la[:, :, 0:1], 0.0).then_inc(*v_s.did("lru_cut"))
                own()
                vec.tensor_tensor_scan(ls[:, :, :].rearrange("p a t -> p (a t)"), la[:, :, :].rearrange("p a t -> p (a t)"),
                                       lu[:, :, :].rearrange("p a t -> p (a t)"), 0.0, MUL, ADD).then_inc(*v_s.did("lru_h"))
                own()
                vec.tensor_copy(lru_h[:, :], ls[:, :, TT - 1]).then_inc(*v_s.did("lru_state"))
                stt(y_out[:, 0:4, :], ls[:, :, :], 0.5, gate[:, 0:4, :], MUL, MUL, "y_lru")
                vec.wait_ge(*a_s.at("dt_ln"))
                named_log1p(vec, v_s, dts[0:TT, 2, :], dts[0:TT, 3, :], dts[0:TT, 4, :], dts[0:TT, 5, :], dts[0:TT, 6, :], "dt")
                own()
                stt(dts[0:TT, 7, :], dts[0:TT, 0, :], 0.0, dts[0:TT, 5, :], ALU.max, ADD, "dt")
                own()
                tt(d_a[0:TT, :], dts[0:TT, 7, :], neg_a[0:TT, :], MUL, "d_a")
                vec.wait_ge(*a_s.at("f_ln"))
                stt(logf[:, :, :], fd, 0.0, logf[:, :, :], ALU.min, SUB_, "logf")
                own()
                tt(hk[:, :, :], logf[:, :, :], fd, SUB_, "log_k")
                vec.tensor_tensor_scan(hcum[:, :, :].rearrange("p a t -> p (a t)"), c["first"][:, 0:4 * TT],
                                       logf[:, :, :].rearrange("p a t -> p (a t)"), 0.0, MUL, ADD).then_inc(*v_s.did("h_cum"))
                own()
                blocks = hcum[:, :, :].rearrange("p a (c u t) -> p (a c) u t", c=NCH, u=NSUB)
                mid = blocks[:, :, :, SUB // 2 - 1]
                end = blocks[:, :, NSUB - 1, SUB - 1]
                vec.tensor_copy(ends[:, :, 0], mid[:, :, 0]).then_inc(*v_s.did("h_m0"))
                vec.tensor_copy(ends[:, :, 1], end).then_inc(*v_s.did("h_end"))
                own()
                tt(mids[:, :, 0, :], mid, bc(ends[:, :, 0], 2, NSUB), SUB_, "h_mid_span")
                tt(mids[:, :, 1, :], bc(ends[:, :, 1], 2, NSUB), mid, SUB_, "h_spans")
                vec.tensor_copy(yd2[:, 0, 0:4 * NCH * NSUB].rearrange("p (a u) -> p a u", u=NSUB), mid).then_inc(*v_s.did("h_mid"))
                own()
                b3 = hcum[:, :, :].rearrange("p a (m t) -> p (a m) t", t=SUB)
                tt(b3, b3, bc(yd2[:, 0, 0:4 * NCH * NSUB], 2, SUB), SUB_, "h_rel")
                own()
                tt(hk[:, :, :], hk[:, :, :], hcum[:, :, :], SUB_, "h_kx")
                vec.wait_ge(*pe_s.at("acs"))
                vec.tensor_copy(acs[0:TT, :], ps[0:TT, 3, 0:HEADS]).then_inc(*v_s.did("acs"))
                own()
                seg4 = seg[0:TT, :, :].rearrange("p (b q) t -> p b q t", b=2)
                tt(seg4, eight(6)[0:TT], bc(acs[0:TT, :], 2, TT).rearrange("p (b q) t -> p b q t", b=2), SUB_, "seg")
                own()
                ts(seg[0:TT, :, :], seg[0:TT, :, :], 0.0, None, ALU.min, None, "seg_clamped")
                for b in range(2):
                    tt(dts[0:TT, 8, 4 * b:4 * b + 4], ps[0:TT, 6 + b, 0:4 * TT].rearrange("p (q t) -> p q t", q=4)[:, :, TT - 1],
                       acs[0:TT, 4 * b:4 * b + 4], SUB_, f"d_last" if b else "d_last0")
                for g in range(2):
                    tt(cb[0:TT, g, :], ps[0:TT, 1 + g, 0:TT], c["triu"][0:TT, 0:TT], MUL, f"cb{g}")
                vec.wait_ge(*pe_s.at("x_tok"))
                x_tok = ps[0:TT, 4, 0:D_GROUP].rearrange("p (h v) -> p h v", h=HEADS)
                tt(x_dt[0:TT, :, :], x_tok, bc(dts[0:TT, 7, :], 2, HEAD), MUL, "x_dt")
                vec.wait_ge(*a_s.at("d_last_exp"))
                tt(dts[0:TT, 9, :], dts[0:TT, 8, :], dts[0:TT, 7, :], MUL, "d_last_dt")
                own()
                tt(x_dd[0:TT, :, :], x_tok, bc(dts[0:TT, 9, :], 2, HEAD), MUL, "x_dd")
                vec.wait_ge(*a_s.at("seg_exp"))
                for g in range(2):
                    sg = seg[0:TT, 4 * g:4 * g + 4, :]
                    tt(sg, sg, bc(cb[0:TT, g, :], 1, 4), MUL, f"ssd_scores{g}")
                tt(yc[:, :, :], xbc[:, 0:4, :], bc(kvec[:, 5, :], 2, TT), MUL, "d_x")
                vec.wait_ge(*pe_s.at("ssd"))
                vec.wait_ge(*a_s.at("tot1"))
                y2 = yc2[:, :, :].rearrange("p (b q) t -> p b q t", b=2)
                tt(y2, ps[:, 2:4, 0:2 * TT].rearrange("p b (q t) -> p b q t", q=2),
                   e_acs[:, :, :].rearrange("p (b q) t -> p b q t", b=2), MUL, "yc_inter")
                own()
                tt(yc[:, :, :], yc[:, :, :], yc2[:, :, :], ADD, "yc_sum")
                own()
                tt(yc[:, :, :], yc[:, :, :], four(1), ADD, "yc_intra")
                own()
                stt(yc[:, :, :], yc[:, :, :], 0.5, gate[:, 8:12, :], MUL, MUL, "yc")
                for g in range(2):
                    hg = ssd_h[halves[g], :, :]
                    tt(hg, hg, bc(tot[halves[g], 4 * g:4 * g + 4], 2, HEAD), MUL, f"ssd_decay{g}")
                own()
                tt(ssd_h[:, :, :].rearrange("p q v -> p (q v)"), ssd_h[:, :, :].rearrange("p q v -> p (q v)"),
                   ps[:, 4, 0:4 * HEAD], ADD, "ssd_state")
                vec.wait_ge(*pe_s.at("bonus"))
                tt(bv[:, :, :], four(5), xm[:, 8:12, :], MUL, "bonus_v")
                vec.wait_ge(*pe_s.at("mats"))
                for b, dst, name in ((6, mt_pt, "mt_pt"), (0, nt_qt, "nt_qt")):
                    for r in rows:
                        tt(dst[r].rearrange("p c q t -> p c (q t)").rearrange("p c (q t) -> p c q t", q=PAIRS),
                           ps[r, b:b + NCH, 0:8 * L].rearrange("p c (q t) -> p c q t", q=PAIRS),
                           bc(bc(c["causal"][r, :, :].rearrange("p a t -> p (a t)"), 1, PAIRS), 1, NCH), MUL,
                           name if r is rows[-1] else f"{name}_0")
                for r in rows:
                    tt(tinv[r].rearrange("p c q t -> p (c q) t"), ps[r, 2, 0:NCH * 4 * L].rearrange("p (m t) -> p m t", t=L),
                       bc(c["low1"][r, :], 1, NCH * PAIRS), MUL, f"t_off{r.start}")
                own()
                for r in rows:
                    tt(tinv[r].rearrange("p c q t -> p (c q) t"), tinv[r].rearrange("p c q t -> p (c q) t"),
                       bc(c["eye"][r, :], 1, NCH * PAIRS), ADD, "t0" if r is rows[-1] else "t0_0")
                vec.wait_ge(*pe_s.at("keys"))
                for r in rows:
                    vec.tensor_copy(b_key[r].rearrange("p c q v -> p (c q v)"), ps[r, 4, 0:NCH * 256]).then_inc(*v_s.did(f"b_key{r.start}"))
                def qi_step(n):
                    vec.wait_ge(*pe_s.at(f"q{n}"))
                    for r in rows:
                        tt(qi[r].rearrange("p c q t -> p (c q) t"), ps[r, 6, 0:NCH * 4 * L].rearrange("p (m t) -> p m t", t=L),
                           bc(c["eye"][r, :], 1, NCH * PAIRS), ADD, f"qi{n}_{r.start}")
                levels = c["levels"][1:]
                qi_step(levels[0])
                vec.wait_ge(*a_s.at("h_eq"))
                stt(hq[:, :, :], tq[:, :, :], 0.5, hcum[:, :, :], MUL, MUL, "h_q")
                own()
                qi_step(levels[1])
                vec.wait_ge(*a_s.at("h_ends"))
                q3 = lambda x: x[:, :, :].rearrange("p a (c u t) -> p (a c) u t", c=NCH, u=NSUB)
                tt(q3(hq2), q3(hq), bc(mids[:, :, 0, :], 3, SUB), MUL, "h_q2")
                if len(levels) > 2: qi_step(levels[2])
                tt(q3(logf), q3(hk), bc(mids[:, :, 1, :], 3, SUB), MUL, "h_k2")
                for n in levels[3:]:
                    qi_step(n)
                vec.wait_ge(*pe_s.at("h_keys"))
                for r in rows:
                    tt(att[r].rearrange("p c q t -> p (c q) t"), ps[r, 5, 0:NCH * 4 * L].rearrange("p (m t) -> p m t", t=L),
                       bc(c["subcausal"][r, :], 1, NCH * PAIRS), MUL, f"att_own{r.start}")
                own()
                if NSUB == 2:
                    for h in range(2):
                        r = slice(64 * h, 64 * h + SUB)
                        vec.tensor_copy(att[r].rearrange("p c q t -> p (c q) t")[:, :, SUB:L],
                                        ps[r, 6, 0:NCH * 4 * SUB].rearrange("p (m t) -> p m t", t=SUB)).then_inc(*v_s.did("att" if h else "att_0"))
                else:
                    vec.tensor_copy(sp[:, 0, :], sp[:, 1, :]).then_inc(*v_s.did("att"))
                for k in range(NCH):
                    for stage, b, dst in (("rhs", 1, rhs), ("sa", 2, sa)):
                        vec.wait_ge(*pe_s.at(f"{stage}{k}"))
                        for r in rows:
                            vec.tensor_copy(dst[r].rearrange("p q v -> p (q v)"), ps[r, b, 0:256]).then_inc(*v_s.did(f"{stage}{k}_{r.start}"))
                    vec.wait_ge(*pe_s.at("y_rwkv" if k == NCH - 1 else f"y_rwkv{k}"))
                    tt(wkv[:, :, :].rearrange("p q v -> p (q v)"), wkv[:, :, :].rearrange("p q v -> p (q v)"), ps[:, 3, 0:256], ADD, f"wkv_sum{k}")
                    own()
                    tt(wkv[:, :, :], wkv[:, :, :], bc(e_cum[:, :, (k + 1) * L - 1], 2, HEAD), MUL, f"wkv{k}")
                vec.wait_ge(*pe_s.at("h_kv"))
                own()
                e2 = ends[:, :, :].rearrange("p (a c) b -> p a c b", c=NCH)
                for k in range(NCH):
                    tt(hs_mid[:, k, :, :], hg_s[:, :, :], bc(e2[:, :, k, 0], 2, HEAD), MUL, f"h_smid{k}")
                    tt(hg_s[:, :, :], hg_s[:, :, :], bc(e2[:, :, k, 1], 2, HEAD), MUL, f"h_decay{k}")
                    own()
                    tt(hg_s[:, :, :].rearrange("p q v -> p (q v)"), hg_s[:, :, :].rearrange("p q v -> p (q v)"),
                       ps[:, 5, k * 256:(k + 1) * 256], ADD, "h_states" if k == NCH - 1 else f"h_state{k}")
                    own()
                vec.wait_ge(*pe_s.at("yb_mean"))
                tt(yb[:, :, :], yb[:, :, :], four(0), SUB_, "yb_centred")
                vec.wait_ge(*a_s.at("yc_rms"))
                tt(yc[:, :, :], yc[:, :, :], bc(rms[:, :], 1, 4), MUL, "yc_normed")
                own()
                tt(y_out[:, 8:12, :], yc[:, :, :], bc(gains[:, 0, :], 2, TT), MUL, "y_ssd")
                vec.wait_ge(*a_s.at("yb_rstd"))
                tt(yb[:, :, :], yb[:, :, :], yb2[:, :, :], MUL, "yb_normed")
                tt(yd[:, :, :], yd[:, :, :], yd2[:, :, :], MUL, "yd_normed")
                own()
                tt(yb[:, :, :], yb[:, :, :], bc(kvec[:, 3, :], 2, TT), MUL, "yb_gain")
                tt(yd[:, :, :], yd[:, :, :], bc(gains[:, 1, :], 2, TT), MUL, "yd_gain")
                own()
                tt(yb[:, :, :], yb[:, :, :], bc(kvec[:, 4, :], 2, TT), ADD, "yb_bias")
                own()
                tt(yb[:, :, :], yb[:, :, :], bv[:, :, :], ADD, "yb_bonus")
                own()
                stt(y_out[:, 4:8, :], yb[:, :, :], 0.5, gate[:, 4:8, :], MUL, MUL, "y_rwkv")
                stt(y_out[:, 12:16, :], yd[:, :, :], 0.5, gate[:, 12:16, :], MUL, MUL, "y_hgrn")

            v_s.start(vec)
            each_tile(vec, body)
            vec.wait_ge(turn_pe, 2 if state_in is not None else 1)
            for k in range(2):
                vec.tensor_copy(turn[:, k, :, :].rearrange("p q v -> p (q v)"), ps[:, k, 0:4 * HEAD]).then_inc(turned_out, 1)


def log1p(vec, link, e, u, ln_u, out, tmp):
    link(vec.tensor_scalar(out, u, -1.0, None, ALU.add))
    link(vec.tensor_scalar(tmp, out, 0.0, None, ALU.is_equal))
    link(vec.tensor_tensor(out, out, tmp, ALU.add))
    link(vec.reciprocal(out, out))
    link(vec.tensor_tensor(tmp, ln_u, tmp, ALU.add))
    link(vec.tensor_tensor(tmp, tmp, e, ALU.mult))
    link(vec.tensor_tensor(out, out, tmp, ALU.mult))


def named_log1p(vec, steps, e, u, ln_u, out, tmp, name):
    n = [0]

    def link(ins):
        n[0] += 1
        ins.then_inc(*steps.did(f"{name}_log1p{n[0]}"))
        vec.wait_ge(*steps.last())

    log1p(vec, link, e, u, ln_u, out, tmp)


def memory_pass(nc, mem_prompt, mem_g, w_k, w_v, w_q, w_o, g_pre_x, cache_k, cache_v, mem_k, mem_v, qk, vo):
    MT = MEM_LEN // P

    with ExitStack() as ctx:
        def sb(name, shape):
            return ctx.enter_context(nc.sbuf_tensor(f"mem_{name}", shape, F32))

        def sem(name):
            return ctx.enter_context(nc.semaphore(f"mem_{name}"))

        ctx.enter_context(nc.allow_non_contiguous_dma(reason="vectors over channels, once"))
        wq = sb("wq", [P, KT, D_MODEL])
        wqT = sb("wqT", [P, KT, D_MODEL])
        wo = sb("wo", [P, KT, D_MODEL])
        w_half = [sb(f"w_half{j}", [P, KT, BANK]) for j in range(2)]
        mem = sb("mem", [P, MT, D_MODEL])
        memT = sb("memT", [P, KT, MEM_LEN])
        kv = sb("kv", [P, 2, MT, D_MODEL])
        kvT = sb("kvT", [P, 2, KT, MEM_LEN])
        out = [sb(f"out{j}", [P, D_MODEL]) for j in range(2)]
        gains = sb("gains", [P, 2, KT])
        rstd = sb("rstd", [P, MT])
        eps = sb("eps", [P, 1])
        ident = sb("ident", [P, P])
        ps = ctx.enter_context(nc.psum_tensor("mem_ps", [P, 8, BANK], F32))

        loaded, wq_in, wo_in = sem("loaded"), sem("wq_in"), sem("wo_in")
        half_in = [sem(f"half_in{j}") for j in range(2)]
        link_s, const_made, act_link = sem("link"), sem("const_made"), sem("act_link")
        normed, filled, emptied = sem("normed"), sem("filled"), sem("emptied")
        cache_in, kv_stored, stored = sem("cache_in"), sem("kv_stored"), [sem(f"stored{j}") for j in range(2)]
        kv_turned = sem("kv_turned")
        block = ctx.enter_context(nc.Block())

        fills = [("memT", m) for m in range(MT)]
        fills += [("kv", (a, m)) for a in range(2) for m in range(MT)]
        fills += [("wqT", k) for k in range(KT)]
        for g in range(2):
            fills += [("kvT", (g, a, m)) for a in range(2) for m in range(MT)]
            fills += [("qk", (g, k)) for k in range(KT)]
            fills += [("vo", (g, k)) for k in range(KT)]
        at = {f: n for n, f in enumerate(fills)}
        pair = lambda n: slice(2 * (n % 4), 2 * (n % 4) + 2)
        n_out = {}
        for f in fills:
            if f[0] in ("qk", "vo"):
                n_out[f] = len(n_out)

        @block.sync
        def _(sync):
            sync.dma_start(mem[:, :, :], mem_prompt[0, :, :].rearrange("(m p) d -> p m d", p=P)).then_inc(loaded, 16)
            sync.dma_start(gains[:, 0, :], mem_g.rearrange("a (k p) -> p (a k)", p=P)).then_inc(loaded, 16)
            sync.dma_start(gains[:, 1, :], g_pre_x.rearrange("a (k p) -> p (a k)", p=P)).then_inc(loaded, 16)
            rows_of = lambda w: w[0, :, :].rearrange("(k p) n -> p k n", p=P)
            for a, w in enumerate((w_k, w_v)):
                for half in range(2):
                    if a:
                        sync.wait_ge(filled, at[("kv", (0, MT - 1))] + 1)
                    sync.dma_start(w_half[half][:, :, :], rows_of(w)[:, :, half * BANK:(half + 1) * BANK]).then_inc(half_in[half], 16)
                if not a:
                    sync.dma_start(wq[:, :, :], rows_of(w_q)).then_inc(wq_in, 16)
                    sync.dma_start(wo[:, :, :], rows_of(w_o)).then_inc(wo_in, 16)
            sync.wait_ge(emptied, at[("kv", (1, MT - 1))] + 1)
            for a, dst in enumerate((mem_k, mem_v)):
                sync.dma_start(dst[0, 0].rearrange("(m p) h d -> p m (h d)", p=P), kv[:, a, :, :]).then_inc(kv_stored, 16)
            sync.wait_ge(kv_stored, 32)
            sync.wait_ge(filled, at[("kvT", (0, 1, MT - 1))] + 1)
            for a, src in enumerate((cache_k, cache_v)):
                sync.dma_start(kv[:, a, :, :], src[0, 0].rearrange("(m p) h d -> p m (h d)", p=P)).then_inc(cache_in, 16)

        @block.gpsimd
        def _(pool):
            count = [0]

            def link(ins):
                count[0] += 1
                ins.then_inc(link_s, 1)
                pool.wait_ge(link_s, count[0])

            link(pool.memset(eps[:, :], NORM_EPS))
            link(pool.memset(ident[:, :], 0.0))
            link(pool.affine_select(out=ident[:, :], in_=ident[:, :], compare_op=ALU.not_equal, fill=1.0,
                                    base=0, pattern=[[-1, P]], channel_multiplier=1))
            pool.sem_inc(const_made, 1)
            for f, n in n_out.items():
                name, (g, k) = f
                pool.wait_ge(emptied, at[f] + 1)
                dst = (qk if name == "qk" else vo)[g]
                pool.dma_start(dst[k, :, :], out[n % 2][:, :]).then_inc(stored[n % 2], 16)
            for j in range(2):
                pool.wait_ge(stored[j], 16 * (len(n_out) // 2))

        @block.scalar
        def _(act):
            act.wait_ge(const_made, 1)
            act.wait_ge(loaded, 48)
            for m in range(MT):
                act.activation(out[m][:, :], mem[:, m, :], ACT.Square, accum_out=rstd[:, m:m + 1]).then_inc(act_link, 1)
            act.wait_ge(act_link, MT)
            act.activation(rstd[:, :], rstd[:, :], ACT.Ln, scale=1.0 / D_MODEL, bias=eps[:, :]).then_inc(act_link, 1)
            act.wait_ge(act_link, MT + 1)
            act.activation(rstd[:, :], rstd[:, :], ACT.Exp, scale=-0.5).then_inc(act_link, 1)

        @block.vector
        def _(vec):
            vec.wait_ge(act_link, MT + 2)
            for m in range(MT):
                vec.tensor_scalar(mem[:, m, :], mem[:, m, :], rstd[:, m:m + 1], None, ALU.mult).then_inc(normed, 1)
            for n, (name, k) in enumerate(fills):
                vec.wait_ge(filled, n + 1)
                b = ps[:, pair(n), :]
                turned = b.rearrange("p b (k t) -> p (b k) t", t=P)
                flat = b.rearrange("p b t -> p (b t)")
                if name == "memT":
                    ins = vec.tensor_tensor(memT[:, :, k * P:(k + 1) * P], turned, bc(gains[:, 0, :], 2, P), ALU.mult)
                elif name == "kv":
                    ins = vec.tensor_copy(kv[:, k[0], k[1], :], flat)
                elif name == "wqT":
                    ins = vec.tensor_copy(wqT[:, :, k * P:(k + 1) * P], turned)
                elif name == "kvT":
                    ins = vec.tensor_copy(kvT[:, k[1], :, k[2] * P:(k[2] + 1) * P], turned)
                else:
                    o = n_out[(name, k)]
                    vec.wait_ge(stored[o % 2], 16 * (o // 2))
                    if name == "qk":
                        ins = vec.tensor_scalar(out[o % 2][:, :], flat, gains[:, 1, k[1]:k[1] + 1],
                                                float(MEM_HEAD_DIM) ** -0.5, ALU.mult, ALU.mult)
                    else:
                        ins = vec.tensor_copy(out[o % 2][:, :], flat)
                ins.then_inc(emptied, 1)

        @block.tensor
        def _(pe):
            pe.wait_ge(const_made, 1)
            for n, (name, k) in enumerate(fills):
                b = ps[:, pair(n), :]
                cols = lambda c: b[:, c // 4, (c % 4) * P:(c % 4 + 1) * P]
                if n >= 4:
                    pe.wait_ge(emptied, n - 3)
                if name == "memT":
                    pe.wait_ge(normed, k + 1)
                    for c in range(KT):
                        last = pe.transpose(cols(c), mem[:, k, c * P:(c + 1) * P], ident[:, :])
                elif name == "kv":
                    a, m = k
                    pe.wait_ge(emptied, at[("memT", MT - 1)] + 1)
                    for half in range(2):
                        pe.wait_ge(half_in[half], 16 * (a + 1))
                        for c in range(KT):
                            last = pe.matmul(b[:, half, :], memT[:, c, m * P:(m + 1) * P], w_half[half][:, c, :],
                                             start=c == 0, stop=c == KT - 1)
                elif name == "wqT":
                    pe.wait_ge(wq_in, 16)
                    for c in range(KT):
                        last = pe.transpose(cols(c), wq[:, k, c * P:(c + 1) * P], ident[:, :])
                elif name == "kvT":
                    g, a, m = k
                    if g:
                        pe.wait_ge(cache_in, 32)
                    else:
                        pe.wait_ge(emptied, at[("kv", (1, MT - 1))] + 1)
                    for c in range(KT):
                        last = pe.transpose(cols(c), kv[:, a, m, c * P:(c + 1) * P], ident[:, :])
                elif name == "qk":
                    g, c = k
                    pe.wait_ge(emptied, at[("kvT", (g, 1, MT - 1))] + 1)
                    for h in range(MEM_HEADS):
                        for d in range(2):
                            last = pe.matmul(b[:, h // 2, (h % 2) * MEM_LEN:(h % 2 + 1) * MEM_LEN],
                                             wqT[:, 2 * h + d, c * P:(c + 1) * P], kvT[:, 0, 2 * h + d, :],
                                             start=d == 0, stop=d == 1)
                else:
                    g, c = k
                    pe.wait_ge(wo_in, 16)
                    for half in range(2):
                        for d in range(2):
                            t = 2 * (c // MT) + d
                            last = pe.matmul(b[:, half, :], kvT[:, 1, t, (c % MT) * P:(c % MT + 1) * P],
                                             wo[:, t, half * BANK:(half + 1) * BANK], start=d == 0, stop=d == 1)
                last.then_inc(filled, 1)


def attend_pass(nc, tag, T, TT, yt, x, y, w_out, g_post, g_post_x, qk, vo):
    TILES = T // TT
    NB = min(2, TILES)
    with ExitStack() as ctx:
        def sb(name, shape):
            return ctx.enter_context(nc.sbuf_tensor(f"{tag}_{name}", shape, F32))

        def sem(name):
            return ctx.enter_context(nc.semaphore(f"{tag}_{name}"))

        w_o = sb("w_o", [P, YT, D_MODEL])
        qk_sb = sb("qk", [P, KT, D_MODEL])
        vo_sb = sb("vo", [P, KT, D_MODEL])
        gains = sb("gains", [P, 2, D_MODEL])
        yt_in = [sb(f"yt_in{j}", [P, YT, TT]) for j in range(NB)]
        x_in = [sb(f"x_in{j}", [TT, D_MODEL]) for j in range(NB)]
        x1 = [sb(f"x1_{j}", [TT, D_MODEL]) for j in range(NB)]
        hx = sb("hx", [TT, D_MODEL])
        turned = sb("turned", [P, KT, TT])
        probs = sb("probs", [TT, D_MODEL])
        o = sb("o", [TT, D_MODEL])
        small = sb("small", [TT, 8])
        mx = sb("mx", [TT, 3, MEM_HEADS])
        eps = sb("eps", [P, 1])
        ident = sb("ident", [P, P])
        ps = ctx.enter_context(nc.psum_tensor(f"{tag}_ps", [P, 8, BANK], F32))

        w_out_in, gains_in, att_weights_in = sem("w_out_in"), sem("gains_in"), sem("att_weights_in")
        yt_loaded = [sem(f"yt_loaded{j}") for j in range(NB)]
        x_loaded = [sem(f"x_loaded{j}") for j in range(NB)]
        waits_met = sem("waits_met")
        link_s, const_made, stored = sem("link"), sem("const_made"), sem("stored")
        STEPS.setdefault(tag, {})
        S = {k: Steps(sem(k), k, STEPS[tag]) for k in ("pe_mix", "pe_att", "vec_mix", "vec_att", "act_mix", "act_att")}
        mix = [S[k] for k in ("pe_mix", "vec_mix", "act_mix")]
        attn = [S[k] for k in ("pe_att", "vec_att", "act_att")]
        pm, vm, am = mix
        pa, va, aa = attn
        block = ctx.enter_context(nc.Block())
        flat2 = lambda b: ps[0:TT, b:b + 2, :].rearrange("p b t -> p (b t)")

        def schedule(eng, mix_tile, att_tile):
            def at_mix(i, j, turns):
                for s in mix:
                    s.iteration(i)
                if mix_tile is not None:
                    mix_tile(i, j, turns)

            def at_att(i, j, turns):
                for s in attn:
                    s.iteration(i)
                for s in mix:
                    s.iteration(i)

                def ahead():
                    if turns is not None:
                        at_mix(i + 1, (j + 1) % NB, turns)
                        for s in mix:
                            s.iteration(i)
                att_tile(i, j, ahead)

            at_mix(0, 0, 0)
            if TILES > 2:
                with eng.Fori(0, TILES // 2 - 1) as n:
                    for j in range(2):
                        at_att(2 * n + j, j, n + j)
            if TILES > 1:
                at_att(TILES - 2, 0, TILES // 2 - 1)
            at_att(TILES - 1, (TILES - 1) % NB, None)

        @block.sync
        def _(sync):
            def load(i, j):
                sync.dma_start(yt_in[j][:, :, :], yt[:, :, bass.ds(i * TT, TT)].rearrange("t p m -> p t m")).then_inc(yt_loaded[j], 16)
                sync.dma_start(x_in[j][:, :], x[0, bass.ds(i * TT, TT), :]).then_inc(x_loaded[j], 16)

            def store(i):
                for s in attn:
                    s.iteration(i)
                sync.wait_ge(*va.at("out"))
                sync.sem_inc(waits_met, 1)
                sync.dma_start(y[0, bass.ds(i * TT, TT), :], o[:, :]).then_inc(stored, 16)

            sync.sem_inc(stored, 16)
            load(0, 0)
            sync.dma_start(w_o[:, :, :], w_out[0, :, :].rearrange("(k p) n -> p k n", p=P)).then_inc(w_out_in, 16)
            sync.dma_start(gains[:, 0, :], g_post.broadcast_to([P, D_MODEL])).then_inc(gains_in, 16)
            sync.dma_start(gains[:, 1, :], g_post_x.broadcast_to([P, D_MODEL])).then_inc(gains_in, 16)
            if NB > 1:
                load(1, 1)
            sync.dma_start(qk_sb[:, :, :], qk.rearrange("t p m -> p t m")).then_inc(att_weights_in, 16)
            sync.dma_start(vo_sb[:, :, :], vo.rearrange("t p m -> p t m")).then_inc(att_weights_in, 16)
            if TILES > NB:
                with sync.Fori(0, TILES // 2 - 1) as n:
                    for j in range(2):
                        i = 2 * n + j
                        for s in mix:
                            s.iteration(i)
                        sync.wait_ge(*pm.at("mix"))
                        sync.wait_ge(*vm.at("x1"))
                        sync.sem_inc(waits_met, 1)
                        load(i + 2, j)
                        store(i)
            for i in range(TILES - NB, TILES):
                store(i)
            sync.wait_ge(stored, 16 * (TILES + 1))

        @block.gpsimd
        def _(pool):
            count = [0]

            def link(ins):
                count[0] += 1
                ins.then_inc(link_s, 1)
                pool.wait_ge(link_s, count[0])

            link(pool.memset(eps[:, :], NORM_EPS))
            link(pool.memset(ident[:, :], 0.0))
            link(pool.affine_select(out=ident[:, :], in_=ident[:, :], compare_op=ALU.not_equal, fill=1.0,
                                    base=0, pattern=[[-1, P]], channel_multiplier=1))
            pool.sem_inc(const_made, 1)


        @block.scalar
        def _(act):
            act.wait_ge(const_made, 1)

            def root(s, src, k, name):
                c = small[:, k:k + 1]
                act.activation(src[1], src[0], ACT.Square, accum_out=c).then_inc(*s.did(f"{name}_squares"))
                act.wait_ge(*s.last())
                act.activation(c, c, ACT.Ln, scale=1.0 / D_MODEL, bias=eps[0:TT, :]).then_inc(*s.did(f"{name}_ln"))
                act.wait_ge(*s.last())
                act.activation(c, c, ACT.Exp, scale=-0.5).then_inc(*s.did(name))

            def mix_tile(i, j, turns):
                act.wait_ge(*pm.at("mix"))
                act.wait_ge(*vm.before())
                root(am, (flat2(0), probs[:, :]), 0, "mix_root")
                act.wait_ge(*vm.at("x1"))
                root(am, (x1[j][:, :], probs[:, :]), 1, "x1_root")

            def att_tile(i, j, ahead):
                act.wait_ge(*pa.at("hx_turned"))
                act.activation(turned[:, :, :], ps[:, 2:4, :].rearrange("p b (k t) -> p (b k) t", t=P)[:, :, 0:TT], ACT.Copy).then_inc(*aa.did("hxT"))
                act.wait_ge(*va.at("neg_max"))
                for h in range(MEM_HEADS):
                    act.activation(hx[:, h * MEM_LEN:(h + 1) * MEM_LEN], ps[0:TT, 4 + h // 2, (h % 2) * MEM_LEN:(h % 2 + 1) * MEM_LEN],
                                   ACT.Exp, bias=mx[:, 0, h:h + 1], accum_out=mx[:, 1, h:h + 1]).then_inc(*aa.did(f"exp{h}"))
                act.wait_ge(*pa.at("p_turned"))
                act.activation(turned[:, :, :], ps[:, 6:8, :].rearrange("p b (k t) -> p (b k) t", t=P)[:, :, 0:TT], ACT.Copy).then_inc(*aa.did("pT"))
                ahead()
                act.wait_ge(*pa.at("att"))
                root(aa, (flat2(2), probs[:, :]), 2, "att_root")

            am.start(act)
            aa.start(act)
            schedule(act, mix_tile, att_tile)

        @block.vector
        def _(vec):
            vec.wait_ge(gains_in, 32)

            def mix_tile(i, j, turns):
                vec.wait_ge(*am.at("mix_root"))
                vec.wait_ge(x_loaded[j], 16 * (turns + 1))
                vec.tensor_tensor(x1[j][:, :], flat2(0), gains[0:TT, 0, :], ALU.mult).then_inc(*vm.did("mix_gain"))
                vec.wait_ge(*vm.last())
                vec.scalar_tensor_tensor(x1[j][:, :], x1[j][:, :], small[:, 0:1], x_in[j][:, :], ALU.mult, ALU.add).then_inc(*vm.did("x1"))
                vec.wait_ge(*am.at("x1_root"))
                vec.tensor_scalar(hx[:, :], x1[j][:, :], small[:, 1:2], None, ALU.mult).then_inc(*vm.did("hx"))

            def att_tile(i, j, ahead):
                vec.wait_ge(*pa.at("scores"))
                s4 = ps[0:TT, 4:6, :].rearrange("p b (h m) -> p (b h) m", h=2)
                vec.tensor_reduce(mx[:, 2, :], s4, AX_X, ALU.max).then_inc(*va.did("max"))
                vec.wait_ge(*va.last())
                vec.tensor_scalar(mx[:, 0, :], mx[:, 2, :], -1.0, None, ALU.mult).then_inc(*va.did("neg_max"))
                vec.wait_ge(*aa.at("exp3"))
                vec.reciprocal(mx[:, 2, :], mx[:, 1, :]).then_inc(*va.did("inverse"))
                vec.wait_ge(*va.last())
                hm = lambda t: t[:, :].rearrange("p (h m) -> p h m", h=MEM_HEADS)
                vec.tensor_tensor(hm(probs), hm(hx), bc(mx[:, 2, :], 2, MEM_LEN), ALU.mult).then_inc(*va.did("probs"))
                ahead()
                vec.wait_ge(*aa.at("att_root"))
                vec.wait_ge(stored, 16 * i + 16)
                vec.tensor_tensor(o[:, :], flat2(2), gains[0:TT, 1, :], ALU.mult).then_inc(*va.did("att_gain"))
                vec.wait_ge(*va.last())
                vec.scalar_tensor_tensor(o[:, :], o[:, :], small[:, 2:3], x1[j][:, :], ALU.mult, ALU.add).then_inc(*va.did("out"))

            vm.start(vec)
            va.start(vec)
            schedule(vec, mix_tile, att_tile)

        @block.tensor
        def _(pe):
            pe.wait_ge(const_made, 1)
            pe.wait_ge(w_out_in, 16)

            def product(b, left, right, n):
                for half in range(2):
                    for k in range(n):
                        last = pe.matmul(ps[0:TT, b + half, :], left[:, k, :], right[:, k, half * BANK:(half + 1) * BANK],
                                         start=k == 0, stop=k == n - 1)
                return last

            def mix_tile(i, j, turns):
                pe.wait_ge(*vm.before())
                pe.wait_ge(yt_loaded[j], 16 * (turns + 1))
                product(0, yt_in[j], w_o, YT).then_inc(*pm.did("mix"))

            def turn(b, src):
                for k in range(KT):
                    last = pe.transpose(ps[:, b + k // 4, (k % 4) * P:(k % 4) * P + TT], src[:, k * P:(k + 1) * P], ident[0:TT, 0:TT])
                return last

            def att_tile(i, j, ahead):
                pe.wait_ge(att_weights_in, 32)
                pe.wait_ge(*vm.at("hx"))
                pe.wait_ge(*va.before())
                turn(2, hx).then_inc(*pa.did("hx_turned"))
                pe.wait_ge(*aa.at("hxT"))
                product(4, turned, qk_sb, KT).then_inc(*pa.did("scores"))
                ahead()
                pe.wait_ge(*va.at("probs"))
                turn(6, probs).then_inc(*pa.did("p_turned"))
                pe.wait_ge(*aa.at("pT"))
                product(2, turned, vo_sb, KT).then_inc(*pa.did("att"))

            pm.start(pe)
            pa.start(pe)
            schedule(pe, mix_tile, att_tile)


def hybrid_stream_encoder_step(nc, a, outs):
    (y_prompt, y_sample, lru_conv_p, lru_conv_s, lru_h_p, lru_h_s, shift_p, shift_s, wkv_p, wkv_s,
     ssd_conv_p, ssd_conv_s, ssd_h_p, ssd_h_s, hgrn_p, hgrn_s, mem_k, mem_v) = outs
    TP, TS = a["x_prompt"].shape[1], a["x_sample"].shape[1]

    def scratch(name, shape):
        return nc.dram_tensor(name, shape, F32, kind="Internal").ap()

    tokens = (TP, TS)
    pc = [scratch(f"pc{g}", [N_CH_TILES, P, HALO + t]) for g, t in enumerate(tokens)]
    dtr = [scratch(f"dtr{g}", [t, HEADS]) for g, t in enumerate(tokens)]
    yt = [scratch(f"yt{g}", [YT, P, t]) for g, t in enumerate(tokens)]
    qk = [scratch(f"qk{g}", [KT, P, D_MODEL]) for g in range(2)]
    vo = [scratch(f"vo{g}", [KT, P, D_MODEL]) for g in range(2)]
    names = ("lru_conv", "lru_h", "shift", "wkv", "ssd_conv", "ssd_h", "hgrn_s")
    sample_in = dict(zip(names, (a["state_lru_conv"], a["state_lru_h"], a["state_rwkv_shift"], a["state_rwkv_wkv"],
                                 a["state_ssd_conv"], a["state_ssd_h"], a["state_hgrn_s"])))
    prompt_out = dict(zip(names, (lru_conv_p, lru_h_p, shift_p, wkv_p, ssd_conv_p, ssd_h_p, hgrn_p)))
    sample_out = dict(zip(names, (lru_conv_s, lru_h_s, shift_s, wkv_s, ssd_conv_s, ssd_h_s, hgrn_s)))

    project_pass(nc, a["x_prompt"], a["x_sample"], a["g_pre"], a["w_in"], pc, dtr, sample_in, TP, TS)
    memory_pass(nc, a["mem_prompt"], a["mem_g"], a["mem_w_k"], a["mem_w_v"], a["mem_w_q"], a["mem_w_o"],
                a["g_pre_x"], a["cache_mem_k"], a["cache_mem_v"], mem_k, mem_v, qk, vo)
    mixer_pass(nc, "mixp", TP, P, 64, pc[0], dtr[0], yt[0], a, None, prompt_out)
    mixer_pass(nc, "mixs", TS, TS, TS, pc[1], dtr[1], yt[1], a, sample_in, sample_out)
    attend_pass(nc, "attp", TP, P, yt[0], a["x_prompt"], y_prompt, a["w_out"], a["g_post"], a["g_post_x"], qk[0], vo[0])
    attend_pass(nc, "atts", TS, TS, yt[1], a["x_sample"], y_sample, a["w_out"], a["g_post"], a["g_post_x"], qk[1], vo[1])


_INS = ['x_prompt', 'x_sample', 'state_lru_conv', 'state_lru_h', 'state_rwkv_shift', 'state_rwkv_wkv',
        'state_ssd_conv', 'state_ssd_h', 'state_hgrn_s', 'cache_mem_k', 'cache_mem_v', 'mem_prompt',
        'g_pre', 'g_post', 'g_pre_x', 'g_post_x', 'w_in', 'w_out',
        'lru_conv_w', 'lru_conv_b', 'lru_w_r', 'lru_b_r', 'lru_w_i', 'lru_b_i', 'lru_lambda',
        'rwkv_mu', 'rwkv_w0', 'rwkv_w_up', 'rwkv_a0', 'rwkv_a_up', 'rwkv_k_k', 'rwkv_k_a', 'rwkv_r_k',
        'rwkv_ln_g', 'rwkv_ln_b', 'ssd_conv_w', 'ssd_conv_b', 'ssd_dt_bias', 'ssd_a_log', 'ssd_d', 'ssd_norm_g',
        'hgrn_lb_logits', 'hgrn_norm_g', 'mem_g', 'mem_w_q', 'mem_w_k', 'mem_w_v', 'mem_w_o']
_OUTS = ['x_prompt', 'x_sample', 'state_lru_conv', 'state_lru_conv', 'state_lru_h', 'state_lru_h',
         'state_rwkv_shift', 'state_rwkv_shift', 'state_rwkv_wkv', 'state_rwkv_wkv', 'state_ssd_conv', 'state_ssd_conv',
         'state_ssd_h', 'state_ssd_h', 'state_hgrn_s', 'state_hgrn_s', 'cache_mem_k', 'cache_mem_k']


def kernel(**inputs):
    import numpy as _np
    import concourse.bacc as _bacc
    from concourse import mybir as _mybir
    from concourse.bass_utils import run_bass_kernel_spmd as _run

    nc = _bacc.Bacc("TRN2", target_bir_lowering=False, num_devices=1)
    arrays, args = {}, {}
    for name in _INS:
        a = _np.ascontiguousarray(inputs[name])
        arrays[f"in_{name}_dram"] = a
        args[name] = nc.dram_tensor(f"in_{name}_dram", a.shape, _mybir.dt.from_np(a.dtype), kind="ExternalInput").ap()
    outs = [nc.dram_tensor(f"out_{i}_dram", arrays[f"in_{like}_dram"].shape, _mybir.dt.float32, kind="ExternalOutput").ap()
            for i, like in enumerate(_OUTS)]
    hybrid_stream_encoder_step(nc, args, outs)
    r = _run(nc, [arrays], core_ids=[0])
    return tuple(r.results[0][f"out_{i}_dram"] for i in range(len(_OUTS)))
```

```python
from contextlib import ExitStack

import concourse.bass as bass
from concourse import mybir

F32 = mybir.dt.float32
F32R = mybir.dt.float32r
ALU = mybir.AluOpType
ACT = mybir.ActivationFunctionType
AX_X = mybir.AxisListType.X

P = 128
BANK = 512
D_MODEL = 1024
D_GROUP = 512
CONV_W = 4
HALO = CONV_W - 1
HEADS = 8
HEAD = 64
PAIRS = HEADS // 2
SUB = 32
MEM_LEN = 256
MEM_HEADS = 4
MEM_HEAD_DIM = D_MODEL // MEM_HEADS
D_MIX = 4 * D_GROUP
SSD_CONV_CH = 768
SHIFT_W = 3 * D_GROUP + 2 * HEAD
LRU_C = 8.0
DECAY_SCALE = 0.6065306597126334
NORM_EPS = 1e-6
RWKV_LN_EPS = 64e-5
KT = D_MODEL // P
YT = D_MIX // P

XA, GA, PB, GB, XBC, Z, QD, FD, ID, GD, N_CH_TILES = 0, 4, 8, 21, 25, 31, 35, 39, 43, 47, 51
DT_COL = P * Z
D_IN_PROJ = P * N_CH_TILES + HEADS


class Steps:

    def __init__(self, sem, key, table):
        self.sem, self.names, self.base, self.seen = sem, table.setdefault(key, []), 1, []
        self.index = {n: k + 1 for k, n in enumerate(self.names)}

    def start(self, eng):
        eng.sem_inc(self.sem, 1)

    def iteration(self, i):
        self.base, self.seen = i * len(self.names) + 1, []

    def did(self, name):
        self.seen.append(name)
        assert self.names[len(self.seen) - 1] == name, (name, self.names[len(self.seen) - 1])
        return self.sem, 1

    def at(self, name, ago=0):
        return self.sem, self.base + (self.index[name] - ago * len(self.names))

    def before(self):
        return self.sem, self.base

    def last(self):
        return self.sem, self.base + len(self.seen)


def load_ln_and_exp(nc, act):
    act.add_instruction(mybir.InstLoadActFuncSet(name=nc.get_next_instruction_name(), act_func_set_id=6,
                                                 engine=mybir.EngineType.Activation, ins=[], outs=[]))


def bc(ap, dim, n):
    v = ap.unsqueeze(dim)
    shape = list(v.shape)
    shape[dim] = n
    return v.broadcast_to(shape)


def project_pass(nc, x_prompt, x_sample, g_pre, w_in, pc, dtr, conv_states, TP, TS):
    TALL = TP + TS
    GROUPS = 5
    N = TALL // GROUPS
    NT = TP // P
    assert GROUPS * N == TALL and N <= BANK and TS <= P

    with ExitStack() as ctx:
        def sb(name, shape, dtype=F32):
            return ctx.enter_context(nc.sbuf_tensor(f"in_{name}", shape, dtype))

        def sem(name):
            return ctx.enter_context(nc.semaphore(f"in_{name}"))

        def parts(name, shape):
            return [sb(f"{name}_{part}", shape, F32R) for part in ("high", "low")]

        ctx.enter_context(nc.allow_non_contiguous_dma(reason="states and vectors over channels, once"))
        hT = parts("hT", [P, KT, TALL])
        h_cols = [sb(f"h_cols{j}", [P, KT, P]) for j in range(2)]
        x_in = [sb(f"x_in{j}", [P, D_MODEL]) for j in range(2)]
        junk = sb("junk", [P, D_MODEL])
        rstd = sb("rstd", [P, 2])
        eps = sb("eps", [P, 1])
        ident = sb("ident", [P, P])
        g_col = sb("g_col", [P, KT])
        w_tile = [sb(f"w_tile{j}", [P, KT, P]) for j in range(2)]
        w_split = [parts(f"w_split{j}", [P, KT, P]) for j in range(2)]
        w_dt = sb("w_dt", [P, KT, P])
        w_dt_split = parts("w_dt_split", [P, KT, P])
        out = [sb(f"out{j}", [P, TALL]) for j in range(2)]
        dt_out = sb("dt_out", [P, NT + 1, HEADS])
        zeros = sb("zeros", [P, 13, HALO])
        ps = ctx.enter_context(nc.psum_tensor("in_ps", [P, 8, BANK], F32))

        const_in, link_s, const_made = sem("const_in"), sem("link"), sem("const_made")
        x_loaded = [sem(f"x_loaded{j}") for j in range(2)]
        squared, rooted = sem("squared"), sem("rooted")
        normed_at, turned, normed = sem("normed_at"), sem("turned"), sem("normed")
        w_loaded = [sem(f"w_loaded{j}") for j in range(2)]
        high_made, h_split, dt_split = sem("high_made"), sem("h_split"), sem("dt_split")
        w_high_made, w_split_made = sem("w_high_made"), sem("w_split_made")
        group_done, group_out = sem("group_done"), sem("group_out")
        stored = [sem(f"stored{j}") for j in range(2)]
        dt_done, dt_copied, dt_stored = sem("dt_done"), sem("dt_copied"), sem("dt_stored")
        halo_stored, waits_met = sem("halo_stored"), sem("waits_met")
        block = ctx.enter_context(nc.Block())

        w_view = w_in[0, :, :].rearrange("(k p) n -> p k n", p=P)

        @block.sync
        def _(sync):
            sync.dma_start(g_col[:, :], g_pre.rearrange("a (k p) -> p (a k)", p=P)).then_inc(const_in, 16)
            sync.dma_start(w_dt[:, :, :], w_view[:, :, DT_COL:DT_COL + P]).then_inc(const_in, 16)

            def load_x(i, j):
                sync.dma_start(x_in[j][:, :], x_prompt[0, bass.ds(i * P, P), :]).then_inc(x_loaded[j], 16)

            def load_w(n, j, skip=0):
                sync.dma_start(w_tile[j][:, :, :], w_view[:, :, bass.ds(n * P + skip, P)]).then_inc(w_loaded[j], 16)

            def store(n, j):
                sync.wait_ge(group_out, (n + 1) * GROUPS + GROUPS)
                sync.sem_inc(waits_met, 1)
                for g, (t0, t1) in enumerate(((0, TP), (TP, TALL))):
                    dst = pc[g][bass.ds(n, 1), :, HALO:HALO + t1 - t0].rearrange("t p m -> (t p) m")
                    sync.dma_start(dst, out[j][:, t0:t1]).then_inc(stored[j], 16)

            for j in range(2):
                sync.sem_inc(stored[j], 16)
                load_x(j, j)
            load_w(0, 0)
            load_w(1, 1)
            with sync.Fori(0, NT // 2 - 1) as i:
                for j in range(2):
                    sync.wait_ge(normed, 2 * i + j + 2)
                    load_x(2 * i + j + 2, j)
            sync.wait_ge(normed, NT)
            sync.dma_start(x_in[0][0:TS, :], x_sample[0, :, :]).then_inc(x_loaded[0], 16)

            def turn_over(n0, n1, skip):
                with sync.Fori(n0 // 2, n1 // 2) as i:
                    for j in range(2):
                        store(2 * i + j, j)
                        load_w(2 * i + j + 2, j, skip)

            turn_over(0, Z - 3, 0)
            for n, skip in ((Z - 3, 0), (Z - 2, HEADS)):
                store(n, n % 2)
                load_w(n + 2, n % 2, skip)
            turn_over(Z - 1, N_CH_TILES - 3, HEADS)
            store(N_CH_TILES - 3, 0)
            load_w(N_CH_TILES - 1, 0, HEADS)
            store(N_CH_TILES - 2, 1)
            store(N_CH_TILES - 1, 0)
            sync.wait_ge(stored[0], 32 * (N_CH_TILES // 2 + 1) + 16)
            sync.wait_ge(stored[1], 32 * (N_CH_TILES // 2) + 16)

        @block.gpsimd
        def _(pool):
            count = [0]

            def link(ins):
                count[0] += 1
                ins.then_inc(link_s, 1)
                pool.wait_ge(link_s, count[0])

            link(pool.memset(eps[:, :], NORM_EPS))
            link(pool.memset(zeros[:, :, :], 0.0))
            link(pool.memset(ident[:, :], 0.0))
            link(pool.affine_select(out=ident[:, :], in_=ident[:, :], compare_op=ALU.not_equal, fill=1.0,
                                    base=0, pattern=[[-1, P]], channel_multiplier=1))
            pool.sem_inc(const_made, 1)
            halo = [(pc[0][XA:XA + 4, :, 0:HALO].rearrange("t p m -> p t m"), zeros[:, 0:4, :]),
                    (pc[0][XBC:XBC + 6, :, 0:HALO].rearrange("t p m -> p t m"), zeros[:, 0:6, :]),
                    (pc[0][PB:PB + 13, :, HALO - 1:HALO].rearrange("t p m -> p t m"), zeros[:, :, 0:1]),
                    (pc[1][PB:PB + 13, :, HALO - 1], conv_states["shift"].rearrange("a b (t p) -> (a b t) p", p=P))]
            for m in range(HALO):
                for t, n, name in ((XA, 4, "lru_conv"), (XBC, 6, "ssd_conv")):
                    halo.append((pc[1][t:t + n, :, m], conv_states[name][0, 0, m, :].rearrange("(t p) -> t p", p=P)))
            for dst, src in halo:
                pool.dma_start(dst, src).then_inc(halo_stored, 16)
            pool.sem_inc(h_split, 1)

            def low(t, j, r, t0):
                pool.wait_ge(high_made, t + 1)
                cols = bass.ds(t0, r)
                pool.tensor_tensor(hT[1][:, :, cols], h_cols[j][:, :, 0:r], hT[0][:, :, cols].bitcast(F32),
                                   ALU.subtract).then_inc(h_split, 1)

            with pool.Fori(0, NT // 2) as i:
                for j in range(2):
                    low(2 * i + j, j, P, (2 * i + j) * P)
            low(NT, 0, TS, TP)
            pool.wait_ge(dt_copied, 2)
            pool.dma_start(dtr[0].rearrange("(t p) h -> p t h", p=P), dt_out[:, 0:NT, :]).then_inc(dt_stored, 16)
            pool.dma_start(dtr[1][:, :], dt_out[P - TS:P, NT, :]).then_inc(dt_stored, 16)
            pool.wait_ge(halo_stored, 16 * len(halo))
            pool.wait_ge(dt_stored, 32)

        @block.scalar
        def _(act):
            load_ln_and_exp(nc, act)
            act.wait_ge(const_made, 1)

            def root(t, j, load, r):
                act.wait_ge(x_loaded[j], load)
                act.activation(junk[0:r, :], x_in[j][0:r, :], ACT.Square, accum_out=rstd[0:r, j:j + 1]).then_inc(squared, 1)
                act.wait_ge(squared, 2 * t + 1)
                act.activation(rstd[0:r, j:j + 1], rstd[0:r, j:j + 1], ACT.Ln, scale=1.0 / D_MODEL, bias=eps[0:r, :]).then_inc(squared, 1)
                act.wait_ge(squared, 2 * t + 2)
                act.activation(rstd[0:r, j:j + 1], rstd[0:r, j:j + 1], ACT.Exp, scale=-0.5).then_inc(rooted, 1)

            with act.Fori(0, NT // 2) as i:
                for j in range(2):
                    act.wait_ge(normed, 2 * i + 1)
                    root(2 * i + j, j, 16 * (i + 1), P)
            root(NT, 0, 16 * (NT // 2 + 1), TS)

            act.sem_inc(group_out, GROUPS)

            def copy_out(n, j, i):
                act.wait_ge(stored[j], 32 * i + 16)
                for g in range(GROUPS):
                    act.wait_ge(group_done, GROUPS * n + g + 1)
                    act.activation(out[j][:, g * N:(g + 1) * N], ps[:, g, 0:N], ACT.Copy).then_inc(group_out, 1)

            with act.Fori(0, N_CH_TILES // 2) as i:
                for j in range(2):
                    copy_out(2 * i + j, j, i)
            copy_out(N_CH_TILES - 1, 0, N_CH_TILES // 2)

        @block.vector
        def _(vec):
            vec.sem_inc(normed, 1)
            vec.wait_ge(const_in, 32)

            def split(x, high, low, made, count, done):
                vec.tensor_copy(high, x).then_inc(made, 1)
                vec.wait_ge(made, count)
                vec.tensor_tensor(low, x, high.bitcast(F32), ALU.subtract).then_inc(done, 1)

            split(w_dt[:, :, :], w_dt_split[0][:, :, :], w_dt_split[1][:, :, :], w_high_made, 1, dt_split)

            def split_w(n, j, i):
                vec.wait_ge(w_loaded[j], 16 * (i + 1))
                split(w_tile[j][:, :, :], w_split[j][0][:, :, :], w_split[j][1][:, :, :], w_high_made, n + 2, w_split_made)

            def norm(t, j, r, t0, back):
                vec.wait_ge(rooted, t + 1)
                vec.tensor_scalar(x_in[j][0:r, :], x_in[j][0:r, :], rstd[0:r, j:j + 1], None, ALU.mult).then_inc(normed_at, 1)
                vec.wait_ge(turned, t + 1)
                src = ps[:, 4 * j:4 * j + 2, :].rearrange("p b (k t) -> p (b k) t", t=P)[:, :, 0:r]
                vec.wait_ge(h_split, back)
                vec.tensor_tensor(h_cols[j][:, :, 0:r], src, bc(g_col[:, :], 2, r), ALU.mult).then_inc(normed, 1)
                vec.wait_ge(normed, t + 2)
                vec.tensor_copy(hT[0][:, :, bass.ds(t0, r)], h_cols[j][:, :, 0:r]).then_inc(high_made, 1)

            with vec.Fori(0, NT // 2) as i:
                for j in range(2):
                    norm(2 * i + j, j, P, (2 * i + j) * P, 2 * i + 1)
            norm(NT, 0, TS, TP, NT + 1)
            for n in range(2):
                split_w(n, n, 0)
            vec.wait_ge(dt_done, 1)
            vec.tensor_copy(out[1][0:HEADS, :].rearrange("p (g n) -> p g n", g=GROUPS), ps[0:HEADS, 0:GROUPS, 0:N]).then_inc(dt_copied, 1)
            vec.wait_ge(dt_done, 2)
            vec.tensor_copy(dt_out[:, :, :].rearrange("p t h -> p (t h)"), ps[:, 5, 0:(NT + 1) * HEADS]).then_inc(dt_copied, 1)

            def split_next(n, j, i):
                vec.wait_ge(group_done, (n - 1) * GROUPS)
                split_w(n, j, i)

            with vec.Fori(0, N_CH_TILES // 2 - 1) as i:
                for j in range(2):
                    split_next(2 * i + j + 2, j, i + 1)
            split_next(N_CH_TILES - 1, 0, N_CH_TILES // 2)

        @block.tensor
        def _(pe):
            pe.wait_ge(const_made, 1)
            pe.wait_ge(const_in, 32)

            def turn(t, j, r, back):
                pe.wait_ge(normed_at, t + 1)
                pe.wait_ge(normed, back)
                for k in range(KT):
                    o = ps[:, 4 * j + k // 4, (k % 4) * P:(k % 4) * P + r]
                    last = pe.transpose(o, x_in[j][0:r, k * P:(k + 1) * P], ident[0:r, 0:r])
                last.then_inc(turned, 1)

            with pe.Fori(0, NT // 2) as i:
                for j in range(2):
                    turn(2 * i + j, j, P, 2 * i + 1)
            turn(NT, 0, TS, NT + 1)
            pe.wait_ge(h_split, NT + 2)
            pe.wait_ge(high_made, NT + 1)
            pe.wait_ge(dt_split, 1)

            def product(o, left, right):
                passes = [(k, a, b) for k in range(KT) for a, b in ((0, 0), (0, 1), (1, 0))]
                for p in passes:
                    k, a, b = p
                    last = pe.matmul(o, left(a, k), right(b, k), start=p is passes[0], stop=p is passes[-1])
                return last

            for g in range(GROUPS):
                last = product(ps[:, g, 0:N], lambda part, k: w_dt_split[part][:, k, :],
                               lambda part, k: hT[part][:, k, g * N:(g + 1) * N])
            last.then_inc(dt_done, 1)
            pe.wait_ge(dt_copied, 1)
            for t in range(NT + 1):
                t0 = t * P if t < NT else TALL - P
                last = pe.transpose(ps[:, 5, t * HEADS:(t + 1) * HEADS], out[1][0:HEADS, t0:t0 + P], ident[0:HEADS, 0:HEADS])
            last.then_inc(dt_done, 1)

            def products(n, j, i):
                pe.wait_ge(w_split_made, n + 1)
                for g in range(GROUPS):
                    pe.wait_ge(group_out, GROUPS * n + g + 1)
                    product(ps[:, g, 0:N], lambda part, k: w_split[j][part][:, k, :],
                            lambda part, k: hT[part][:, k, g * N:(g + 1) * N]).then_inc(group_done, 1)

            with pe.Fori(0, N_CH_TILES // 2) as i:
                for j in range(2):
                    products(2 * i + j, j, i)
            products(N_CH_TILES - 1, 0, N_CH_TILES // 2)
STEPS = {
    'mixp': {
        'pe': [
            'mt', 'n_off', 'nt', 'keys', 'bonus', 'q2_0', 'q2_1', 'h_att', 'tu2_0', 'tu2_1', 'h_keys', 'q4_0',
            'q4_1', 'tu4_0', 'tu4_1', 'q8_0', 'q8_1', 'tu8_0', 'tu8_1', 'q16_0', 'q16_1', 'tu16_0', 'tu16_1',
            'q32_0', 'q32_1', 'tu32_0', 'tu32_1', 'h_kv', 'rhs0', 'sa0', 'kv0', 'y_rwkv0', 'rhs1', 'sa1',
            'kv1', 'h_out', 'y_rwkv', 'yb_mean', 'yb_var',
        ],
        'vector': [
            'mt_pt', 't_off0', 't0', 'nt_qt', 'b_key0', 'bonus_v', 'qi2_0_0', 'qi2_1_0', 'att_own0', 'att_0',
            'att', 'qi4_0_0', 'qi4_1_0', 'qi8_0_0', 'qi8_1_0', 'qi16_0_0', 'qi16_1_0', 'qi32_0_0', 'qi32_1_0',
            'h_smid0', 'h_decay0', 'h_state0', 'h_smid1', 'h_decay1', 'h_states', 'rhs0_0', 'sa0_0',
            'wkv_sum0', 'wkv0', 'rhs1_0', 'sa1_0', 'wkv_sum1', 'wkv1', 'yb_centred', 'yb_normed', 'yd_normed',
            'yb_bonus', 'y_hgrn', 'y_rwkv',
        ],
        'scalar': [
            'v_tok0', 'k_key0', 'tu2_0_0', 'tu2_1_0', 'hk_key0', 'hv_tok0', 'tu4_0_0', 'tu4_1_0', 'tu8_0_0',
            'tu8_1_0', 'tu16_0_0', 'tu16_1_0', 'tu32_0_0', 'tu32_1_0', 'yd_square', 'yd_copy', 'yb_copy',
            'yb_ln', 'yd_ln', 'yb_rstd', 'yd_rms',
        ],
        'pool': [
            'u_off0', 'u00', 'lev2_0', 'lev4_0', 'lev8_0', 'lev16_0', 'lev32_0', 'bonus_bias', 'yd_gain',
            'yb_square', 'yb_gain',
        ],
        'pe_front': [
            'lru_gates', 'kk_norm', 'up', 'acs', 'cb0', 'cb', 'x_tok', 'ssd_inter0', 'ssd', 'yc_ms',
        ],
        'vector_front': [
            'tap0_0', 'tap0_1', 'tap0_2', 'tap0_3', 'tap0_4', 'tap0_5', 'tap0_6', 'tap0_7', 'tap0_8',
            'tap0_9', 'tap1_0', 'tap1_1', 'tap1_2', 'tap1_3', 'tap1_4', 'tap1_5', 'tap1_6', 'tap1_7',
            'tap1_8', 'tap1_9', 'tap2_0', 'tap2_1', 'tap2_2', 'tap2_3', 'tap2_4', 'tap2_5', 'tap2_6',
            'tap2_7', 'tap2_8', 'tap2_9', 'tap3_0', 'tap3_1', 'tap3_2', 'tap3_3', 'tap3_4', 'tap3_5',
            'tap3_6', 'tap3_7', 'tap3_8', 'conv', 'shift_0', 'shift_1', 'shift_2', 'shift_3', 'shift_4',
            'shift_5', 'shift_6', 'shift_7', 'shift_8', 'shift_9', 'shift_10', 'shift_11', 'shift', 'dt_x',
            'lru_biased', 'gates', 'q_twice', 'f_one_plus', 'dt_one_plus', 'xbc_twice', 'lru_s', 'lru_ix',
            'up_biased', 'a_square', 'one_less', 'one_less_floor', 'log_w', 'cum', 'cum_before', 'kp_factor',
            'kp', 'dt_log1p1', 'dt_log1p2', 'dt_log1p3', 'dt_log1p4', 'dt_log1p5', 'dt_log1p6', 'dt_log1p7',
            'dt', 'd_a', 'kk_unit', 'r_hat', 'kappa', 'b_twice', 'khat', 'bneg', 'e_end', 'acs', 'seg',
            'seg_clamped', 'd_last', 'lru_u', 'lru_carry', 'lru_u0', 'lru_cut', 'lru_h', 'lru_state', 'y_lru',
            'cb', 'd_last_dt', 'ssd_scores0', 'ssd_scores1', 'x_dt', 'x_dd', 'd_x', 'logf', 'log_k', 'h_cum',
            'h_m0', 'h_end', 'h_mid', 'h_mid_span', 'h_spans', 'h_rel', 'h_kx', 'yc_inter', 'yc_intra',
            'yc_sum', 'yc', 'ssd_decay0', 'ssd_decay1', 'ssd_state', 'h_q', 'h_k2', 'h_q2', 'y_ssd',
        ],
        'scalar_front': [
            'gate_tanh', 'q_tanh', 'f_abs', 'f_exp', 'dt_abs', 'dt_exp', 'wl_tanh', 'ri_tanh', 'xbc_tanh',
            'xbc', 'lru_a', 'lru_th', 'wa_tanh', 'dt_ln', 'f_ln', 'kk_ln', 'one_less_ln', 'kk_exp',
            'one_less_root', 'e_cum', 'e_neg', 'e_before', 'e_acs', 'seg_exp', 'tot0', 'tot1', 'd_last_exp',
            'b_tok', 'h_k', 'h_eq', 'h_mids', 'h_ends', 'yc_ln', 'yc_rms',
        ],
        'pool_front': [
            'shift_diff', 'kk_raw', 'kk_square', 'rk', 'rk_weighed', 'yc_square', 'yc_gain',
        ],
    },
    'mixs': {
        'pe': [
            'mt', 'n_off', 'nt', 'keys', 'bonus', 'q2_0', 'h_att', 'tu2_0', 'h_keys', 'q4_0', 'tu4_0', 'q8_0',
            'tu8_0', 'q16_0', 'tu16_0', 'h_kv', 'rhs0', 'sa0', 'kv0', 'h_out', 'y_rwkv', 'yb_mean', 'yb_var',
        ],
        'vector': [
            'mt_pt_0', 'mt_pt', 't_off0', 't_off64', 't0_0', 't0', 'nt_qt_0', 'nt_qt', 'b_key0', 'b_key64',
            'bonus_v', 'qi2_0_0', 'qi2_0_64', 'att_own0', 'att', 'qi4_0_0', 'qi4_0_64', 'qi8_0_0', 'qi8_0_64',
            'qi16_0_0', 'qi16_0_64', 'h_smid0', 'h_decay0', 'h_states', 'rhs0_0', 'rhs0_64', 'sa0_0',
            'sa0_64', 'wkv_sum0', 'wkv0', 'yb_centred', 'yb_normed', 'yd_normed', 'yb_bonus', 'y_hgrn',
            'y_rwkv',
        ],
        'scalar': [
            'v_tok0', 'k_key0', 'v_tok64', 'k_key64', 'tu2_0_0', 'tu2_0_64', 'hk_key0', 'hv_tok0', 'hk_key64',
            'hv_tok64', 'tu4_0_0', 'tu4_0_64', 'tu8_0_0', 'tu8_0_64', 'tu16_0_0', 'tu16_0_64', 'yd_square',
            'yd_copy', 'yb_copy', 'yb_ln', 'yd_ln', 'yb_rstd', 'yd_rms',
        ],
        'pool': [
            'u_off0', 'u_off64', 'u00', 'u064', 'lev2_0', 'lev2_64', 'lev4_0', 'lev4_64', 'lev8_0', 'lev8_64',
            'lev16_0', 'lev16_64', 'bonus_bias', 'yd_gain', 'yb_square', 'yb_gain',
        ],
        'pe_front': [
            'lru_gates', 'kk_norm', 'up', 'acs', 'cb0', 'cb', 'x_tok', 'ssd_inter0', 'ssd', 'yc_ms',
        ],
        'vector_front': [
            'tap0_0', 'tap0_1', 'tap0_2', 'tap0_3', 'tap0_4', 'tap0_5', 'tap0_6', 'tap0_7', 'tap0_8',
            'tap0_9', 'tap1_0', 'tap1_1', 'tap1_2', 'tap1_3', 'tap1_4', 'tap1_5', 'tap1_6', 'tap1_7',
            'tap1_8', 'tap1_9', 'tap2_0', 'tap2_1', 'tap2_2', 'tap2_3', 'tap2_4', 'tap2_5', 'tap2_6',
            'tap2_7', 'tap2_8', 'tap2_9', 'tap3_0', 'tap3_1', 'tap3_2', 'tap3_3', 'tap3_4', 'tap3_5',
            'tap3_6', 'tap3_7', 'tap3_8', 'conv', 'shift_0', 'shift_1', 'shift_2', 'shift_3', 'shift_4',
            'shift_5', 'shift_6', 'shift_7', 'shift_8', 'shift_9', 'shift_10', 'shift_11', 'shift', 'dt_x',
            'lru_biased', 'gates', 'q_twice', 'f_one_plus', 'dt_one_plus', 'xbc_twice', 'lru_s', 'lru_ix',
            'up_biased', 'a_square', 'one_less', 'one_less_floor', 'log_w', 'cum', 'cum_before', 'kp_factor',
            'kp', 'dt_log1p1', 'dt_log1p2', 'dt_log1p3', 'dt_log1p4', 'dt_log1p5', 'dt_log1p6', 'dt_log1p7',
            'dt', 'd_a', 'kk_unit', 'r_hat', 'kappa', 'b_twice', 'khat', 'bneg', 'e_end', 'acs', 'seg',
            'seg_clamped', 'd_last', 'lru_u', 'lru_carry', 'lru_u0', 'lru_cut', 'lru_h', 'lru_state', 'y_lru',
            'cb', 'd_last_dt', 'ssd_scores0', 'ssd_scores1', 'x_dt', 'x_dd', 'd_x', 'logf', 'log_k', 'h_cum',
            'h_m0', 'h_end', 'h_mid', 'h_mid_span', 'h_spans', 'h_rel', 'h_kx', 'yc_inter', 'yc_intra',
            'yc_sum', 'yc', 'ssd_decay0', 'ssd_decay1', 'ssd_state', 'h_q', 'h_k2', 'h_q2', 'y_ssd',
        ],
        'scalar_front': [
            'gate_tanh', 'q_tanh', 'f_abs', 'f_exp', 'dt_abs', 'dt_exp', 'wl_tanh', 'ri_tanh', 'xbc_tanh',
            'xbc', 'lru_a', 'lru_th', 'wa_tanh', 'dt_ln', 'f_ln', 'kk_ln', 'one_less_ln', 'kk_exp',
            'one_less_root', 'e_cum', 'e_neg', 'e_before', 'e_acs', 'seg_exp', 'tot0', 'tot1', 'd_last_exp',
            'b_tok', 'h_k', 'h_eq', 'h_mids', 'h_ends', 'yc_ln', 'yc_rms',
        ],
        'pool_front': [
            'shift_diff', 'kk_raw', 'kk_square', 'rk', 'rk_weighed', 'yc_square', 'yc_gain',
        ],
    },
    'attp': {
        'pe_mix': [
            'mix',
        ],
        'pe_att': [
            'hx_turned', 'scores', 'p_turned', 'att',
        ],
        'vec_mix': [
            'mix_gain', 'x1', 'hx',
        ],
        'vec_att': [
            'max', 'neg_max', 'inverse', 'probs', 'att_gain', 'out',
        ],
        'act_mix': [
            'mix_root_squares', 'mix_root_ln', 'mix_root', 'x1_root_squares', 'x1_root_ln', 'x1_root',
        ],
        'act_att': [
            'hxT', 'exp0', 'exp1', 'exp2', 'exp3', 'pT', 'att_root_squares', 'att_root_ln', 'att_root',
        ],
    },
    'atts': {
        'pe_mix': [
            'mix',
        ],
        'pe_att': [
            'hx_turned', 'scores', 'p_turned', 'att',
        ],
        'vec_mix': [
            'mix_gain', 'x1', 'hx',
        ],
        'vec_att': [
            'max', 'neg_max', 'inverse', 'probs', 'att_gain', 'out',
        ],
        'act_mix': [
            'mix_root_squares', 'mix_root_ln', 'mix_root', 'x1_root_squares', 'x1_root_ln', 'x1_root',
        ],
        'act_att': [
            'hxT', 'exp0', 'exp1', 'exp2', 'exp3', 'pT', 'att_root_squares', 'att_root_ln', 'att_root',
        ],
    },
}

def make_masks(nc, ctx, L, tag):
    def sb(name, shape):
        return ctx.enter_context(nc.sbuf_tensor(f"{tag}_{name}", shape, F32))

    c = {
        "ident": sb("ident", [P, P]),
        "ones": sb("ones", [P, P]),
        "headones": sb("headones", [P, P]),
        "headmean": sb("headmean", [P, P]),
        "triu": sb("triu", [P, P]),
        "causal": sb("causal", [P, 2, L]),
        "subcausal": sb("subcausal", [P, L]),
        "eye": sb("eye", [P, L]),
        "first": sb("first", [P, 4 * P]),
    }
    levels = []
    n = 1
    while n < L:
        levels.append(n)
        n *= 2
    for n in levels:
        c[f"up{n}"] = sb(f"up{n}", [P, L])
    c["low1"] = sb("low1", [P, L])
    c["levels"] = levels
    return c


def fill_masks(pool, link, c, L):
    half = [slice(0, 64), slice(64, 128)]
    link(pool.memset(c["ones"][:, :], 1.0 / 512))
    link(pool.memset(c["headones"][:, :], 0.0))
    link(pool.memset(c["headmean"][:, :], 0.0))
    for a in half:
        link(pool.memset(c["headones"][a, a], 1.0))
        link(pool.memset(c["headmean"][a, a], 1.0 / 64))
    link(pool.memset(c["ident"][:, :], 0.0))
    link(pool.affine_select(out=c["ident"][:, :], in_=c["ident"][:, :], compare_op=ALU.not_equal,
                            fill=1.0, base=0, pattern=[[-1, P]], channel_multiplier=1))
    link(pool.memset(c["triu"][:, :], 1.0))
    link(pool.affine_select(out=c["triu"][:, :], in_=c["triu"][:, :], compare_op=ALU.is_ge,
                            fill=0.0, base=0, pattern=[[1, P]], channel_multiplier=-1))
    link(pool.memset(c["causal"][:, :, :], 1.0))
    link(pool.memset(c["subcausal"][:, :], 1.0))
    link(pool.memset(c["eye"][:, :], 0.0))
    link(pool.memset(c["low1"][:, :], 0.0))
    for n in c["levels"]:
        link(pool.memset(c[f"up{n}"][:, :], 0.0))
        v = c[f"up{n}"][:, :].rearrange("p (b r) -> p b r", r=2 * n)
        link(pool.memset(v[:, :, n:2 * n], 1.0))
    v = c["low1"][:, :].rearrange("p (b r) -> p b r", r=2)
    link(pool.memset(v[:, :, 0:1], 1.0))
    link(pool.memset(c["first"][:, :], 1.0))
    v = c["first"][:, :].rearrange("p (b r) -> p b r", r=L)
    link(pool.memset(v[:, :, 0:1], 0.0))
    for a in half:
        for k, base in ((0, -1), (1, 0)):
            v = c["causal"][a, k, :]
            link(pool.affine_select(out=v, in_=v, compare_op=ALU.is_ge, fill=0.0, base=base,
                                    pattern=[[1, L]], channel_multiplier=-1))
        v = c["subcausal"][a, :]
        link(pool.affine_select(out=v, in_=v, compare_op=ALU.is_ge, fill=0.0, base=0,
                                pattern=[[1, L]], channel_multiplier=-1))
        if L > SUB:
            v = c["subcausal"][a, SUB:L]
            link(pool.affine_select(out=v, in_=v, compare_op=ALU.is_ge, fill=0.0, base=-SUB,
                                    pattern=[[0, SUB]], channel_multiplier=1))
        v = c["eye"][a, :]
        link(pool.affine_select(out=v, in_=v, compare_op=ALU.not_equal, fill=1.0, base=0,
                                pattern=[[-1, L]], channel_multiplier=1))
        for n in c["levels"]:
            v = c[f"up{n}"][a, :].rearrange("p (b r) -> p b r", r=2 * n)
            link(pool.affine_select(out=v, in_=v, compare_op=ALU.is_ge, fill=0.0, base=0,
                                    pattern=[[-2 * n, L // (2 * n)], [0, 2 * n]], channel_multiplier=1))
            link(pool.affine_select(out=v, in_=v, compare_op=ALU.is_ge, fill=0.0, base=n - 1,
                                    pattern=[[2 * n, L // (2 * n)], [0, 2 * n]], channel_multiplier=-1))
        v = c["low1"][a, :].rearrange("p (b r) -> p b r", r=2)
        link(pool.affine_select(out=v, in_=v, compare_op=ALU.is_equal, fill=0.0, base=-1,
                                pattern=[[-2, L // 2], [0, 2]], channel_multiplier=1))


def mixer_pass(nc, tag, T, TT, L, pc, dtr, yt, w, state_in, state_out, ahead=(), ahead_in=None):
    NCH, NSUB = TT // L, L // SUB
    NB = min(2, T // TT)
    rows = [slice(0, P)] if L == 64 else [slice(0, L), slice(64, 64 + L)]
    halves = [slice(0, 64), slice(64, 128)]
    hrows = [slice(0, L), slice(64, 64 + L)]

    with ExitStack() as ctx:
        def sb(name, shape):
            return ctx.enter_context(nc.sbuf_tensor(f"{tag}_{name}", shape, F32))

        def sem(name):
            return ctx.enter_context(nc.semaphore(f"{tag}_{name}"))

        ctx.enter_context(nc.allow_non_contiguous_dma(reason="vectors over channels, one value per partition, once"))
        c = make_masks(nc, ctx, L, tag)
        ps = ctx.enter_context(nc.psum_tensor(f"{tag}_ps", [P, 8, BANK], F32))

        conv_in = sb("conv_in", [P, 10, HALO + TT])
        mix_in = sb("mix_in", [P, 13, 1 + TT])
        gate_io = [sb(f"gate_io{j}", [P, 16, TT]) for j in range(NB)]
        hg_in = [sb(f"hg_in{j}", [P, 12, TT]) for j in range(NB)]
        dt_in = [sb(f"dt_in{j}", [TT, HEADS]) for j in range(NB)]

        conv_w = sb("conv_w", [P, 4, 10])
        conv_b = sb("conv_b", [P, 10])
        lru_w = sb("lru_w", [P, 2, 4, P])
        lru_b = sb("lru_b", [P, 2, 4])
        lam = sb("lam", [P, 4])
        mu = sb("mu", [P, 13])
        up_w = sb("up_w", [P, D_GROUP])
        up_b = sb("up_b", [P, 2, 4])
        kvec = sb("kvec", [P, 6, 4])
        gains = sb("gains", [P, 2, 4])
        dt_par = sb("dt_par", [P, 2, HEADS])
        half_ka = sb("half_ka", [P, 4])
        neg_a = sb("neg_a", [P, HEADS])
        sp = sb("sp", [P, 4, 4])

        lru_h = sb("lru_h", [P, 4])
        wkv = [sb(f"wkv{k}", [P, PAIRS, HEAD]) for k in range(2)]
        ssd_h = sb("ssd_h", [P, 4, HEAD])
        hg_s = sb("hg_s", [P, PAIRS, HEAD])
        turn = sb("turn", [P, 2, PAIRS, HEAD])

        def by_channel(name, n=4):
            return sb(name, [P, n, TT])

        def of_heads(name, n):
            return sb(name, [P, NCH, PAIRS, n])

        cv = by_channel("cv", 10)
        ri_buf = sb("ri_buf", [P, 2 * D_GROUP])
        ri = ri_buf[:, 0:8 * TT].rearrange("p (a t) -> p a t", a=8)
        x_dt, x_dd = (ri_buf[:, a:a + D_GROUP].rearrange("p (h v) -> p h v", h=HEADS) for a in (0, D_GROUP))
        ls, la, lth, lu = (by_channel(n) for n in ("ls", "la", "lth", "lu"))
        gate_tanh = by_channel("gate_tanh", 16)
        xbc = by_channel("xbc", 6)
        seg = by_channel("seg", HEADS)
        dts = sb("dts", [P, 10, HEADS])
        d_a = sb("d_a", [P, HEADS])
        acs = sb("acs", [P, HEADS])
        cb = sb("cb", [P, 2, TT])
        e_acs = by_channel("e_acs")
        tot = sb("tot", [P, HEADS])
        b_tok = sb("b_tok", [P, P])
        yc, yc2 = by_channel("yc"), by_channel("yc2")
        rms = sb("rms", [P, TT])
        eps = sb("eps", [P, 3])
        xm = by_channel("xm", 13)
        tw = sb("tw", [64, TT])
        wa = by_channel("wa", 8)
        cum, cum_b, e_cum, e_neg = (by_channel(n) for n in ("cum", "cum_b", "e_cum", "e_neg"))
        e_end = [sb(f"e_end{j}", [P, 4, NCH]) for j in range(NB)]
        kk, kk2, kp = (by_channel(n) for n in ("kk", "kk2", "kp"))
        kr = [sb(f"kr{j}", [P, 4, 2, TT]) for j in range(NB)]
        bneg, khat, bv = (by_channel(n) for n in ("bneg", "khat", "bv"))
        rhs, sa = (sb(n, [P, PAIRS, HEAD]) for n in ("rhs", "sa"))
        mt_pt, nt_qt = of_heads("mt_pt", 2 * L), of_heads("nt_qt", 2 * L)
        lev = {n: of_heads(f"lev{n}", L) for n in c["levels"][1:]}
        qi = of_heads("qi", L)
        tu_inv = sb("tu_inv", [P, NCH, 2, PAIRS, L])
        tinv, uinv = tu_inv[:, :, 0, :, :], tu_inv[:, :, 1, :, :]
        v_tok, b_key, k_key = (of_heads(n, HEAD) for n in ("v_tok", "b_key", "k_key"))
        yb, yb2 = by_channel("yb"), by_channel("yb2")
        fe, logf, hcum, tq = (by_channel(n) for n in ("fe", "logf", "hcum", "tq"))
        hk, hk2, hq = (by_channel(n) for n in ("hk", "hk2", "hq"))
        hq2 = [by_channel(f"hq2_{j}") for j in range(NB)]
        mid_sum = sb("mid_sum", [P, 4 * NCH, NSUB])
        mids = sb("mids", [P, 4 * NCH, 2, NSUB])
        ends = [sb(f"ends{j}", [P, 4 * NCH, 2]) for j in range(NB)]
        att = of_heads("att", L)
        hv_tok, hk_key, hs_mid = (of_heads(n, HEAD) for n in ("hv_tok", "hk_key", "hs_mid"))
        yd, yd2 = by_channel("yd"), by_channel("yd2")

        weights_in, states_in = sem("weights_in"), sem("states_in")
        in_loaded = sem("in_loaded")
        loaded = [sem(f"loaded{j}") for j in range(NB)]
        stored = sem("stored")
        states_stored = sem("states_stored")
        lru_w_clear, masks_made, pool_link = sem("lru_w_clear"), sem("masks_made"), sem("pool_link")
        vec_link, prep_vec, prep_act = sem("vec_link"), sem("prep_vec"), sem("prep_act")
        waits_met = sem("waits_met")
        turned_in, turned_out = sem("turned_in"), sem("turned_out")
        states_set, turn_pe = sem("states_set"), sem("turn_pe")
        table = STEPS.setdefault(tag, {})
        pe_s = Steps(sem("pe_steps"), "pe", table)
        v_s = Steps(sem("vector_steps"), "vector", table)
        a_s = Steps(sem("scalar_steps"), "scalar", table)
        g_s = Steps(sem("pool_steps"), "pool", table)
        back_steps = (pe_s, v_s, a_s, g_s)
        pe_f = Steps(sem("pe_front_steps"), "pe_front", table)
        v_f = Steps(sem("vector_front_steps"), "vector_front", table)
        a_f = Steps(sem("scalar_front_steps"), "scalar_front", table)
        g_f = Steps(sem("pool_front_steps"), "pool_front", table)
        front_steps = (pe_f, v_f, a_f, g_f)

        def col(v):
            return v.rearrange("a (t p) -> p (a t)", p=P)

        weights = [
            (conv_b[:, 0:4], col(w["lru_conv_b"])), (conv_b[:, 4:10], col(w["ssd_conv_b"])),
            (lru_b[:, 0, :], col(w["lru_b_r"])), (lru_b[:, 1, :], col(w["lru_b_i"])),
            (lam[:, :], col(w["lru_lambda"])), (mu[:, :], col(w["rwkv_mu"])),
            (up_w[0:64, :], w["rwkv_w_up"][0, :, :]), (up_w[64:128, :], w["rwkv_a_up"][0, :, :]),
            (up_b[:, 0, :], col(w["rwkv_w0"])), (up_b[:, 1, :], col(w["rwkv_a0"])),
            (kvec[:, 0, :], col(w["rwkv_k_k"])), (kvec[:, 1, :], col(w["rwkv_k_a"])),
            (kvec[:, 2, :], col(w["rwkv_r_k"].rearrange("a h k -> a (h k)"))),
            (kvec[:, 3, :], col(w["rwkv_ln_g"])), (kvec[:, 4, :], col(w["rwkv_ln_b"])),
            (gains[:, 0, :], col(w["ssd_norm_g"])), (gains[:, 1, :], col(w["hgrn_norm_g"])),
            (dt_par[:, 0, :], w["ssd_dt_bias"].broadcast_to([P, HEADS])),
            (dt_par[:, 1, :], w["ssd_a_log"].broadcast_to([P, HEADS])),
        ]
        for j in range(CONV_W):
            weights += [(conv_w[:, j, 0:4], col(w["lru_conv_w"][:, j, :])),
                        (conv_w[:, j, 4:10], col(w["ssd_conv_w"][:, j, :]))]
        for h in range(2):
            d = w["ssd_d"].rearrange("a (q h) -> h (a q)", h=2)[h:h + 1, :]
            weights.append((kvec[halves[h], 5, :], d.broadcast_to([64, PAIRS])))
            for g, name in ((0, "lru_w_r"), (1, "lru_w_i")):
                block_w = w[name].rearrange("a (q h) d e -> h d (a q) e", h=2)
                weights.append((lru_w[halves[h], g, :, halves[h]], block_w[h, :, :, :]))

        def state_views(s):
            out = [(lru_h[:, :], col(s["lru_h"].rearrange("a b c -> (a b) c"))),
                   (hg_s[:, :, :], s["hgrn_s"].rearrange("a b (q h) k v -> (h k) (a b q) v", h=2))]
            for h in range(2):
                wk = s["wkv"].rearrange("a b (q h) v k -> h v (a b q) k", h=2)
                out.append((turn[halves[h], 0, :, :], wk[h, :, :, :]))
                sh = s["ssd_h"].rearrange("a b h p n -> p (a b h) n")
                out.append((turn[halves[h], 1, :, :], sh[:, 4 * h:4 * h + 4, :]))
            return out

        IN_LOADS, LOADS = 3, 6
        TILES = T // TT
        block = ctx.enter_context(nc.Block())

        def at_tile(i):
            for s in back_steps:
                s.iteration(i)
            for s in front_steps:
                s.iteration(i + 1)

        def each_tile(eng, front, body):
            at_tile(-1)
            front()
            if TILES > NB:
                with eng.Fori(0, TILES // NB - 1) as n:
                    for j in range(NB):
                        at_tile(NB * n + j)
                        body(j, n, True)
            for j in range(NB):
                at_tile(TILES - NB + j)
                body(j, TILES // NB - 1, j < NB - 1)

        def next_of(j, n):
            return (j + 1) % NB, n + (j + 1) // NB

        def in_ready(eng, i):
            eng.wait_ge(in_loaded, i * 16 * IN_LOADS + 16 * IN_LOADS)

        def ready(eng, j, n):
            eng.wait_ge(loaded[j], n * 16 * LOADS + 16 * LOADS)

        def fronts_done(eng, me):
            for s in front_steps:
                if s is not me:
                    eng.wait_ge(*s.before())

        @block.sync
        def _(sync):
            def load_in(i):
                for dst, t, n, off, m in (
                        (conv_in[:, 0:4, :], XA, 4, 0, HALO + TT), (conv_in[:, 4:10, :], XBC, 6, 0, HALO + TT),
                        (mix_in[:, :, :], PB, 13, HALO - 1, 1 + TT)):
                    src = pc[t:t + n, :, bass.ds(i * TT + off, m)].rearrange("t p m -> p t m")
                    sync.dma_start(dst, src).then_inc(in_loaded, 16)

            def load(i, j):
                for dst, t, n in ((gate_io[j][:, 0:4, :], GA, 4), (gate_io[j][:, 4:8, :], GB, 4),
                                  (gate_io[j][:, 8:12, :], Z, 4), (gate_io[j][:, 12:16, :], GD, 4),
                                  (hg_in[j][:, :, :], QD, 12)):
                    src = pc[t:t + n, :, bass.ds(i * TT + HALO, TT)].rearrange("t p m -> p t m")
                    sync.dma_start(dst, src).then_inc(loaded[j], 16)
                sync.dma_start(dt_in[j][:, :], dtr[bass.ds(i * TT, TT), :]).then_inc(loaded[j], 16)

            def settle():
                sync.sem_inc(waits_met, 1)

            def tile(i, j, more):
                at_tile(i)
                if more:
                    sync.wait_ge(*v_f.at("conv"))
                    settle()
                    sync.wait_ge(*v_f.at("shift"))
                    settle()
                    load_in(i + 2)
                sync.wait_ge(*v_s.at("y_rwkv"))
                settle()
                sync.wait_ge(*v_f.before())
                settle()
                sync.dma_start(yt[:, :, bass.ds(i * TT, TT)].rearrange("t p m -> p t m"),
                               gate_io[j][:, :, :]).then_inc(stored, 16)
                if more:
                    sync.wait_ge(stored, i * 16 + 16)
                    settle()
                    sync.wait_ge(*pe_s.at("h_keys"))
                    settle()
                    load(i + 2, j)

            load_in(0)
            for dst, src in weights[:len(weights) // 2]:
                sync.dma_start(dst, src).then_inc(weights_in, 16)
            load(0, 0)
            if state_in is not None:
                for dst, src in state_views(state_in):
                    sync.dma_start(dst, src).then_inc(states_in, 16)
            for dst, src in ahead:
                sync.dma_start(dst, src).then_inc(ahead_in, 16)
            if TILES > 1:
                at_tile(-1)
                sync.wait_ge(*v_f.at("conv"))
                sync.wait_ge(*v_f.at("shift"))
                load_in(1)
                load(1, 1)
                with sync.Fori(0, TILES // NB - 1) as i:
                    for j in range(NB):
                        tile(NB * i + j, j, True)
            for j in range(NB):
                tile(TILES - NB + j, j, False)
            sync.wait_ge(stored, 16 * TILES)
            sync.wait_ge(turned_out, 2)
            out = [(src, dst) for dst, src in state_views(state_out)]
            for j in range(HALO):
                for name, a, n in (("lru_conv", 0, 4), ("ssd_conv", 4, 6)):
                    out.append((col(state_out[name][:, 0, j, :]), conv_in[:, a:a + n, TT + j]))
            out.append((col(state_out["shift"][:, 0, :]), mix_in[:, :, TT]))
            for dst, src in out:
                sync.dma_start(dst, src).then_inc(states_stored, 16)
            sync.wait_ge(states_stored, 16 * len(out))

        def chunk(ap, k):
            return ap[..., k * L:(k + 1) * L]

        @block.gpsimd
        def _(pool):
            count = [0]

            def link(ins):
                count[0] += 1
                ins.then_inc(pool_link, 1)
                pool.wait_ge(pool_link, count[0])

            link(pool.memset(lru_w[:, :, :, :], 0.0))
            pool.sem_inc(lru_w_clear, 1)
            for k, e in enumerate((1e-12, NORM_EPS, RWKV_LN_EPS)):
                link(pool.memset(eps[:, k:k + 1], e))
            fill_masks(pool, link, c, L)
            pool.sem_inc(masks_made, 1)
            pool.wait_ge(weights_in, 16 * len(weights))

            def mul(steps, o, a, b, name, op=ALU.mult):
                pool.tensor_tensor(o, a, b, op).then_inc(*steps.did(name))
                pool.wait_ge(*steps.last())

            def front_shift(prev):
                if prev:
                    pool.wait_ge(*v_s.at("bonus_v"))
                    pool.wait_ge(*pe_s.at("keys"))
                mul(g_f, xm[:, :, :], mix_in[:, :, 0:TT], mix_in[:, :, 1:1 + TT], "shift_diff", ALU.subtract)

            def front_keys():
                pool.wait_ge(*v_f.at("shift"))
                mul(g_f, kk[:, :, :], xm[:, 4:8, :], bc(kvec[:, 0, :], 2, TT), "kk_raw")
                mul(g_f, kk2[:, :, :], kk[:, :, :], kk[:, :, :], "kk_square")

            def front_bonus():
                pool.wait_ge(*v_f.at("kk_unit"))
                mul(g_f, kk2[:, :, :], xm[:, 0:4, :], kp[:, :, :], "rk")
                mul(g_f, kk2[:, :, :], kk2[:, :, :], bc(kvec[:, 2, :], 2, TT), "rk_weighed")

            def front_square():
                pool.wait_ge(*v_f.at("yc"))
                mul(g_f, yc2[:, :, :], yc[:, :, :], yc[:, :, :], "yc_square")
                mul(g_f, yc[:, :, :], yc[:, :, :], bc(gains[:, 0, :], 2, TT), "yc_gain")

            def front():
                in_ready(pool, 0)
                front_shift(False)
                front_keys()
                front_bonus()
                front_square()

            def body(j, n, more):
                pool.wait_ge(*v_s.at("mt_pt"))
                mt = mt_pt[:, :, :, 0:L].rearrange("p c q t -> p (c q) t")
                both = lambda a, r: a[r].rearrange("p c q t -> p (c q) t")
                for r in rows:
                    mul(g_s, uinv[r], mt_pt[r, :, :, 0:L], bc(bc(c["up1"][r, :], 1, PAIRS), 1, NCH), f"u_off{r.start}")
                for r in rows:
                    mul(g_s, uinv[r], uinv[r], bc(bc(c["eye"][r, :], 1, PAIRS), 1, NCH), f"u0{r.start}", ALU.add)
                for m in c["levels"][1:]:
                    for r in rows:
                        mul(g_s, both(lev[m], r), mt[r], bc(c[f"up{m}"][r, :], 1, NCH * PAIRS), f"lev{m}_{r.start}")
                    if more and m == 2:
                        in_ready(pool, NB * n + j + 1)
                        front_shift(True)
                if more:
                    front_keys()
                pool.wait_ge(*v_s.at("bonus_v"))
                mul(g_s, bv[:, :, :], bv[:, :, :], bc(kvec[:, 4, :], 2, TT), "bonus_bias", ALU.add)
                if more:
                    front_bonus()
                pool.wait_ge(*a_s.at("yd_copy"))
                mul(g_s, yd[:, :, :], yd[:, :, :], bc(gains[:, 1, :], 2, TT), "yd_gain")
                pool.wait_ge(*v_s.at("yb_centred"))
                mul(g_s, yb2[:, :, :], yb[:, :, :], yb[:, :, :], "yb_square")
                mul(g_s, yb[:, :, :], yb[:, :, :], bc(kvec[:, 3, :], 2, TT), "yb_gain")
                if more:
                    front_square()

            g_s.start(pool)
            g_f.start(pool)
            each_tile(pool, front, body)

        @block.scalar
        def _(act):
            act.wait_ge(lru_w_clear, 1)
            for dst, src in weights[len(weights) // 2:]:
                act.dma_start(dst, src).then_inc(weights_in, 16)
            act.wait_ge(weights_in, 16 * len(weights))
            act.activation(sp[:, 0, :], lam[:, :], ACT.Exp, scale=-1.0).then_inc(prep_act, 1)
            act.activation(neg_a[:, :], dt_par[:, 1, :], ACT.Exp).then_inc(prep_act, 1)
            act.wait_ge(prep_vec, 1)
            act.activation(sp[:, 2, :], sp[:, 1, :], ACT.Ln).then_inc(prep_act, 1)

            def f(o, x, fn, name, scale=1.0, **k):
                act.activation(o, x, fn, scale=scale, **k).then_inc(*a_f.did(name))

            def b(o, x, fn, name, scale=1.0, **k):
                act.activation(o, x, fn, scale=scale, **k).then_inc(*a_s.did(name))

            def tile_of(k):
                return ps[:, k, 0:4 * TT].rearrange("p (q t) -> p q t", q=4)

            def front_inputs(j):
                f(gate_tanh[:, :, :], gate_io[j][:, :, :], ACT.Tanh, "gate_tanh", 0.5)
                f(tq[:, :, :], hg_in[j][:, 0:4, :], ACT.Tanh, "q_tanh", 0.5)
                f(fe[:, :, :], hg_in[j][:, 4:8, :], ACT.Abs, "f_abs")
                act.wait_ge(*a_f.last())
                f(fe[:, :, :], fe[:, :, :], ACT.Exp, "f_exp", -1.0)
                act.wait_ge(*v_f.at("dt_x"))
                f(dts[0:TT, 1, :], dts[0:TT, 0, :], ACT.Abs, "dt_abs")
                act.wait_ge(*a_f.last())
                f(dts[0:TT, 2, :], dts[0:TT, 1, :], ACT.Exp, "dt_exp", -1.0)

            def front_conv():
                act.wait_ge(*v_f.at("conv"))
                f(xbc[:, :, :], cv[:, 4:10, :], ACT.Tanh, "xbc_tanh", 0.5)
                act.wait_ge(*v_f.at("xbc_twice"))
                f(xbc[:, :, :], xbc[:, :, :], ACT.Copy, "xbc", 0.5)

            def front_decay_input():
                act.wait_ge(*v_f.at("shift"))
                f(tw[:, :], xm[0:64, 12, :], ACT.Tanh, "wl_tanh")

            def front_lru():
                act.wait_ge(*v_f.at("lru_biased"))
                f(ri[:, :, :], ri[:, :, :], ACT.Tanh, "ri_tanh", 0.5)

            def front_lru_decay():
                act.wait_ge(*v_f.at("lru_s"))
                f(la[:, :, :], ls[:, :, :], ACT.Exp, "lru_a", -1.0)
                f(lth[:, :, :], ls[:, :, :], ACT.Tanh, "lru_th")

            def front_decay():
                act.wait_ge(*v_f.at("up_biased"))
                f(wa[:, :, :], wa[:, :, :], ACT.Tanh, "wa_tanh", 0.5)

            def front_decay_sums():
                act.wait_ge(*v_f.at("cum_before"))
                f(e_cum[:, :, :], cum[:, :, :], ACT.Exp, "e_cum")
                f(e_neg[:, :, :], cum[:, :, :], ACT.Exp, "e_neg", -1.0)
                f(cum_b[:, :, :], cum_b[:, :, :], ACT.Exp, "e_before")

            def front_logs():
                act.wait_ge(*v_f.at("dt_one_plus"))
                f(dts[0:TT, 4, :], dts[0:TT, 3, :], ACT.Ln, "dt_ln")
                f(logf[:, :, :], logf[:, :, :], ACT.Ln, "f_ln")
                act.wait_ge(*pe_f.at("kk_norm"))
                f(kk2[:, :, :], tile_of(5), ACT.Ln, "kk_ln", bias=eps[:, 0:1])
                act.wait_ge(*v_f.at("one_less_floor"))
                f(lth[:, :, :], lth[:, :, :], ACT.Ln, "one_less_ln")
                act.wait_ge(*a_f.last())
                f(kk2[:, :, :], kk2[:, :, :], ACT.Exp, "kk_exp", -0.5)
                f(lth[:, :, :], lth[:, :, :], ACT.Exp, "one_less_root", 0.5)

            def front_ssd(jn):
                act.wait_ge(*pe_f.at("acs"))
                f(e_acs[:, :, :], tile_of(5), ACT.Exp, "e_acs")
                act.wait_ge(*v_f.at("seg_clamped"))
                f(seg[0:TT, :, :], seg[0:TT, :, :], ACT.Exp, "seg_exp")
                act.wait_ge(*v_f.at("d_last"))
                f(tot[:, 0:4], tile_of(3)[:, :, TT - 1], ACT.Exp, "tot0")
                f(tot[:, 4:8], tile_of(4)[:, :, TT - 1], ACT.Exp, "tot1")
                f(dts[0:TT, 8, :], dts[0:TT, 8, :], ACT.Exp, "d_last_exp")

            def front_hgrn(j):
                act.wait_ge(*v_f.at("h_kx"))
                f(hk[:, :, :], hk[:, :, :], ACT.Exp, "h_k")
                f(hcum[:, :, :], hcum[:, :, :], ACT.Exp, "h_eq")
                f(mids[:, :, :, :].rearrange("p a b u -> p (a b u)"), mids[:, :, :, :].rearrange("p a b u -> p (a b u)"), ACT.Exp, "h_mids")
                f(ends[j][:, :, :].rearrange("p a b -> p (a b)"), ends[j][:, :, :].rearrange("p a b -> p (a b)"), ACT.Exp, "h_ends")

            def front_b_tok():
                act.wait_ge(*pe_f.at("x_tok"))
                f(b_tok[0:TT, :], ps[0:TT, 0, 0:P], ACT.Copy, "b_tok")

            def front_norm_ln():
                act.wait_ge(*pe_f.at("yc_ms"))
                f(rms[:, :], ps[:, 0, 0:TT], ACT.Ln, "yc_ln", bias=eps[:, 1:2])

            def front_norm_exp():
                act.wait_ge(*a_f.last())
                f(rms[:, :], rms[:, :], ACT.Exp, "yc_rms", -0.5)

            def front():
                ready(act, 0, 0)
                front_inputs(0)
                front_decay_input()
                front_lru()
                front_conv()
                front_lru_decay()
                front_decay()
                front_logs()
                front_decay_sums()
                front_ssd(0)
                front_b_tok()
                front_hgrn(0)
                front_norm_ln()
                front_norm_exp()

            def body(j, n, more):
                jn, nn = next_of(j, n)
                fronts_done(act, a_f)
                act.wait_ge(*pe_s.at("keys"))
                for r in rows:
                    b(v_tok[r].rearrange("p c q v -> p (c q v)"), ps[r, 3, 0:NCH * 256], ACT.Copy, f"v_tok{r.start}")
                    b(k_key[r].rearrange("p c q v -> p (c q v)"), ps[r, 5, 0:NCH * 256], ACT.Copy, f"k_key{r.start}")
                def level(m):
                    first = 1 if m == c["levels"][-1] else 0
                    for k in range(NCH):
                        act.wait_ge(*pe_s.at(f"tu{m}_{k}"))
                        for r in rows:
                            b(tu_inv[r, k, first:2, :, :].rearrange("p a q t -> p (a q t)"), ps[r, 1 + k, first * 4 * L:8 * L],
                              ACT.Copy, f"tu{m}_{k}_{r.start}")
                level(2)
                act.wait_ge(*pe_s.at("h_keys"))
                for r in rows:
                    b(hk_key[r].rearrange("p c q v -> p (c q v)"), ps[r, 4, 0:NCH * 256], ACT.Copy, f"hk_key{r.start}")
                    b(hv_tok[r].rearrange("p c q v -> p (c q v)"), ps[r, 5, 0:NCH * 256], ACT.Copy, f"hv_tok{r.start}")
                level(4)
                if more:
                    ready(act, jn, nn)
                    front_inputs(jn)
                    front_decay_input()
                level(8)
                if more:
                    front_lru()
                    front_conv()
                    front_lru_decay()
                    front_decay()
                level(16)
                if more:
                    front_logs()
                if L > 32:
                    level(32)
                if more:
                    front_decay_sums()
                if more:
                    front_ssd(jn)
                act.wait_ge(*pe_s.at("h_out"))
                b(yd2[:, :, :], tile_of(7), ACT.Square, "yd_square")
                b(yd[:, :, :], tile_of(7), ACT.Copy, "yd_copy")
                if more:
                    front_b_tok()
                act.wait_ge(*pe_s.at("y_rwkv"))
                b(yb[:, :, :], tile_of(2), ACT.Copy, "yb_copy")
                if more:
                    front_hgrn(jn)
                act.wait_ge(*pe_s.at("yb_var"))
                b(yb2[:, :, :], tile_of(2), ACT.Ln, "yb_ln", bias=eps[:, 2:3])
                b(yd2[:, :, :], tile_of(1), ACT.Ln, "yd_ln", bias=eps[:, 1:2])
                if more:
                    front_norm_ln()
                act.wait_ge(*a_s.last())
                b(yb2[:, :, :], yb2[:, :, :], ACT.Exp, "yb_rstd", -0.5)
                b(yd2[:, :, :], yd2[:, :, :], ACT.Exp, "yd_rms", -0.5)
                if more:
                    front_norm_exp()

            a_s.start(act)
            a_f.start(act)
            each_tile(act, front, body)

        @block.tensor
        def _(pe):
            pe.wait_ge(masks_made, 1)
            pe.wait_ge(weights_in, 16 * len(weights))
            ident = c["ident"]

            def mm(o, a, b, start=True, stop=True):
                return pe.matmul(o, a, b, start=start, stop=stop)

            def settle():
                pe.sem_inc(waits_met, 1)

            def tile_of(b, n=4):
                return ps[:, b, 0:n * TT].rearrange("p (q t) -> p q t", q=n)

            def flat(x):
                return x[:, :, :].rearrange("p a b -> p (a b)")

            def turn_states(src_of):
                for k in range(2):
                    for h in halves:
                        for q in range(PAIRS):
                            last = mm(ps[h, k, q * HEAD:(q + 1) * HEAD], src_of(k)[h, q, :], ident[h, h])
                last.then_inc(turn_pe, 1)

            if state_in is not None:
                pe.wait_ge(states_in, 16 * 6)
                turn_states(lambda k: turn[:, k, :, :])
            pe.wait_ge(states_set, 1)

            def front_gates(prev):
                pe.wait_ge(*v_f.at("conv"))
                if prev:
                    pe.wait_ge(*v_s.at("att"))
                    pe.wait_ge(*a_s.at(f"hk_key{rows[-1].start}"))
                settle()
                for g in range(2):
                    for t in range(4):
                        last = mm(tile_of(3 + g)[:, t, :], lru_w[:, g, t, :], cv[:, t, :])
                last.then_inc(*pe_f.did("lru_gates"))

            def front_up():
                pe.wait_ge(*a_f.at("wl_tanh"))
                pe.wait_ge(*v_f.at("lru_biased"))
                settle()
                for t in range(4):
                    mm(tile_of(3)[:, t, :], up_w[0:64, t * P:(t + 1) * P], tw[:, :])
                for t in range(4):
                    last = mm(tile_of(4)[:, t, :], up_w[64:128, t * P:(t + 1) * P], xm[64:128, 12, :])
                last.then_inc(*pe_f.did("up"))

            def front_kk(prev):
                pe.wait_ge(*g_f.at("kk_square"))
                if prev:
                    pe.wait_ge(*a_s.at(f"hv_tok{rows[-1].start}"))
                settle()
                mm(ps[:, 5, 0:4 * TT], c["headones"][:, :], flat(kk2)).then_inc(*pe_f.did("kk_norm"))

            def front_sums():
                pe.wait_ge(*v_f.at("d_a"))
                pe.wait_ge(*a_f.at("kk_ln"))
                settle()
                mm(ps[0:TT, 0, 0:HEADS], c["triu"][0:TT, 0:TT], d_a[0:TT, :])
                for h in range(HEADS):
                    row = d_a[0:TT, h:h + 1].broadcast_to([TT, P])
                    mm(tile_of(3 + h // 4)[:, h % 4, :], row, c["triu"][0:TT, 0:TT])

            def front_head_sums():
                for h in range(HEADS):
                    row = d_a[0:TT, h:h + 1].broadcast_to([TT, 64])
                    last = mm(tile_of(5)[halves[h % 2], h // 2, :], row, c["triu"][0:TT, 0:TT])
                last.then_inc(*pe_f.did("acs"))

            def front_cb():
                pe.wait_ge(*a_f.at("xbc"))
                pe.wait_ge(*v_f.at("acs"))
                settle()
                mm(ps[0:TT, 0, 0:TT], xbc[halves[0], 4, :], xbc[halves[0], 5, :]).then_inc(*pe_f.did("cb0"))
                pe.wait_ge(*pe_f.last())
                settle()
                mm(ps[0:TT, 0, TT:2 * TT], xbc[halves[1], 4, :], xbc[halves[1], 5, :]).then_inc(*pe_f.did("cb"))

            def front_x_tok():
                pe.wait_ge(*a_f.at("e_acs"))
                pe.wait_ge(*v_f.at("cb"))
                settle()
                for t in range(4):
                    pe.transpose(ps[0:TT, 5, t * P:(t + 1) * P], xbc[:, t, :], ident[:, :])
                pe.transpose(ps[0:TT, 0, 0:P], xbc[:, 4, :], ident[:, :]).then_inc(*pe_f.did("x_tok"))

            def front_ssd():
                pe.wait_ge(*v_f.at("x_dd"))
                pe.wait_ge(*a_f.at("b_tok"))
                settle()
                for h in range(HEADS):
                    mm(tile_of(3)[halves[h % 2], h // 2, :], x_dt[0:TT, h, :], seg[0:TT, h, :])
                for h in range(4):
                    last = mm(tile_of(4)[halves[h % 2], h // 2, :], ssd_h[halves[0], h, :], xbc[halves[0], 5, :])
                last.then_inc(*pe_f.did("ssd_inter0"))
                pe.wait_ge(*pe_f.last())
                settle()
                for h in range(4, HEADS):
                    mm(tile_of(4)[halves[h % 2], h // 2, :], ssd_h[halves[1], h - 4, :], xbc[halves[1], 5, :])
                for g in range(2):
                    last = mm(ps[halves[g], 5, 0:4 * HEAD], b_tok[0:TT, halves[g]],
                              x_dd[0:TT, 4 * g:4 * g + 4, :].rearrange("p h v -> p (h v)"))
                last.then_inc(*pe_f.did("ssd"))

            def front_norm():
                pe.wait_ge(*g_f.at("yc_square"))
                settle()
                for t in range(4):
                    last = mm(ps[:, 0, 0:TT], c["ones"][:, :], yc2[:, t, :], t == 0, t == 3)
                last.then_inc(*pe_f.did("yc_ms"))

            def front():
                front_gates(False)
                front_kk(False)
                front_up()
                front_sums()
                front_head_sums()
                front_cb()
                front_x_tok()
                front_ssd()
                front_norm()

            def by_head(o, left, right, width):
                for k in range(NCH):
                    for h in range(HEADS):
                        hh, q = h % 2, h // 2
                        last = mm(ps[hrows[hh], o, (k * PAIRS + q) * width:(k * PAIRS + q + 1) * width],
                                  left(hh, q, k), right(hh, q, k))
                return last

            def chan(x):
                return lambda hh, q, k: chunk(x[halves[hh], q, :], k)

            def toks(x):
                return lambda hh, q, k: x[hrows[hh], k, q, :]

            def eye(hh, q, k):
                return ident[halves[hh], halves[hh]]

            def body(j, n, more):
                jn, nn = next_of(j, n)
                pe.wait_ge(*v_f.at("e_end", 1))
                settle()
                def scores(bank, left):
                    for k in range(NCH):
                        for h in range(HEADS):
                            hh, q = h % 2, h // 2
                            last = mm(ps[hrows[hh], bank + k, q * 2 * L:(q + 1) * 2 * L].rearrange("p (a t) -> p a t", a=2),
                                      chunk(left[halves[hh], q, :], k), chunk(kr[j][halves[hh], q, :, :], k))
                    return last
                scores(6, bneg).then_inc(*pe_s.did("mt"))
                pe.wait_ge(*a_s.before())
                pe.wait_ge(*a_f.before())
                settle()
                by_head(0, lambda hh, q, k: chunk(kr[j][halves[hh], q, 0, :], k), chan(bneg), L).then_inc(*pe_s.did("n_off"))
                scores(1, khat).then_inc(*pe_s.did("nt"))
                pe.wait_ge(*v_f.at("h_q2", 1))
                settle()
                by_head(3, chan(xm[:, 8:12, :]), eye, HEAD)
                by_head(4, chan(bneg), eye, HEAD)
                by_head(5, chan(khat), eye, HEAD).then_inc(*pe_s.did("keys"))
                pe.wait_ge(*g_f.before())
                pe.wait_ge(*v_s.at(f"t_off{rows[-1].start}"))
                settle()
                mm(ps[:, 0, 0:4 * TT], c["headones"][:, :], flat(kk2)).then_inc(*pe_s.did("bonus"))

                def of_chunk(bank, at, left, right, k):
                    for h in range(HEADS):
                        hh, q = h % 2, h // 2
                        last = mm(ps[hrows[hh], bank + k, at + q * L:at + (q + 1) * L],
                                  left[hrows[hh], k, q, :], right[hrows[hh], k, q, :])
                    return last

                def q_level(m):
                    for k in range(NCH):
                        if m == 2:
                            pe.wait_ge(*v_s.at("t0"))
                        else:
                            pe.wait_ge(*a_s.at(f"tu{m // 2}_{k}_{rows[-1].start}"))
                        pe.wait_ge(*g_s.at(f"lev{m}_{rows[-1].start}"))
                        settle()
                        of_chunk(6, 0, lev[m], tinv, k).then_inc(*pe_s.did(f"q{m}_{k}"))

                def tu_level(m):
                    for k in range(NCH):
                        pe.wait_ge(*v_s.at(f"qi{m}_{k}_{rows[-1].start}"))
                        settle()
                        if m != c["levels"][-1]:
                            of_chunk(1, 0, uinv, qi, k)
                        of_chunk(1, 4 * L, qi, uinv, k).then_inc(*pe_s.did(f"tu{m}_{k}"))

                q_level(2)
                pe.wait_ge(*v_s.at("bonus_v"))
                pe.wait_ge(*a_s.at(f"k_key{rows[-1].start}"))
                settle()
                last = by_head(0, chan(hk), chan(hq), L)
                if NSUB == 2:
                    for k in range(NCH):
                        for h in range(HEADS):
                            hh, q = h % 2, h // 2
                            o = ps[64 * hh:64 * hh + SUB, 3, (k * PAIRS + q) * SUB:(k * PAIRS + q + 1) * SUB]
                            last = mm(o, hk[halves[hh], q, k * L:k * L + SUB], hq2[j][halves[hh], q, k * L + SUB:(k + 1) * L])
                last.then_inc(*pe_s.did("h_att"))
                tu_level(2)
                pe.wait_ge(*v_s.at(f"b_key{rows[-1].start}"))
                ready(pe, j, n)
                settle()
                by_head(4, chan(hk2), eye, HEAD)
                by_head(5, chan(hg_in[j][:, 8:12, :]), eye, HEAD).then_inc(*pe_s.did("h_keys"))
                q_level(4)
                tu_level(4)
                q_level(8)
                if more:
                    front_gates(True)
                tu_level(8)
                if more:
                    front_kk(True)
                    front_up()
                q_level(16)
                tu_level(16)
                pe.wait_ge(*a_s.at(f"hv_tok{rows[-1].start}"))
                settle()
                def states():
                    for k in range(NCH):
                        for h in range(HEADS):
                            hh, q = h % 2, h // 2
                            last = mm(ps[halves[hh], 6, (k * PAIRS + q) * HEAD:(k * PAIRS + q + 1) * HEAD],
                                      hk_key[hrows[hh], k, q, :], hv_tok[hrows[hh], k, q, :])
                    return last
                if L > 32:
                    q_level(32)
                    tu_level(32)
                pe.wait_ge(*v_s.at(f"qi{c['levels'][-1]}_{NCH - 1}_{rows[-1].start}"))
                settle()
                states().then_inc(*pe_s.did("h_kv"))
                pe.wait_ge(*a_s.at(f"tu{c['levels'][-1]}_{NCH - 1}_{rows[-1].start}"))
                settle()
                def outputs_hgrn():
                    pe.wait_ge(*v_s.at("h_states"))
                    settle()
                    for k in range(NCH):
                        for h in range(HEADS):
                            hh, q = h % 2, h // 2
                            o = chunk(ps[halves[hh], 7, q * TT:(q + 1) * TT], k)
                            mm(o, hs_mid[halves[hh], k, q, :], chunk(hq2[j][halves[hh], q, :], k), True, False)
                            last = mm(o, hv_tok[hrows[hh], k, q, :], att[hrows[hh], k, q, :], False, True)
                    last.then_inc(*pe_s.did("h_out"))

                for k in range(NCH):
                    now = wkv[k % 2]
                    if k:
                        pe.wait_ge(*v_s.at(f"wkv{k - 1}"))
                        settle()
                    for h in range(HEADS):
                        hh, q = h % 2, h // 2
                        o = ps[hrows[hh], 1, q * HEAD:(q + 1) * HEAD]
                        mm(o, chunk(kr[j][halves[hh], q, 0, :], k), now[halves[hh], q, :], True, False)
                        last = mm(o, nt_qt[hrows[hh], k, q, 0:L], v_tok[hrows[hh], k, q, :], False, True)
                    last.then_inc(*pe_s.did(f"rhs{k}"))
                    if more and k == 0:
                        front_sums()
                    if more and k == NCH - 1:
                        front_cb()
                    pe.wait_ge(*v_s.at(f"rhs{k}_{rows[-1].start}"))
                    settle()
                    for h in range(HEADS):
                        hh, q = h % 2, h // 2
                        last = mm(ps[hrows[hh], 1, 256 + q * HEAD:256 + (q + 1) * HEAD], uinv[hrows[hh], k, q, :], rhs[hrows[hh], q, :])
                    last.then_inc(*pe_s.did(f"sa{k}"))
                    if more and k == 0:
                        front_head_sums()
                    pe.wait_ge(*v_s.at(f"sa{k}_{rows[-1].start}"))
                    settle()
                    for h in range(HEADS):
                        hh, q = h % 2, h // 2
                        o = ps[halves[hh], 1, q * HEAD:(q + 1) * HEAD]
                        mm(o, b_key[hrows[hh], k, q, :], sa[hrows[hh], q, :], True, False)
                        last = mm(o, k_key[hrows[hh], k, q, :], v_tok[hrows[hh], k, q, :], False, True)
                    last.then_inc(*pe_s.did(f"kv{k}"))
                    if k == NCH - 1:
                        outputs_hgrn()
                        if more:
                            front_x_tok()
                    for h in range(HEADS):
                        hh, q = h % 2, h // 2
                        o = chunk(ps[halves[hh], 2, q * TT:(q + 1) * TT], k)
                        mm(o, now[halves[hh], q, :], chunk(kr[j][halves[hh], q, 1, :], k), True, False)
                        mm(o, sa[hrows[hh], q, :], mt_pt[hrows[hh], k, q, L:2 * L], False, False)
                        last = mm(o, v_tok[hrows[hh], k, q, :], nt_qt[hrows[hh], k, q, L:2 * L], False, True)
                    last.then_inc(*pe_s.did(f"y_rwkv" if k == NCH - 1 else f"y_rwkv{k}"))
                pe.wait_ge(*a_s.at("yd_copy"))
                pe.wait_ge(*v_s.at(f"wkv{NCH - 1}"))
                settle()
                mm(ps[:, 1, 0:4 * TT], c["headmean"][:, :], flat(yd2))
                pe.wait_ge(*a_s.at("yb_copy"))
                settle()
                mm(ps[:, 6, 0:4 * TT], c["headmean"][:, :], flat(yb)).then_inc(*pe_s.did("yb_mean"))
                if more:
                    front_ssd()
                pe.wait_ge(*g_s.at("yb_square"))
                settle()
                mm(ps[:, 2, 0:4 * TT], c["headmean"][:, :], flat(yb2)).then_inc(*pe_s.did("yb_var"))
                if more:
                    front_norm()

            pe_s.start(pe)
            pe_f.start(pe)
            each_tile(pe, front, body)
            at_tile(TILES)
            for s in back_steps:
                pe.wait_ge(*s.before())
                settle()
            turn_states(lambda k: (wkv[NCH % 2], ssd_h)[k][:, :, :])

        @block.vector
        def _(vec):
            count = [0]

            def link(ins):
                count[0] += 1
                ins.then_inc(vec_link, 1)
                vec.wait_ge(vec_link, count[0])

            vec.wait_ge(masks_made, 1)
            vec.wait_ge(weights_in, 16 * len(weights))
            vec.wait_ge(prep_act, 2)
            vec.tensor_scalar(sp[:, 1, :], sp[:, 0, :], 1.0, None, ALU.add).then_inc(prep_vec, 1)
            vec.wait_ge(prep_vec, 1)
            vec.wait_ge(prep_act, 3)
            log1p(vec, link, sp[:, 0, :], sp[:, 1, :], sp[:, 2, :], sp[:, 3, :], ls[:, 0:4, 0])
            link(vec.tensor_scalar(sp[:, 3, :], sp[:, 3, :], LRU_C / 2, None, ALU.mult))
            link(vec.tensor_scalar(half_ka[:, :], kvec[:, 1, :], 0.5, None, ALU.mult))
            link(vec.tensor_scalar(neg_a[:, :], neg_a[:, :], -1.0, None, ALU.mult))
            if state_in is None:
                for s in (lru_h[:, :], wkv[0][:, :, :], ssd_h[:, :, :], hg_s[:, :, :]):
                    link(vec.memset(s, 0.0))
            else:
                vec.wait_ge(turn_pe, 1)
                for k, s in enumerate((wkv[0], ssd_h)):
                    link(vec.tensor_copy(s[:, :, :].rearrange("p q v -> p (q v)"), ps[:, k, 0:4 * HEAD]))
            vec.sem_inc(states_set, 1)

            MUL, ADD, SUBTRACT = ALU.mult, ALU.add, ALU.subtract

            def makers(steps):
                def tt(o, a, b, op, name):
                    vec.tensor_tensor(o, a, b, op).then_inc(*steps.did(name))

                def ts(o, a, s1, s2, op0, op1, name):
                    vec.tensor_scalar(o, a, s1, s2, op0, *([op1] if op1 is not None else [])).then_inc(*steps.did(name))

                def stt(o, a, s1, b, op0, op1, name):
                    vec.scalar_tensor_tensor(o, a, s1, b, op0, op1).then_inc(*steps.did(name))

                def copy(o, a, name):
                    vec.tensor_copy(o, a).then_inc(*steps.did(name))

                def scan(o, a, b, name):
                    flat = [x.rearrange("p a t -> p (a t)") if len(x.shape) == 3 else x for x in (o, a, b)]
                    vec.tensor_tensor_scan(*flat, 0.0, MUL, ADD).then_inc(*steps.did(name))

                def own():
                    vec.wait_ge(*steps.last())

                return tt, ts, stt, copy, scan, own

            def four(b):
                return ps[:, b, 0:4 * TT].rearrange("p (q t) -> p q t", q=4)

            def eight(b):
                return ps[:, b:b + 2, 0:4 * TT].rearrange("p b (q t) -> p b q t", q=4)

            def as8(x):
                return x[:, :, :].rearrange("p (b q) t -> p b q t", b=2)

            def by_block(x):
                return x[:, :, :].rearrange("p a (c u t) -> p (a c) u t", c=NCH, u=NSUB)

            tt, ts, stt, copy, scan, own = makers(v_f)

            def front_taps(first, end):
                for k in range(first, end):
                    if k:
                        own()
                    for t in range(10):
                        x, w_k = conv_in[:, t, k:k + TT], conv_w[:, k, t:t + 1]
                        if k == 0:
                            ts(cv[:, t, :], x, w_k, conv_b[:, t:t + 1], MUL, ADD, f"tap0_{t}")
                        else:
                            stt(cv[:, t, :], x, w_k, cv[:, t, :], MUL, ADD,
                                "conv" if (k, t) == (CONV_W - 1, 9) else f"tap{k}_{t}")

            def front_dt_input(j):
                tt(dts[0:TT, 0, :], dt_in[j][:, :], dt_par[0:TT, 0, :], ADD, "dt_x")

            def front_inputs(j):
                vec.wait_ge(*a_f.at("q_tanh"))
                stt(gate_io[j][:, :, :], gate_tanh[:, :, :], 1.0, gate_io[j][:, :, :], ADD, MUL, "gates")
                stt(tq[:, :, :], tq[:, :, :], 1.0, hg_in[j][:, 0:4, :], ADD, MUL, "q_twice")
                vec.wait_ge(*a_f.at("dt_exp"))
                ts(logf[:, :, :], fe[:, :, :], 1.0, None, ADD, None, "f_one_plus")
                ts(dts[0:TT, 3, :], dts[0:TT, 2, :], 1.0, None, ADD, None, "dt_one_plus")
                vec.wait_ge(*a_f.at("xbc_tanh"))
                stt(xbc[:, :, :], xbc[:, :, :], 1.0, cv[:, 4:10, :], ADD, MUL, "xbc_twice")

            def front_shift():
                vec.wait_ge(*g_f.at("shift_diff"))
                for t in range(13):
                    stt(xm[:, t, :], xm[:, t, :], mu[:, t:t + 1], mix_in[:, t, 1:1 + TT], MUL, ADD,
                        "shift" if t == 12 else f"shift_{t}")

            def front_lru_gates():
                vec.wait_ge(*pe_f.at("lru_gates"))
                tt(as8(ri), eight(3), bc(lru_b[:, :, :], 3, TT), ADD, "lru_biased")

            def front_lru_inputs():
                vec.wait_ge(*a_f.at("ri_tanh"))
                stt(ls[:, :, :], ri[:, 0:4, :], 1.0, bc(sp[:, 3, :], 2, TT), ADD, MUL, "lru_s")
                stt(lu[:, :, :], ri[:, 4:8, :], 1.0, cv[:, 0:4, :], ADD, MUL, "lru_ix")

            def front_up():
                vec.wait_ge(*pe_f.at("up"))
                tt(as8(wa), eight(3), bc(up_b[:, :, :], 3, TT), ADD, "up_biased")

            def front_one_less():
                vec.wait_ge(*a_f.at("lru_th"))
                tt(ls[:, :, :], la[:, :, :], la[:, :, :], MUL, "a_square")
                own()
                stt(lth[:, :, :], ls[:, :, :], 1.0, lth[:, :, :], ADD, MUL, "one_less")
                own()
                ts(lth[:, :, :], lth[:, :, :], 1e-18, None, ALU.max, None, "one_less_floor")

            def front_decays():
                vec.wait_ge(*a_f.at("wa_tanh"))
                ts(wa[:, 0:4, :], wa[:, 0:4, :], -DECAY_SCALE / 2, -DECAY_SCALE / 2, MUL, ADD, "log_w")
                own()
                scan(cum[:, :, :], c["first"][:, 0:4 * TT], wa[:, 0:4, :], "cum")
                own()
                tt(cum_b[:, :, :], cum[:, :, :], wa[:, 0:4, :], SUBTRACT, "cum_before")
                stt(kp[:, :, :], wa[:, 4:8, :], -1.0, bc(half_ka[:, :], 2, TT), ADD, MUL, "kp_factor")
                own()
                stt(kp[:, :, :], kp[:, :, :], 1.0, xm[:, 4:8, :], ADD, MUL, "kp")

            def front_dt():
                vec.wait_ge(*a_f.at("dt_ln"))
                named_log1p(vec, v_f, dts[0:TT, 2, :], dts[0:TT, 3, :], dts[0:TT, 4, :], dts[0:TT, 5, :], dts[0:TT, 6, :], "dt")
                stt(dts[0:TT, 7, :], dts[0:TT, 0, :], 0.0, dts[0:TT, 5, :], ALU.max, ADD, "dt")
                own()
                tt(d_a[0:TT, :], dts[0:TT, 7, :], neg_a[0:TT, :], MUL, "d_a")

            def front_rwkv(j):
                vec.wait_ge(*a_f.at("kk_exp"))
                tt(kk[:, :, :], kk[:, :, :], kk2[:, :, :], MUL, "kk_unit")
                vec.wait_ge(*a_f.at("e_before"))
                tt(kr[j][:, :, 1, :], xm[:, 0:4, :], e_cum[:, :, :], MUL, "r_hat")
                own()
                tt(kr[j][:, :, 0, :], kk[:, :, :], cum_b[:, :, :], MUL, "kappa")

            def front_rwkv_keys(j):
                stt(bneg[:, :, :], wa[:, 4:8, :], 1.0, kk[:, :, :], ADD, MUL, "b_twice")
                tt(khat[:, :, :], kp[:, :, :], e_neg[:, :, :], MUL, "khat")
                own()
                stt(bneg[:, :, :], bneg[:, :, :], -0.5, e_neg[:, :, :], MUL, MUL, "bneg")
                copy(e_end[j][:, :, :], e_cum[:, :, :].rearrange("p a (c t) -> p a c t", t=L)[:, :, :, L - 1], "e_end")

            def front_lru(j):
                vec.wait_ge(*a_f.at("one_less_root"))
                stt(lu[:, :, :], lu[:, :, :], 0.5, lth[:, :, :], MUL, MUL, "lru_u")
                tt(sp[:, 0, :], la[:, :, 0], lru_h[:, :], MUL, "lru_carry")
                own()
                tt(lu[:, :, 0], lu[:, :, 0], sp[:, 0, :], ADD, "lru_u0")
                vec.memset(la[:, :, 0:1], 0.0).then_inc(*v_f.did("lru_cut"))
                own()
                scan(ls[:, :, :], la[:, :, :], lu[:, :, :], "lru_h")
                own()
                copy(lru_h[:, :], ls[:, :, TT - 1], "lru_state")
                stt(gate_io[j][:, 0:4, :], ls[:, :, :], 0.5, gate_io[j][:, 0:4, :], MUL, MUL, "y_lru")

            def front_hgrn(j):
                vec.wait_ge(*a_f.at("f_ln"))
                fd = hg_in[j][:, 4:8, :]
                stt(logf[:, :, :], fd, 0.0, logf[:, :, :], ALU.min, SUBTRACT, "logf")
                own()
                tt(hk[:, :, :], logf[:, :, :], fd, SUBTRACT, "log_k")
                scan(hcum[:, :, :], c["first"][:, 0:4 * TT], logf[:, :, :], "h_cum")
                own()
                mid = by_block(hcum)[:, :, :, SUB // 2 - 1]
                end = by_block(hcum)[:, :, NSUB - 1, SUB - 1]
                copy(ends[j][:, :, 0], mid[:, :, 0], "h_m0")
                copy(ends[j][:, :, 1], end, "h_end")
                copy(mid_sum[:, :, :], mid, "h_mid")
                own()
                tt(mids[:, :, 0, :], mid_sum[:, :, :], bc(ends[j][:, :, 0], 2, NSUB), SUBTRACT, "h_mid_span")
                tt(mids[:, :, 1, :], bc(ends[j][:, :, 1], 2, NSUB), mid_sum[:, :, :], SUBTRACT, "h_spans")
                b3 = hcum[:, :, :].rearrange("p a (m t) -> p (a m) t", t=SUB)
                tt(b3, b3, bc(mid_sum[:, :, :].rearrange("p a u -> p (a u)"), 2, SUB), SUBTRACT, "h_rel")
                own()
                tt(hk[:, :, :], hk[:, :, :], hcum[:, :, :], SUBTRACT, "h_kx")

            def front_hgrn_queries(j):
                vec.wait_ge(*a_f.at("h_ends"))
                stt(hq[:, :, :], tq[:, :, :], 0.5, hcum[:, :, :], MUL, MUL, "h_q")
                tt(by_block(hk2), by_block(hk), bc(mids[:, :, 1, :], 3, SUB), MUL, "h_k2")
                own()
                tt(by_block(hq2[j]), by_block(hq), bc(mids[:, :, 0, :], 3, SUB), MUL, "h_q2")

            def front_seg():
                vec.wait_ge(*pe_f.at("acs"))
                copy(acs[0:TT, :], ps[0:TT, 0, 0:HEADS], "acs")
                own()
                seg4 = seg[0:TT, :, :].rearrange("p (b q) t -> p b q t", b=2)
                tt(seg4, eight(3)[0:TT], bc(acs[0:TT, :], 2, TT).rearrange("p (b q) t -> p b q t", b=2), SUBTRACT, "seg")
                own()
                ts(seg[0:TT, :, :], seg[0:TT, :, :], 0.0, None, ALU.min, None, "seg_clamped")
                tt(dts[0:TT, 8, :].rearrange("p (b q) -> p b q", b=2), eight(3)[0:TT, :, :, TT - 1],
                   acs[0:TT, :].rearrange("p (b q) -> p b q", b=2), SUBTRACT, "d_last")

            def front_scores():
                vec.wait_ge(*pe_f.at("cb"))
                cb_ps = ps[0:TT, 0, 0:2 * TT].rearrange("p (g t) -> p g t", g=2)
                tt(cb[0:TT, :, :], cb_ps, bc(c["triu"][0:TT, 0:TT], 1, 2), MUL, "cb")
                vec.wait_ge(*a_f.at("d_last_exp"))
                tt(dts[0:TT, 9, :], dts[0:TT, 8, :], dts[0:TT, 7, :], MUL, "d_last_dt")
                own()
                for g in range(2):
                    sg = seg[0:TT, 4 * g:4 * g + 4, :]
                    tt(sg, sg, bc(cb[0:TT, g, :], 1, 4), MUL, f"ssd_scores{g}")

            def front_x():
                vec.wait_ge(*pe_f.at("x_tok"))
                x_tok = ps[0:TT, 5, 0:D_GROUP].rearrange("p (h v) -> p h v", h=HEADS)
                tt(x_dt[0:TT, :, :], x_tok, bc(dts[0:TT, 7, :], 2, HEAD), MUL, "x_dt")
                tt(x_dd[0:TT, :, :], x_tok, bc(dts[0:TT, 9, :], 2, HEAD), MUL, "x_dd")
                tt(yc[:, :, :], xbc[:, 0:4, :], bc(kvec[:, 5, :], 2, TT), MUL, "d_x")

            def front_ssd(j):
                vec.wait_ge(*pe_f.at("ssd"))
                tt(yc2[:, :, :], four(4), e_acs[:, :, :], MUL, "yc_inter")
                own()
                tt(yc[:, :, :], yc[:, :, :], four(3), ADD, "yc_intra")
                own()
                tt(yc[:, :, :], yc[:, :, :], yc2[:, :, :], ADD, "yc_sum")
                own()
                stt(yc[:, :, :], yc[:, :, :], 0.5, gate_io[j][:, 8:12, :], MUL, MUL, "yc")
                vec.wait_ge(*a_f.at("tot1"))
                for g in range(2):
                    hg = ssd_h[halves[g], :, :]
                    tt(hg, hg, bc(tot[halves[g], 4 * g:4 * g + 4], 2, HEAD), MUL, f"ssd_decay{g}")
                own()
                tt(ssd_h[:, :, :].rearrange("p q v -> p (q v)"), ssd_h[:, :, :].rearrange("p q v -> p (q v)"),
                   ps[:, 5, 0:4 * HEAD], ADD, "ssd_state")

            def front_norm(j):
                vec.wait_ge(*a_f.at("yc_rms"))
                vec.wait_ge(*g_f.at("yc_gain"))
                tt(gate_io[j][:, 8:12, :], yc[:, :, :], bc(rms[:, :], 1, 4), MUL, "y_ssd")

            def front():
                in_ready(vec, 0)
                ready(vec, 0, 0)
                front_taps(0, CONV_W)
                front_shift()
                front_dt_input(0)
                front_lru_gates()
                front_inputs(0)
                front_lru_inputs()
                front_up()
                front_one_less()
                front_decays()
                front_dt()
                front_rwkv(0)
                front_rwkv_keys(0)
                front_seg()
                front_lru(0)
                front_scores()
                front_x()
                front_hgrn(0)
                front_ssd(0)
                front_hgrn_queries(0)
                front_norm(0)

            btt, bts, bstt, bcopy, _, bown = makers(v_s)

            def body(j, n, more):
                jn, nn = next_of(j, n)
                fronts_done(vec, None)
                def masked(bank, dst, name):
                    for r in rows:
                        btt(dst[r].rearrange("p c q t -> p c (q t)").rearrange("p c (q t) -> p c q t", q=PAIRS),
                            ps[r, bank:bank + NCH, 0:8 * L].rearrange("p c (q t) -> p c q t", q=PAIRS),
                            bc(bc(c["causal"][r, :, :].rearrange("p a t -> p (a t)"), 1, PAIRS), 1, NCH), MUL,
                            name if r is rows[-1] else f"{name}_0")

                def mats(x, r):
                    return x[r].rearrange("p c q t -> p (c q) t")

                def bank_mats(bank, r, width=L):
                    return ps[r, bank, 0:NCH * 4 * width].rearrange("p (m t) -> p m t", t=width)

                vec.wait_ge(*pe_s.at("mt"))
                masked(6, mt_pt, "mt_pt")
                vec.wait_ge(*pe_s.at("n_off"))
                for r in rows:
                    btt(tinv[r], ps[r, 0, 0:NCH * 4 * L].rearrange("p (c q t) -> p c q t", c=NCH, t=L),
                        bc(bc(c["low1"][r, :], 1, PAIRS), 1, NCH), MUL, f"t_off{r.start}")
                bown()
                for r in rows:
                    btt(tinv[r], tinv[r], bc(bc(c["eye"][r, :], 1, PAIRS), 1, NCH), ADD, "t0" if r is rows[-1] else "t0_0")
                vec.wait_ge(*pe_s.at("nt"))
                masked(1, nt_qt, "nt_qt")
                vec.wait_ge(*pe_s.at("keys"))
                for r in rows:
                    bcopy(b_key[r].rearrange("p c q v -> p (c q v)"), ps[r, 4, 0:NCH * 256], f"b_key{r.start}")
                vec.wait_ge(*pe_s.at("bonus"))
                btt(bv[:, :, :], four(0), xm[:, 8:12, :], MUL, "bonus_v")

                def qi_level(m):
                    for k in range(NCH):
                        vec.wait_ge(*pe_s.at(f"q{m}_{k}"))
                        for r in rows:
                            btt(qi[r, k, :, :], ps[r, 6 + k, 0:4 * L].rearrange("p (m t) -> p m t", t=L),
                                bc(c["eye"][r, :], 1, PAIRS), ADD, f"qi{m}_{k}_{r.start}")

                qi_level(2)
                vec.wait_ge(*pe_s.at("h_att"))
                for r in rows:
                    btt(mats(att, r), bank_mats(0, r), bc(c["subcausal"][r, :], 1, NCH * PAIRS), MUL,
                        "att" if NSUB == 1 and r is rows[-1] else f"att_own{r.start}")
                if NSUB == 2:
                    bown()
                    for h in range(2):
                        r = slice(64 * h, 64 * h + SUB)
                        bcopy(mats(att, r)[:, :, SUB:L], bank_mats(3, r, SUB), "att" if h else "att_0")
                if more:
                    in_ready(vec, NB * n + j + 1)
                    front_taps(0, 2)
                qi_level(4)
                if more:
                    front_taps(2, CONV_W)
                    front_shift()
                qi_level(8)
                if more:
                    ready(vec, jn, nn)
                    front_dt_input(jn)
                    front_lru_gates()
                    front_inputs(jn)
                    front_lru_inputs()
                    front_up()
                qi_level(16)
                if more:
                    front_one_less()
                    front_decays()
                if L > 32:
                    qi_level(32)
                if more:
                    front_dt()
                vec.wait_ge(*pe_s.at("h_kv"))
                e2 = ends[j][:, :, :].rearrange("p (a c) b -> p a c b", c=NCH)
                for k in range(NCH):
                    btt(hs_mid[:, k, :, :], hg_s[:, :, :], bc(e2[:, :, k, 0], 2, HEAD), MUL, f"h_smid{k}")
                    btt(hg_s[:, :, :], hg_s[:, :, :], bc(e2[:, :, k, 1], 2, HEAD), MUL, f"h_decay{k}")
                    bown()
                    btt(hg_s[:, :, :].rearrange("p q v -> p (q v)"), hg_s[:, :, :].rearrange("p q v -> p (q v)"),
                        ps[:, 6, k * 256:(k + 1) * 256], ADD, "h_states" if k == NCH - 1 else f"h_state{k}")
                    bown()
                if more:
                    front_rwkv(jn)
                for k in range(NCH):
                    for stage, at, dst in (("rhs", 0, rhs), ("sa", 256, sa)):
                        vec.wait_ge(*pe_s.at(f"{stage}{k}"))
                        for r in rows:
                            bcopy(dst[r].rearrange("p q v -> p (q v)"), ps[r, 1, at:at + 256], f"{stage}{k}_{r.start}")
                    if more and k == 0:
                        front_rwkv_keys(jn)
                    if more and k == NCH - 1:
                        front_lru(jn)
                    vec.wait_ge(*pe_s.at(f"kv{k}"))
                    new = wkv[(k + 1) % 2]
                    btt(new[:, :, :].rearrange("p q v -> p (q v)"), wkv[k % 2][:, :, :].rearrange("p q v -> p (q v)"), ps[:, 1, 0:256], ADD, f"wkv_sum{k}")
                    bown()
                    btt(new[:, :, :], new[:, :, :], bc(e_end[j][:, :, k], 2, HEAD), MUL, f"wkv{k}")
                    if more and k == 0:
                        front_seg()
                if more:
                    front_scores()
                    front_x()
                    front_hgrn(jn)
                vec.wait_ge(*pe_s.at("yb_mean"))
                btt(yb[:, :, :], yb[:, :, :], four(6), SUBTRACT, "yb_centred")
                if more:
                    front_ssd(jn)
                    front_hgrn_queries(jn)
                vec.wait_ge(*a_s.at("yd_rms"))
                vec.wait_ge(*g_s.at("yb_gain"))
                btt(yb[:, :, :], yb[:, :, :], yb2[:, :, :], MUL, "yb_normed")
                btt(yd[:, :, :], yd[:, :, :], yd2[:, :, :], MUL, "yd_normed")
                bown()
                btt(yb[:, :, :], yb[:, :, :], bv[:, :, :], ADD, "yb_bonus")
                bstt(gate_io[j][:, 12:16, :], yd[:, :, :], 0.5, gate_io[j][:, 12:16, :], MUL, MUL, "y_hgrn")
                bown()
                bstt(gate_io[j][:, 4:8, :], yb[:, :, :], 0.5, gate_io[j][:, 4:8, :], MUL, MUL, "y_rwkv")
                if more:
                    front_norm(jn)

            v_s.start(vec)
            v_f.start(vec)
            each_tile(vec, front, body)
            vec.wait_ge(turn_pe, 2 if state_in is not None else 1)
            for k in range(2):
                vec.tensor_copy(turn[:, k, :, :].rearrange("p q v -> p (q v)"), ps[:, k, 0:4 * HEAD]).then_inc(turned_out, 1)


def log1p(vec, link, e, u, ln_u, out, tmp):
    link(vec.tensor_scalar(out, u, -1.0, None, ALU.add))
    link(vec.tensor_scalar(tmp, out, 0.0, None, ALU.is_equal))
    link(vec.tensor_tensor(out, out, tmp, ALU.add))
    link(vec.reciprocal(out, out))
    link(vec.tensor_tensor(tmp, ln_u, tmp, ALU.add))
    link(vec.tensor_tensor(tmp, tmp, e, ALU.mult))
    link(vec.tensor_tensor(out, out, tmp, ALU.mult))


def named_log1p(vec, steps, e, u, ln_u, out, tmp, name):
    n = [0]

    def link(ins):
        n[0] += 1
        ins.then_inc(*steps.did(f"{name}_log1p{n[0]}"))
        vec.wait_ge(*steps.last())

    log1p(vec, link, e, u, ln_u, out, tmp)


def memory_pass(nc, mem_prompt, mem_g, w_k, w_v, w_q, w_o, g_pre_x, cache_k, cache_v, mem_k, mem_v, qk, vo):
    MT = MEM_LEN // P

    with ExitStack() as ctx:
        def sb(name, shape):
            return ctx.enter_context(nc.sbuf_tensor(f"mem_{name}", shape, F32))

        def sem(name):
            return ctx.enter_context(nc.semaphore(f"mem_{name}"))

        ctx.enter_context(nc.allow_non_contiguous_dma(reason="vectors over channels, once"))
        wq = sb("wq", [P, KT, D_MODEL])
        wqT = sb("wqT", [P, KT, D_MODEL])
        wo = sb("wo", [P, KT, D_MODEL])
        w_half = [sb(f"w_half{j}", [P, KT, BANK]) for j in range(2)]
        mem = sb("mem", [P, MT, D_MODEL])
        memT = sb("memT", [P, KT, MEM_LEN])
        kv = sb("kv", [P, 2, MT, D_MODEL])
        kvT = sb("kvT", [P, 2, KT, MEM_LEN])
        out = [sb(f"out{j}", [P, D_MODEL]) for j in range(2)]
        gains = sb("gains", [P, 2, KT])
        rstd = sb("rstd", [P, MT])
        eps = sb("eps", [P, 1])
        ident = sb("ident", [P, P])
        ps = ctx.enter_context(nc.psum_tensor("mem_ps", [P, 8, BANK], F32))

        loaded, wq_in, wo_in = sem("loaded"), sem("wq_in"), sem("wo_in")
        half_in = [sem(f"half_in{j}") for j in range(2)]
        link_s, const_made, act_link = sem("link"), sem("const_made"), sem("act_link")
        normed, filled, emptied = sem("normed"), sem("filled"), sem("emptied")
        cache_in, kv_stored, stored = sem("cache_in"), sem("kv_stored"), [sem(f"stored{j}") for j in range(2)]
        kv_turned = sem("kv_turned")
        block = ctx.enter_context(nc.Block())

        fills = [("memT", m) for m in range(MT)]
        fills += [("kv", (a, m)) for a in range(2) for m in range(MT)]
        fills += [("wqT", k) for k in range(KT)]
        for g in range(2):
            fills += [("kvT", (g, a, m)) for a in range(2) for m in range(MT)]
            fills += [("qk", (g, k)) for k in range(KT)]
            fills += [("vo", (g, k)) for k in range(KT)]
        at = {f: n for n, f in enumerate(fills)}
        pair = lambda n: slice(2 * (n % 4), 2 * (n % 4) + 2)
        n_out = {}
        for f in fills:
            if f[0] in ("qk", "vo"):
                n_out[f] = len(n_out)

        @block.sync
        def _(sync):
            sync.dma_start(mem[:, :, :], mem_prompt[0, :, :].rearrange("(m p) d -> p m d", p=P)).then_inc(loaded, 16)
            sync.dma_start(gains[:, 0, :], mem_g.rearrange("a (k p) -> p (a k)", p=P)).then_inc(loaded, 16)
            sync.dma_start(gains[:, 1, :], g_pre_x.rearrange("a (k p) -> p (a k)", p=P)).then_inc(loaded, 16)
            rows_of = lambda w: w[0, :, :].rearrange("(k p) n -> p k n", p=P)
            for a, w in enumerate((w_k, w_v)):
                for half in range(2):
                    if a:
                        sync.wait_ge(filled, at[("kv", (0, MT - 1))] + 1)
                    sync.dma_start(w_half[half][:, :, :], rows_of(w)[:, :, half * BANK:(half + 1) * BANK]).then_inc(half_in[half], 16)
                if not a:
                    sync.dma_start(wq[:, :, :], rows_of(w_q)).then_inc(wq_in, 16)
                    sync.dma_start(wo[:, :, :], rows_of(w_o)).then_inc(wo_in, 16)
            sync.wait_ge(emptied, at[("kv", (1, MT - 1))] + 1)
            for a, dst in enumerate((mem_k, mem_v)):
                sync.dma_start(dst[0, 0].rearrange("(m p) h d -> p m (h d)", p=P), kv[:, a, :, :]).then_inc(kv_stored, 16)
            sync.wait_ge(kv_stored, 32)
            sync.wait_ge(filled, at[("kvT", (0, 1, MT - 1))] + 1)
            for a, src in enumerate((cache_k, cache_v)):
                sync.dma_start(kv[:, a, :, :], src[0, 0].rearrange("(m p) h d -> p m (h d)", p=P)).then_inc(cache_in, 16)

        @block.gpsimd
        def _(pool):
            count = [0]

            def link(ins):
                count[0] += 1
                ins.then_inc(link_s, 1)
                pool.wait_ge(link_s, count[0])

            link(pool.memset(eps[:, :], NORM_EPS))
            link(pool.memset(ident[:, :], 0.0))
            link(pool.affine_select(out=ident[:, :], in_=ident[:, :], compare_op=ALU.not_equal, fill=1.0,
                                    base=0, pattern=[[-1, P]], channel_multiplier=1))
            pool.sem_inc(const_made, 1)
            for f, n in n_out.items():
                name, (g, k) = f
                pool.wait_ge(emptied, at[f] + 1)
                dst = (qk if name == "qk" else vo)[g]
                pool.dma_start(dst[k, :, :], out[n % 2][:, :]).then_inc(stored[n % 2], 16)
            for j in range(2):
                pool.wait_ge(stored[j], 16 * (len(n_out) // 2))

        @block.scalar
        def _(act):
            load_ln_and_exp(nc, act)
            act.wait_ge(const_made, 1)
            act.wait_ge(loaded, 48)
            for m in range(MT):
                act.activation(out[m][:, :], mem[:, m, :], ACT.Square, accum_out=rstd[:, m:m + 1]).then_inc(act_link, 1)
            act.wait_ge(act_link, MT)
            act.activation(rstd[:, :], rstd[:, :], ACT.Ln, scale=1.0 / D_MODEL, bias=eps[:, :]).then_inc(act_link, 1)
            act.wait_ge(act_link, MT + 1)
            act.activation(rstd[:, :], rstd[:, :], ACT.Exp, scale=-0.5).then_inc(act_link, 1)

        @block.vector
        def _(vec):
            vec.wait_ge(act_link, MT + 2)
            for m in range(MT):
                vec.tensor_scalar(mem[:, m, :], mem[:, m, :], rstd[:, m:m + 1], None, ALU.mult).then_inc(normed, 1)
            for n, (name, k) in enumerate(fills):
                vec.wait_ge(filled, n + 1)
                b = ps[:, pair(n), :]
                turned = b.rearrange("p b (k t) -> p (b k) t", t=P)
                flat = b.rearrange("p b t -> p (b t)")
                if name == "memT":
                    ins = vec.tensor_tensor(memT[:, :, k * P:(k + 1) * P], turned, bc(gains[:, 0, :], 2, P), ALU.mult)
                elif name == "kv":
                    ins = vec.tensor_copy(kv[:, k[0], k[1], :], flat)
                elif name == "wqT":
                    ins = vec.tensor_copy(wqT[:, :, k * P:(k + 1) * P], turned)
                elif name == "kvT":
                    ins = vec.tensor_copy(kvT[:, k[1], :, k[2] * P:(k[2] + 1) * P], turned)
                else:
                    o = n_out[(name, k)]
                    vec.wait_ge(stored[o % 2], 16 * (o // 2))
                    if name == "qk":
                        ins = vec.tensor_scalar(out[o % 2][:, :], flat, gains[:, 1, k[1]:k[1] + 1],
                                                float(MEM_HEAD_DIM) ** -0.5, ALU.mult, ALU.mult)
                    else:
                        ins = vec.tensor_copy(out[o % 2][:, :], flat)
                ins.then_inc(emptied, 1)

        @block.tensor
        def _(pe):
            pe.wait_ge(const_made, 1)
            for n, (name, k) in enumerate(fills):
                b = ps[:, pair(n), :]
                cols = lambda c: b[:, c // 4, (c % 4) * P:(c % 4 + 1) * P]
                if n >= 4:
                    pe.wait_ge(emptied, n - 3)
                if name == "memT":
                    pe.wait_ge(normed, k + 1)
                    for c in range(KT):
                        last = pe.transpose(cols(c), mem[:, k, c * P:(c + 1) * P], ident[:, :])
                elif name == "kv":
                    a, m = k
                    pe.wait_ge(emptied, at[("memT", MT - 1)] + 1)
                    for half in range(2):
                        pe.wait_ge(half_in[half], 16 * (a + 1))
                        for c in range(KT):
                            last = pe.matmul(b[:, half, :], memT[:, c, m * P:(m + 1) * P], w_half[half][:, c, :],
                                             start=c == 0, stop=c == KT - 1)
                elif name == "wqT":
                    pe.wait_ge(wq_in, 16)
                    for c in range(KT):
                        last = pe.transpose(cols(c), wq[:, k, c * P:(c + 1) * P], ident[:, :])
                elif name == "kvT":
                    g, a, m = k
                    if g:
                        pe.wait_ge(cache_in, 32)
                    else:
                        pe.wait_ge(emptied, at[("kv", (1, MT - 1))] + 1)
                    for c in range(KT):
                        last = pe.transpose(cols(c), kv[:, a, m, c * P:(c + 1) * P], ident[:, :])
                elif name == "qk":
                    g, c = k
                    pe.wait_ge(emptied, at[("kvT", (g, 1, MT - 1))] + 1)
                    for h in range(MEM_HEADS):
                        for d in range(2):
                            last = pe.matmul(b[:, h // 2, (h % 2) * MEM_LEN:(h % 2 + 1) * MEM_LEN],
                                             wqT[:, 2 * h + d, c * P:(c + 1) * P], kvT[:, 0, 2 * h + d, :],
                                             start=d == 0, stop=d == 1)
                else:
                    g, c = k
                    pe.wait_ge(wo_in, 16)
                    for half in range(2):
                        for d in range(2):
                            t = 2 * (c // MT) + d
                            last = pe.matmul(b[:, half, :], kvT[:, 1, t, (c % MT) * P:(c % MT + 1) * P],
                                             wo[:, t, half * BANK:(half + 1) * BANK], start=d == 0, stop=d == 1)
                last.then_inc(filled, 1)


def attend_pass(nc, tag, T, TT, yt, x, y, g_post, g_post_x, weights, ahead_in, qk_vo):
    TILES = T // TT
    NB = min(2, TILES)
    with ExitStack() as ctx:
        def sb(name, shape):
            return ctx.enter_context(nc.sbuf_tensor(f"{tag}_{name}", shape, F32))

        def sem(name):
            return ctx.enter_context(nc.semaphore(f"{tag}_{name}"))

        w_o, qk_sb, vo_sb = weights
        gains = sb("gains", [P, 2, D_MODEL])
        yt_in = [sb(f"yt_in{j}", [P, YT, TT]) for j in range(NB)]
        x_in = [sb(f"x_in{j}", [TT, D_MODEL]) for j in range(NB)]
        x1 = [sb(f"x1_{j}", [TT, D_MODEL]) for j in range(NB)]
        hx = sb("hx", [TT, D_MODEL])
        turned = sb("turned", [P, KT, TT])
        probs = sb("probs", [TT, D_MODEL])
        o = sb("o", [TT, D_MODEL])
        small = sb("small", [TT, 8])
        mx = sb("mx", [TT, 3, MEM_HEADS])
        eps = sb("eps", [P, 1])
        ident = sb("ident", [P, P])
        ps = ctx.enter_context(nc.psum_tensor(f"{tag}_ps", [P, 8, BANK], F32))

        gains_in, qk_in, vo_in = sem("gains_in"), sem("qk_in"), sem("vo_in")
        yt_loaded = [sem(f"yt_loaded{j}") for j in range(NB)]
        x_loaded = [sem(f"x_loaded{j}") for j in range(NB)]
        waits_met = sem("waits_met")
        link_s, const_made, stored = sem("link"), sem("const_made"), sem("stored")
        STEPS.setdefault(tag, {})
        S = {k: Steps(sem(k), k, STEPS[tag]) for k in ("pe_mix", "pe_att", "vec_mix", "vec_att", "act_mix", "act_att")}
        mix = [S[k] for k in ("pe_mix", "vec_mix", "act_mix")]
        attn = [S[k] for k in ("pe_att", "vec_att", "act_att")]
        pm, vm, am = mix
        pa, va, aa = attn
        block = ctx.enter_context(nc.Block())
        flat2 = lambda b: ps[0:TT, b:b + 2, :].rearrange("p b t -> p (b t)")

        def schedule(eng, mix_tile, att_tile):
            def at_mix(i, j, turns):
                for s in mix:
                    s.iteration(i)
                if mix_tile is not None:
                    mix_tile(i, j, turns)

            def at_att(i, j, turns):
                for s in attn:
                    s.iteration(i)
                for s in mix:
                    s.iteration(i)

                def ahead():
                    if turns is not None:
                        at_mix(i + 1, (j + 1) % NB, turns)
                        for s in mix:
                            s.iteration(i)
                att_tile(i, j, ahead)

            at_mix(0, 0, 0)
            if TILES > 2:
                with eng.Fori(0, TILES // 2 - 1) as n:
                    for j in range(2):
                        at_att(2 * n + j, j, n + j)
            if TILES > 1:
                at_att(TILES - 2, 0, TILES // 2 - 1)
            at_att(TILES - 1, (TILES - 1) % NB, None)

        @block.sync
        def _(sync):
            def load(i, j):
                sync.dma_start(yt_in[j][:, :, :], yt[:, :, bass.ds(i * TT, TT)].rearrange("t p m -> p t m")).then_inc(yt_loaded[j], 16)
                sync.dma_start(x_in[j][:, :], x[0, bass.ds(i * TT, TT), :]).then_inc(x_loaded[j], 16)

            def store(i):
                for s in attn:
                    s.iteration(i)
                sync.wait_ge(*va.at("out"))
                sync.sem_inc(waits_met, 1)
                sync.dma_start(y[0, bass.ds(i * TT, TT), :], o[:, :]).then_inc(stored, 16)

            sync.sem_inc(stored, 16)
            load(0, 0)
            sync.dma_start(gains[:, 0, :], g_post.broadcast_to([P, D_MODEL])).then_inc(gains_in, 16)
            sync.dma_start(gains[:, 1, :], g_post_x.broadcast_to([P, D_MODEL])).then_inc(gains_in, 16)
            if qk_vo is not None:
                for dst, src, loaded in zip((qk_sb, vo_sb), qk_vo, (qk_in, vo_in)):
                    sync.dma_start(dst[:, :, :], src.rearrange("t p m -> p t m")).then_inc(loaded, 16)
            if NB > 1:
                load(1, 1)
            if TILES > NB:
                with sync.Fori(0, TILES // 2 - 1) as n:
                    for j in range(2):
                        i = 2 * n + j
                        for s in mix:
                            s.iteration(i)
                        sync.wait_ge(*pm.at("mix"))
                        sync.wait_ge(*vm.at("x1"))
                        sync.sem_inc(waits_met, 1)
                        load(i + 2, j)
                        store(i)
            for i in range(TILES - NB, TILES):
                store(i)
            sync.wait_ge(stored, 16 * (TILES + 1))

        @block.gpsimd
        def _(pool):
            count = [0]

            def link(ins):
                count[0] += 1
                ins.then_inc(link_s, 1)
                pool.wait_ge(link_s, count[0])

            link(pool.memset(eps[:, :], NORM_EPS))
            link(pool.memset(ident[:, :], 0.0))
            link(pool.affine_select(out=ident[:, :], in_=ident[:, :], compare_op=ALU.not_equal, fill=1.0,
                                    base=0, pattern=[[-1, P]], channel_multiplier=1))
            pool.sem_inc(const_made, 1)


        @block.scalar
        def _(act):
            load_ln_and_exp(nc, act)
            act.wait_ge(const_made, 1)

            def root(s, src, k, name):
                c = small[:, k:k + 1]
                act.activation(src[1], src[0], ACT.Square, accum_out=c).then_inc(*s.did(f"{name}_squares"))
                act.wait_ge(*s.last())
                act.activation(c, c, ACT.Ln, scale=1.0 / D_MODEL, bias=eps[0:TT, :]).then_inc(*s.did(f"{name}_ln"))
                act.wait_ge(*s.last())
                act.activation(c, c, ACT.Exp, scale=-0.5).then_inc(*s.did(name))

            def mix_tile(i, j, turns):
                act.wait_ge(*pm.at("mix"))
                act.wait_ge(*vm.before())
                root(am, (flat2(0), probs[:, :]), 0, "mix_root")
                act.wait_ge(*vm.at("x1"))
                root(am, (x1[j][:, :], probs[:, :]), 1, "x1_root")

            def att_tile(i, j, ahead):
                act.wait_ge(*pa.at("hx_turned"))
                act.activation(turned[:, :, :], ps[:, 6:8, :].rearrange("p b (k t) -> p (b k) t", t=P)[:, :, 0:TT], ACT.Copy).then_inc(*aa.did("hxT"))
                act.wait_ge(*va.at("neg_max"))
                for h in range(MEM_HEADS):
                    act.activation(hx[:, h * MEM_LEN:(h + 1) * MEM_LEN], ps[0:TT, 4 + h // 2, (h % 2) * MEM_LEN:(h % 2 + 1) * MEM_LEN],
                                   ACT.Exp, bias=mx[:, 0, h:h + 1], accum_out=mx[:, 1, h:h + 1]).then_inc(*aa.did(f"exp{h}"))
                act.wait_ge(*pa.at("p_turned"))
                act.activation(turned[:, :, :], ps[:, 6:8, :].rearrange("p b (k t) -> p (b k) t", t=P)[:, :, 0:TT], ACT.Copy).then_inc(*aa.did("pT"))
                ahead()
                act.wait_ge(*pa.at("att"))
                root(aa, (flat2(2), probs[:, :]), 2, "att_root")

            am.start(act)
            aa.start(act)
            schedule(act, mix_tile, att_tile)

        @block.vector
        def _(vec):
            vec.wait_ge(gains_in, 32)

            def mix_tile(i, j, turns):
                vec.wait_ge(*am.at("mix_root"))
                vec.wait_ge(x_loaded[j], 16 * (turns + 1))
                vec.tensor_tensor(x1[j][:, :], flat2(0), gains[0:TT, 0, :], ALU.mult).then_inc(*vm.did("mix_gain"))
                vec.wait_ge(*vm.last())
                vec.scalar_tensor_tensor(x1[j][:, :], x1[j][:, :], small[:, 0:1], x_in[j][:, :], ALU.mult, ALU.add).then_inc(*vm.did("x1"))
                vec.wait_ge(*am.at("x1_root"))
                vec.tensor_scalar(hx[:, :], x1[j][:, :], small[:, 1:2], None, ALU.mult).then_inc(*vm.did("hx"))

            def att_tile(i, j, ahead):
                vec.wait_ge(*pa.at("scores"))
                s4 = ps[0:TT, 4:6, :].rearrange("p b (h m) -> p (b h) m", h=2)
                vec.tensor_reduce(mx[:, 2, :], s4, AX_X, ALU.max).then_inc(*va.did("max"))
                vec.wait_ge(*va.last())
                vec.tensor_scalar(mx[:, 0, :], mx[:, 2, :], -1.0, None, ALU.mult).then_inc(*va.did("neg_max"))
                vec.wait_ge(*aa.at("exp3"))
                vec.reciprocal(mx[:, 2, :], mx[:, 1, :]).then_inc(*va.did("inverse"))
                vec.wait_ge(*va.last())
                hm = lambda t: t[:, :].rearrange("p (h m) -> p h m", h=MEM_HEADS)
                vec.tensor_tensor(hm(probs), hm(hx), bc(mx[:, 2, :], 2, MEM_LEN), ALU.mult).then_inc(*va.did("probs"))
                ahead()
                vec.wait_ge(*aa.at("att_root"))
                vec.wait_ge(stored, 16 * i + 16)
                vec.tensor_tensor(o[:, :], flat2(2), gains[0:TT, 1, :], ALU.mult).then_inc(*va.did("att_gain"))
                vec.wait_ge(*va.last())
                vec.scalar_tensor_tensor(o[:, :], o[:, :], small[:, 2:3], x1[j][:, :], ALU.mult, ALU.add).then_inc(*va.did("out"))

            vm.start(vec)
            va.start(vec)
            schedule(vec, mix_tile, att_tile)

        @block.tensor
        def _(pe):
            pe.wait_ge(const_made, 1)
            pe.wait_ge(ahead_in, 16 * len(weights))

            def product(b, left, right, n):
                for half in range(2):
                    for k in range(n):
                        last = pe.matmul(ps[0:TT, b + half, :], left[:, k, :], right[:, k, half * BANK:(half + 1) * BANK],
                                         start=k == 0, stop=k == n - 1)
                return last

            def mix_tile(i, j, turns):
                pe.wait_ge(*vm.before())
                pe.wait_ge(yt_loaded[j], 16 * (turns + 1))
                product(0, yt_in[j], w_o, YT).then_inc(*pm.did("mix"))

            def turn(b, src):
                for k in range(KT):
                    last = pe.transpose(ps[:, b + k // 4, (k % 4) * P:(k % 4) * P + TT], src[:, k * P:(k + 1) * P], ident[0:TT, 0:TT])
                return last

            def att_tile(i, j, ahead):
                if qk_vo is not None:
                    pe.wait_ge(qk_in, 16)
                pe.wait_ge(*vm.at("hx"))
                turn(6, hx).then_inc(*pa.did("hx_turned"))
                pe.wait_ge(*aa.at("hxT"))
                product(4, turned, qk_sb, KT).then_inc(*pa.did("scores"))
                ahead()
                if qk_vo is not None:
                    pe.wait_ge(vo_in, 16)
                pe.wait_ge(*va.at("probs"))
                turn(6, probs).then_inc(*pa.did("p_turned"))
                pe.wait_ge(*aa.at("pT"))
                product(2, turned, vo_sb, KT).then_inc(*pa.did("att"))

            pm.start(pe)
            pa.start(pe)
            schedule(pe, mix_tile, att_tile)


def hybrid_stream_encoder_step(nc, a, outs):
    (y_prompt, y_sample, lru_conv_p, lru_conv_s, lru_h_p, lru_h_s, shift_p, shift_s, wkv_p, wkv_s,
     ssd_conv_p, ssd_conv_s, ssd_h_p, ssd_h_s, hgrn_p, hgrn_s, mem_k, mem_v) = outs
    TP, TS = a["x_prompt"].shape[1], a["x_sample"].shape[1]

    def scratch(name, shape):
        return nc.dram_tensor(name, shape, F32, kind="Internal").ap()

    tokens = (TP, TS)
    pc = [scratch(f"pc{g}", [N_CH_TILES, P, HALO + t]) for g, t in enumerate(tokens)]
    dtr = [scratch(f"dtr{g}", [t, HEADS]) for g, t in enumerate(tokens)]
    yt = [scratch(f"yt{g}", [YT, P, t]) for g, t in enumerate(tokens)]
    qk = [scratch(f"qk{g}", [KT, P, D_MODEL]) for g in range(2)]
    vo = [scratch(f"vo{g}", [KT, P, D_MODEL]) for g in range(2)]
    names = ("lru_conv", "lru_h", "shift", "wkv", "ssd_conv", "ssd_h", "hgrn_s")
    sample_in = dict(zip(names, (a["state_lru_conv"], a["state_lru_h"], a["state_rwkv_shift"], a["state_rwkv_wkv"],
                                 a["state_ssd_conv"], a["state_ssd_h"], a["state_hgrn_s"])))
    prompt_out = dict(zip(names, (lru_conv_p, lru_h_p, shift_p, wkv_p, ssd_conv_p, ssd_h_p, hgrn_p)))
    sample_out = dict(zip(names, (lru_conv_s, lru_h_s, shift_s, wkv_s, ssd_conv_s, ssd_h_s, hgrn_s)))

    project_pass(nc, a["x_prompt"], a["x_sample"], a["g_pre"], a["w_in"], pc, dtr, sample_in, TP, TS)
    memory_pass(nc, a["mem_prompt"], a["mem_g"], a["mem_w_k"], a["mem_w_v"], a["mem_w_q"], a["mem_w_o"],
                a["g_pre_x"], a["cache_mem_k"], a["cache_mem_v"], mem_k, mem_v, qk, vo)
    mixer_pass(nc, "mixp", TP, P, 64, pc[0], dtr[0], yt[0], a, None, prompt_out)
    with ExitStack() as ctx:
        weights = [ctx.enter_context(nc.sbuf_tensor(name, [P, k, D_MODEL], F32))
                   for name, k in (("w_out_sb", YT), ("qk_sb", KT), ("vo_sb", KT))]
        ahead_in = ctx.enter_context(nc.semaphore("ahead_in"))
        ahead = [(weights[0][:, :, :], a["w_out"][0, :, :].rearrange("(k p) n -> p k n", p=P)),
                 (weights[1][:, :, :], qk[0].rearrange("t p m -> p t m")),
                 (weights[2][:, :, :], vo[0].rearrange("t p m -> p t m"))]
        mixer_pass(nc, "mixs", TS, TS, TS, pc[1], dtr[1], yt[1], a, sample_in, sample_out, ahead, ahead_in)
        attend_pass(nc, "attp", TP, P, yt[0], a["x_prompt"], y_prompt, a["g_post"], a["g_post_x"], weights, ahead_in, None)
        attend_pass(nc, "atts", TS, TS, yt[1], a["x_sample"], y_sample, a["g_post"], a["g_post_x"], weights, ahead_in,
                    (qk[1], vo[1]))


_INS = ['x_prompt', 'x_sample', 'state_lru_conv', 'state_lru_h', 'state_rwkv_shift', 'state_rwkv_wkv',
        'state_ssd_conv', 'state_ssd_h', 'state_hgrn_s', 'cache_mem_k', 'cache_mem_v', 'mem_prompt',
        'g_pre', 'g_post', 'g_pre_x', 'g_post_x', 'w_in', 'w_out',
        'lru_conv_w', 'lru_conv_b', 'lru_w_r', 'lru_b_r', 'lru_w_i', 'lru_b_i', 'lru_lambda',
        'rwkv_mu', 'rwkv_w0', 'rwkv_w_up', 'rwkv_a0', 'rwkv_a_up', 'rwkv_k_k', 'rwkv_k_a', 'rwkv_r_k',
        'rwkv_ln_g', 'rwkv_ln_b', 'ssd_conv_w', 'ssd_conv_b', 'ssd_dt_bias', 'ssd_a_log', 'ssd_d', 'ssd_norm_g',
        'hgrn_lb_logits', 'hgrn_norm_g', 'mem_g', 'mem_w_q', 'mem_w_k', 'mem_w_v', 'mem_w_o']
_OUTS = ['x_prompt', 'x_sample', 'state_lru_conv', 'state_lru_conv', 'state_lru_h', 'state_lru_h',
         'state_rwkv_shift', 'state_rwkv_shift', 'state_rwkv_wkv', 'state_rwkv_wkv', 'state_ssd_conv', 'state_ssd_conv',
         'state_ssd_h', 'state_ssd_h', 'state_hgrn_s', 'state_hgrn_s', 'cache_mem_k', 'cache_mem_k']


def kernel(**inputs):
    import numpy as _np
    import concourse.bacc as _bacc
    from concourse import mybir as _mybir
    from concourse.bass_utils import run_bass_kernel_spmd as _run

    nc = _bacc.Bacc("TRN2", target_bir_lowering=False, num_devices=1)
    arrays, args = {}, {}
    for name in _INS:
        a = _np.ascontiguousarray(inputs[name])
        arrays[f"in_{name}_dram"] = a
        args[name] = nc.dram_tensor(f"in_{name}_dram", a.shape, _mybir.dt.from_np(a.dtype), kind="ExternalInput").ap()
    outs = [nc.dram_tensor(f"out_{i}_dram", arrays[f"in_{like}_dram"].shape, _mybir.dt.float32, kind="ExternalOutput").ap()
            for i, like in enumerate(_OUTS)]
    hybrid_stream_encoder_step(nc, args, outs)
    r = _run(nc, [arrays], core_ids=[0])
    return tuple(r.results[0][f"out_{i}_dram"] for i in range(len(_OUTS)))
```
